# Optimizing a Trainium2 kernel written in Bass

```python
import jax
import jax.numpy as jnp
from jax import lax
import numpy as np

D_MODEL = 1024
BATCH = 1
SEQ = 512
DEPTH = 2
DEC_BATCH = 1
DEC_SEQ = 64
PAST_LEN = 128

CHUNK = 64
ML_HEADS = 4
ML_DH = 128
ML_W = ML_HEADS * ML_DH
SG_GROUPS = 4
SG_CHUNK = 128
SG_W = 512
SG_GDIM = SG_W // SG_GROUPS
SW_HEADS = 8
SW_KV = 2
SW_REP = SW_HEADS // SW_KV
SW_DH = 64
SW_W = SW_HEADS * SW_DH
SW_KVW = SW_KV * SW_DH
WINDOW = 128
WIN_CHUNKS = WINDOW // CHUNK
BAND = (WIN_CHUNKS + 1) * CHUNK
ROPE_THETA = 10000.0
FFN_HIDDEN = 2816
N_BRANCH = 3
EPS = 1e-6
SPLIT_SIZES = (ML_W, ML_W, ML_W, ML_W, ML_HEADS, ML_HEADS, SG_W, SG_W, SW_W, SW_KVW, SW_KVW, N_BRANCH * D_MODEL)
D_IN = 4 * ML_W + 2 * ML_HEADS + 2 * SG_W + SW_W + 2 * SW_KVW + N_BRANCH * D_MODEL

kernel_name = 'hybrid_mlstm_gmlp_swa_stream_step'

def rms_norm(x, g):
    xf = x.astype(jnp.float32)
    y = xf * lax.rsqrt(jnp.mean(xf * xf, axis=-1, keepdims=True) + EPS)
    return (y * g.astype(jnp.float32)).astype(x.dtype)

def layer_norm(x, g, b):
    xf = x.astype(jnp.float32)
    mu = jnp.mean(xf, axis=-1, keepdims=True)
    var = jnp.mean(jnp.square(xf - mu), axis=-1, keepdims=True)
    y = (xf - mu) * lax.rsqrt(var + EPS)
    return (y * g.astype(jnp.float32) + b.astype(jnp.float32)).astype(x.dtype)

def rope(x, pos):
    half = x.shape[-1] // 2
    inv = ROPE_THETA ** (-jnp.arange(half, dtype=jnp.float32) / half)
    ang = pos.astype(jnp.float32)[:, None] * inv[None, :]
    cos = jnp.cos(ang)[:, None, :]
    sin = jnp.sin(ang)[:, None, :]
    xf = x.astype(jnp.float32)
    x1, x2 = xf[..., :half], xf[..., half:]
    return jnp.concatenate([x1 * cos - x2 * sin, x1 * sin + x2 * cos], axis=-1).astype(x.dtype)

def split_in(z):
    idx = np.cumsum(np.array(SPLIT_SIZES))[:-1].tolist()
    return jnp.split(z, idx, axis=-1)

def mlstm_chunk(carry, q, k, v, ig, lf):
    C, n, m = carry
    L = q.shape[2]
    b = jnp.cumsum(lf, axis=-1)
    logD = b[..., :, None] - b[..., None, :] + ig[..., None, :]
    logD = jnp.where(jnp.tril(jnp.ones((L, L), bool)), logD, -jnp.inf)
    inter = b + m[..., None]
    m_t = jnp.maximum(inter, jnp.max(logD, axis=-1))
    w_intra = jnp.exp(logD - m_t[..., None])
    w_inter = jnp.exp(inter - m_t)
    s = jnp.einsum('bhtd,bhsd->bhts', q, k) * w_intra
    num = w_inter[..., None] * jnp.einsum('bhtd,bhde->bhte', q, C) + jnp.einsum('bhts,bhse->bhte', s, v)
    den = w_inter * jnp.einsum('bhtd,bhd->bht', q, n) + jnp.sum(s, axis=-1)
    h = num / jnp.maximum(jnp.abs(den), jnp.exp(-m_t))[..., None]
    bL = b[..., -1]
    log_ws = bL[..., None] - b + ig
    m_new = jnp.maximum(bL + m, jnp.max(log_ws, axis=-1))
    decay = jnp.exp(bL + m - m_new)
    ws = jnp.exp(log_ws - m_new[..., None])
    C_new = decay[..., None, None] * C + jnp.einsum('bhs,bhsd,bhse->bhde', ws, k, v)
    n_new = decay[..., None] * n + jnp.einsum('bhs,bhsd->bhd', ws, k)
    return (C_new, n_new, m_new), h

def mlstm_scan(q, k, v, ig, lf):
    B, H, S, _ = q.shape
    nC = S // CHUNK

    def chunks(t):
        return jnp.moveaxis(t.reshape(t.shape[:2] + (nC, CHUNK) + t.shape[3:]), 2, 0)

    init = (jnp.zeros((B, H, ML_DH, ML_DH), jnp.float32),
            jnp.zeros((B, H, ML_DH), jnp.float32),
            jnp.zeros((B, H), jnp.float32))
    state, hs = lax.scan(lambda carry, xs: mlstm_chunk(carry, *xs), init,
                         (chunks(q), chunks(k), chunks(v), chunks(ig), chunks(lf)))
    h = jnp.moveaxis(hs, 0, 2).reshape(B, H, S, ML_DH)
    return h, state

def spatial_gating(u, v, ln_g, ln_b, w_s, b_s, L):
    B, S, _ = v.shape
    vn = layer_norm(v, ln_g, ln_b)
    vc = vn.reshape(B, S // L, L, SG_GROUPS, SG_GDIM)
    w = jnp.where(jnp.tril(jnp.ones((L, L), bool)), w_s[:, :L, :L], 0)
    z = jnp.einsum('gpr,bnrgc->bnpgc', w, vc) + b_s[:, :L].T[None, None, :, :, None]
    return u * z.reshape(B, S, SG_W), vn

def sink_softmax(s, sink):
    mx = jnp.maximum(jnp.max(s, axis=-1, keepdims=True), sink)
    p = jnp.exp(s - mx)
    return p / (jnp.sum(p, axis=-1, keepdims=True) + jnp.exp(sink - mx))

def swa_prompt(q, k, v, sinks):
    B, S = q.shape[:2]
    nC = S // CHUNK
    pad = WIN_CHUNKS * CHUNK

    def bands(t):
        tp = jnp.pad(t, ((0, 0), (pad, 0), (0, 0), (0, 0))).reshape(B, nC + WIN_CHUNKS, CHUNK, SW_KV, SW_DH)
        return jnp.concatenate([tp[:, j:j + nC] for j in range(WIN_CHUNKS + 1)], axis=2)

    kb, vb = bands(k), bands(v)
    qb = q.reshape(B, nC, CHUNK, SW_KV, SW_REP, SW_DH)
    s = jnp.einsum('bcqgrd,bckgd->bcgrqk', qb, kb).astype(jnp.float32) * (SW_DH ** -0.5)
    key_chunk = jnp.arange(nC)[:, None] - WIN_CHUNKS + jnp.arange(BAND)[None, :] // CHUNK
    s = jnp.where((key_chunk >= 0)[None, :, None, None, None, :], s, -jnp.inf)
    sink = sinks.astype(jnp.float32).reshape(SW_KV, SW_REP)[None, None, :, :, None, None]
    p = sink_softmax(s, sink).astype(v.dtype)
    return jnp.einsum('bcgrqk,bckgd->bcqgrd', p, vb).reshape(B, S, SW_W)

def swa_sample(q, k, v, cache_k, cache_v, sinks):
    B, T = q.shape[:2]
    kf = jnp.concatenate([cache_k.astype(k.dtype), k], axis=1)
    vf = jnp.concatenate([cache_v.astype(v.dtype), v], axis=1)
    qb = q.reshape(B, T, SW_KV, SW_REP, SW_DH)
    s = jnp.einsum('bqgrd,bkgd->bgrqk', qb, kf).astype(jnp.float32) * (SW_DH ** -0.5)
    sink = sinks.astype(jnp.float32).reshape(SW_KV, SW_REP)[None, :, :, None, None]
    p = sink_softmax(s, sink).astype(v.dtype)
    return jnp.einsum('bgrqk,bkgd->bqgrd', p, vf).reshape(B, T, SW_W)

def block(x, c, p, pos, st):
    B, S, _ = x.shape
    mod = jax.nn.silu(c) @ p['w_ada'] + p['b_ada']
    sh1, sc1, g1, sh2, sc2, g2 = [t[:, None, :] for t in jnp.split(mod, 6, axis=-1)]
    h = rms_norm(x, p['g_pre_mix']) * (1 + sc1) + sh1
    mq, mk, mv, mo, mi, mf, su, sv, wq, wk, wv, gl = split_in(h @ p['w_in'])

    def heads(t):
        return t.reshape(B, S, ML_HEADS, ML_DH).transpose(0, 2, 1, 3).astype(jnp.float32)

    q = heads(mq)
    k = heads(mk) * (ML_DH ** -0.5)
    v = heads(mv)
    ig = (mi.astype(jnp.float32) + p['b_igate'].astype(jnp.float32)).transpose(0, 2, 1)
    lf = jax.nn.log_sigmoid(mf.astype(jnp.float32) + p['b_fgate'].astype(jnp.float32)).transpose(0, 2, 1)
    if st is None:
        h_ml, (C, n, m) = mlstm_scan(q, k, v, ig, lf)
    else:
        carry = (st[0].astype(jnp.float32), st[1].astype(jnp.float32), st[2].astype(jnp.float32))
        (C, n, m), h_ml = mlstm_chunk(carry, q, k, v, ig, lf)
    h_ml = h_ml.transpose(0, 2, 1, 3).reshape(B, S, ML_W).astype(x.dtype)
    y_ml = jax.nn.sigmoid(mo) * h_ml

    L = SG_CHUNK if st is None else S
    y_sg, v_norm = spatial_gating(su, sv, p['ln_v_g'], p['ln_v_b'], p['w_spatial'], p['b_spatial'], L)

    qs = rope(wq.reshape(B, S, SW_HEADS, SW_DH), pos)
    ks = rope(wk.reshape(B, S, SW_KV, SW_DH), pos)
    vs = wv.reshape(B, S, SW_KV, SW_DH)
    if st is None:
        y_sw = swa_prompt(qs, ks, vs, p['swa_sinks'])
        new_k, new_v = ks[:, -WINDOW:], vs[:, -WINDOW:]
    else:
        y_sw = swa_sample(qs, ks, vs, st[3], st[4], p['swa_sinks'])
        new_k, new_v = ks, vs

    gates = jax.nn.sigmoid(gl).reshape(B, S, N_BRANCH, D_MODEL)
    merged = (gates[:, :, 0] * (y_ml @ p['w_br_mlstm'])
              + gates[:, :, 1] * (y_sg @ p['w_br_gmlp'])
              + gates[:, :, 2] * (y_sw @ p['w_br_swa']))
    x = x + g1 * rms_norm(merged @ p['w_out'], p['g_post_mix'])

    h2 = rms_norm(x, p['g_pre_ffn']) * (1 + sc2) + sh2
    gate, up = jnp.split(h2 @ p['w_ffn_in'], 2, axis=-1)
    f = (jax.nn.silu(gate) * up) @ p['w_ffn_out']
    x = x + g2 * rms_norm(f, p['g_post_ffn'])
    return x, (C, n, m, new_k, new_v, v_norm)

def setup_inputs(seed: int = 0) -> dict:
    key = jax.random.key(seed)
    ks = jax.random.split(key, 32)
    nrm = jax.random.normal
    f32 = jnp.float32
    wc = min(WINDOW, PAST_LEN)
    return {
        'x_prompt': nrm(ks[0], (BATCH, SEQ, D_MODEL), f32),
        'x_sample': nrm(ks[1], (DEC_BATCH, DEC_SEQ, D_MODEL), f32),
        'c_prompt': nrm(ks[2], (BATCH, D_MODEL), f32),
        'c_sample': nrm(ks[3], (DEC_BATCH, D_MODEL), f32),
        'state_mlstm_C': nrm(ks[4], (DEPTH, DEC_BATCH, ML_HEADS, ML_DH, ML_DH), f32) * ML_DH ** -0.5,
        'state_mlstm_n': nrm(ks[5], (DEPTH, DEC_BATCH, ML_HEADS, ML_DH), f32) * 0.5,
        'state_mlstm_m': jax.random.uniform(ks[6], (DEPTH, DEC_BATCH, ML_HEADS), f32, -1.0, 1.0),
        'cache_swa_k': nrm(ks[7], (DEPTH, DEC_BATCH, wc, SW_KV, SW_DH), f32),
        'cache_swa_v': nrm(ks[8], (DEPTH, DEC_BATCH, wc, SW_KV, SW_DH), f32),
        'w_ada': nrm(ks[9], (DEPTH, D_MODEL, 6 * D_MODEL), f32) * 0.5 * D_MODEL ** -0.5,
        'b_ada': nrm(ks[10], (DEPTH, 6 * D_MODEL), f32) * 0.02,
        'g_pre_mix': 1.0 + 0.02 * nrm(ks[11], (DEPTH, D_MODEL), f32),
        'g_post_mix': 1.0 + 0.02 * nrm(ks[12], (DEPTH, D_MODEL), f32),
        'g_pre_ffn': 1.0 + 0.02 * nrm(ks[13], (DEPTH, D_MODEL), f32),
        'g_post_ffn': 1.0 + 0.02 * nrm(ks[14], (DEPTH, D_MODEL), f32),
        'w_in': nrm(ks[15], (DEPTH, D_MODEL, D_IN), f32) * D_MODEL ** -0.5,
        'b_igate': 0.1 * nrm(ks[16], (DEPTH, ML_HEADS), f32),
        'b_fgate': jnp.linspace(3.0, 6.0, ML_HEADS, dtype=f32)[None, :] + 0.1 * nrm(ks[17], (DEPTH, ML_HEADS), f32),
        'ln_v_g': 1.0 + 0.02 * nrm(ks[18], (DEPTH, SG_W), f32),
        'ln_v_b': 0.02 * nrm(ks[19], (DEPTH, SG_W), f32),
        'w_spatial': nrm(ks[20], (DEPTH, SG_GROUPS, SG_CHUNK, SG_CHUNK), f32) * 0.5 * SG_CHUNK ** -0.5,
        'b_spatial': 1.0 + 0.02 * nrm(ks[21], (DEPTH, SG_GROUPS, SG_CHUNK), f32),
        'swa_sinks': 0.5 * nrm(ks[22], (DEPTH, SW_HEADS), f32),
        'w_br_mlstm': nrm(ks[23], (DEPTH, ML_W, D_MODEL), f32) * ML_W ** -0.5,
        'w_br_gmlp': nrm(ks[24], (DEPTH, SG_W, D_MODEL), f32) * SG_W ** -0.5,
        'w_br_swa': nrm(ks[25], (DEPTH, SW_W, D_MODEL), f32) * SW_W ** -0.5,
        'w_out': nrm(ks[26], (DEPTH, D_MODEL, D_MODEL), f32) * D_MODEL ** -0.5,
        'w_ffn_in': nrm(ks[27], (DEPTH, D_MODEL, 2 * FFN_HIDDEN), f32) * D_MODEL ** -0.5,
        'w_ffn_out': nrm(ks[28], (DEPTH, FFN_HIDDEN, D_MODEL), f32) * FFN_HIDDEN ** -0.5,
    }

def reference(x_prompt, x_sample, c_prompt, c_sample, state_mlstm_C, state_mlstm_n, state_mlstm_m,
              cache_swa_k, cache_swa_v, w_ada, b_ada, g_pre_mix, g_post_mix, g_pre_ffn, g_post_ffn,
              w_in, b_igate, b_fgate, ln_v_g, ln_v_b, w_spatial, b_spatial, swa_sinks,
              w_br_mlstm, w_br_gmlp, w_br_swa, w_out, w_ffn_in, w_ffn_out):
    pos_p = jnp.arange(x_prompt.shape[1])
    pos_s = PAST_LEN + jnp.arange(x_sample.shape[1])
    xp, xs = x_prompt, x_sample
    new_p = [[] for _ in range(5)]
    new_s = [[] for _ in range(6)]
    for l in range(DEPTH):
        p = dict(w_ada=w_ada[l], b_ada=b_ada[l], g_pre_mix=g_pre_mix[l], g_post_mix=g_post_mix[l],
                 g_pre_ffn=g_pre_ffn[l], g_post_ffn=g_post_ffn[l], w_in=w_in[l], b_igate=b_igate[l],
                 b_fgate=b_fgate[l], ln_v_g=ln_v_g[l], ln_v_b=ln_v_b[l], w_spatial=w_spatial[l],
                 b_spatial=b_spatial[l], swa_sinks=swa_sinks[l], w_br_mlstm=w_br_mlstm[l],
                 w_br_gmlp=w_br_gmlp[l], w_br_swa=w_br_swa[l], w_out=w_out[l],
                 w_ffn_in=w_ffn_in[l], w_ffn_out=w_ffn_out[l])
        xp, st_p = block(xp, c_prompt, p, pos_p, None)
        xs, st_s = block(xs, c_sample, p, pos_s,
                         (state_mlstm_C[l], state_mlstm_n[l], state_mlstm_m[l], cache_swa_k[l], cache_swa_v[l]))
        for lst, a in zip(new_p, st_p[:5]):
            lst.append(a)
        for lst, a in zip(new_s, st_s):
            lst.append(a)
    C_p, n_p, m_p, k_p, v_p = [jnp.stack(a) for a in new_p]
    C_s, n_s, m_s, k_s, v_s, gv_s = [jnp.stack(a) for a in new_s]
    return (xp, xs, C_p, n_p, m_p, k_p, v_p, C_s, n_s, m_s, k_s, v_s, gv_s)


_drawn_inputs = setup_inputs


def setup_inputs(seed=0):
    import zlib

    import numpy as np

    out = dict(_drawn_inputs(seed))
    spreads = {}
    factors = {'g_post_mix': 4.629,
     'g_pre_ffn': 3.911,
     'g_post_ffn': 5.72,
     'ln_v_g': 2.907,
     'ln_v_b': 2.84,
     'b_spatial': 7.572,
     'swa_sinks': 8.0}
    for name, (base, spread) in spreads.items():
        noise = np.random.default_rng([zlib.crc32(name.encode()), seed]).standard_normal(out[name].shape)
        drawn = base * np.exp(spread * noise) if base else spread * noise
        out[name] = jnp.asarray(drawn.astype(out[name].dtype))
    for name, factor in factors.items():
        out[name] = (out[name] * factor).astype(out[name].dtype)
    return out
```

```python
import numpy as np
import concourse.bass as bass
from concourse import mybir
from contextlib import ExitStack

DEPTH, D, SEQ, DSEQ, PAST = 2, 1024, 512, 64, 128
T = SEQ + DSEQ
HALF = T // 2
KT_ = D // 128
MLH, SGG, SWH, SWD = 4, 4, 8, 64
FFN = 2816
EPS = 1e-6
NTT = SEQ // 128
C_Q, C_K, C_V, C_MO, C_IF, C_SU, C_SV, C_WQ, C_WK, C_WV, C_GL = (
    0, 512, 1024, 1536, 2048, 2056, 2568, 3080, 3592, 3720, 3848)
BLOCKS = (8, 8, 6)
SLOT = 8 * 136
NEG = -1.0e30
ML_SCALE, SW_SCALE = 128 ** -0.5, 64 ** -0.5
WOFF = {0: 0, 1: 512, 3: 896, 2: 1024, 4: 1280}

CO = {}
_at = 0
for _n, _w in (("ident", 128), ("perm", 128), ("mneg", 128), ("ones", 128), ("cos", T),
               ("sin", T), ("m1", 256), ("sel", 512)):
    CO[_n] = (_at, _at + _w)
    _at += _w
NCONST = _at


def constants():
    c = np.zeros((128, NCONST), np.float32)

    def put(n, a):
        c[:a.shape[0], CO[n][0]:CO[n][1]] = a
    p = np.arange(128)
    put("ident", np.eye(128, dtype=np.float32))
    swap = np.where(p % 64 < 32, p + 32, p - 32)
    perm = np.zeros((128, 128), np.float32)
    perm[swap, p] = 1.0
    put("perm", perm)
    put("mneg", np.where(p[:, None] <= p[None, :], 0.0, NEG).astype(np.float32))
    put("ones", np.ones((128, 128), np.float32))
    pos = np.concatenate([np.arange(SEQ), PAST + np.arange(DSEQ)]).astype(np.float32)
    inv = (np.float32(10000.0) ** (-np.arange(32, dtype=np.float32) / np.float32(32))).astype(np.float32)
    ang = (inv[p % 32][:, None] * pos[None, :]).astype(np.float32)
    put("cos", np.cos(ang))
    put("sin", np.sin(ang) * np.where(p % 64 < 32, -1.0, 1.0)[:, None].astype(np.float32))
    k = np.arange(256)
    late = p[:, None] >= 64
    put("m1", np.where((late & (k[None] < 64)) | (~late & (k[None] >= 192)), NEG, 0.0).astype(np.float32))
    sel = np.zeros((128, 4, 128), np.float32)
    for h in range(4):
        sel[h, h] = 1.0
    put("sel", sel.reshape(128, 512))
    return c


SWA = [(t, g) for t in range(NTT + 1) for g in range(2)]
ORDER = ["par", "wst"] + [f"ada{i}" for i in range(24)] + ["ckt", "n1", "n1b"] + [f"qk{i}" for i in range(8)]
ORDER += ["wvif", "wk", "gt1", "gt2", "v0", "gt3", "v1", "kt0", "v2", "cm0", "kt1", "v3", "cm1", "kt2",
          "mo0", "cm2", "kt3", "mo1", "cm3"]


def _a(h):
    return [f"a1_{h}", f"a2_{h}", f"a3_{h}"]


def _b(h):
    return [f"b1_{h}"], [f"b2_{h}"]


def swa_slot(i):
    return (["pv%d" % (i - 2)] if 0 <= i - 2 < len(SWA) else []) + \
        (["tp%d" % (i - 1)] if 0 <= i - 1 < len(SWA) else []) + (["sc%d" % i] if i < len(SWA) else [])


ORDER += _a(0) + ["mo2"] + _b(0)[0] + ["mo3"] + _b(0)[1] + _a(1) + ["wq0"] + _b(1)[0] + ["wq1"] + _b(1)[1] \
    + _a(2) + ["wq2"] + _b(2)[0] + ["wq3"] + _b(2)[1] + _a(3) + ["su0"] + _b(3)[0] + ["su1"] + _b(3)[1] \
    + ["r4", "r0", "su2", "r1", "r2", "su3", "r3", "ko"]
for _i in range(4):
    ORDER += [f"sv{_i}"] + swa_slot(_i)
BRANCHES = (("ml", 0, 0), ("sw", 2, 1), ("sg", 1, 0))
_s = 4
for _b_, (_nm, _g, _set) in enumerate(BRANCHES):
    for _n in range(0, 8, 2):
        for _e in (f"g{_b_}_{_n}", f"g{_b_}_{_n + 1}"):
            ORDER.append(_e)
            if _b_ == 0:
                ORDER += swa_slot(_s)
                _s += 1
        if _b_ == 1:
            ORDER.append(f"z{_n // 2}")
        ORDER += [f"br{_b_}_{_n}", f"br{_b_}_{_n + 1}"]
        if _b_ == 0:
            ORDER += swa_slot(_s)
            _s += 1
ORDER += [f"wo{i}" for i in range(8)] + ["p1", "p1b", "n2", "n2b"]
for _c, _nb in enumerate(BLOCKS):
    ORDER += [f"fi{_c}_{i}" for i in range(2 * _nb)] + [f"fo{_c}_{i}" for i in range(8)]
ORDER += ["p2", "p2b"]
G = {n: i for i, n in enumerate(ORDER)}
NG = len(ORDER)
assert len(G) == NG
UNITS = 4
PER_UNIT = [sum(1 for i in range(NG) if i % UNITS == u) for u in range(UNITS)]

P_QK, P_WVIF, P_WK, P_V, P_MO, P_WQ, P_SU, P_SV, P_BR = 0, 8, 9, 10, 14, 18, 22, 26, 30
P_WO = P_BR + 36
P_FFN = P_WO + 8
NCH = P_FFN + sum(2 * b + 8 for b in BLOCKS)
assert NCH % 2 == 0

CHUNK_OF = {}
CHUNK_OF.update({f"qk{i}": i for i in range(8)})
CHUNK_OF.update({"wvif": P_WVIF, "wk": P_WK})
for _i in range(4):
    CHUNK_OF.update({f"v{_i}": P_V + _i, f"mo{_i}": P_MO + _i, f"wq{_i}": P_WQ + _i, f"su{_i}": P_SU + _i,
                     f"sv{_i}": P_SV + _i})
for _b_ in range(3):
    for _n in range(8):
        _p = P_BR + 12 * _b_ + 3 * (_n // 2)
        CHUNK_OF[f"g{_b_}_{_n}"] = _p + _n % 2
        if _n % 2:
            CHUNK_OF[f"br{_b_}_{_n}"] = _p + 2
CHUNK_OF.update({f"wo{i}": P_WO + i for i in range(8)})
_p = P_FFN
for _c, _nb in enumerate(BLOCKS):
    CHUNK_OF.update({f"fi{_c}_{i}": _p + i for i in range(2 * _nb)})
    _p += 2 * _nb
    CHUNK_OF.update({f"fo{_c}_{i}": _p + i for i in range(8)})
    _p += 8
assert sorted(CHUNK_OF.values()) == list(range(NCH))
_plain = [n for n in ORDER if n not in CHUNK_OF]
PLAIN = {n: i for i, n in enumerate(_plain)}
NPLAIN = len(_plain)
RAW_LOADS = [NCH // 2 + 1, NCH // 2]
PARAM_DMAS = 15
ACT_STEPS, DVE_STEPS = 1, 220
C_STORES, O_STORES = 18, 5


def build(nc, A, O):
    f32, f32r = mybir.dt.float32, mybir.dt.float32r
    ALU, ACT, AX = mybir.AluOpType, mybir.ActivationFunctionType, mybir.AxisListType
    ds = bass.ds
    ctx = ExitStack()
    with ctx:
        def sb(name, shape, dt=f32):
            return ctx.enter_context(nc.sbuf_tensor(name, shape, dt))

        def sem(name):
            return ctx.enter_context(nc.semaphore(name))

        def overlay(name, size, *uses):
            out = {}
            for use in uses:
                with ExitStack() as s:
                    for n, shape, dt in use:
                        out[n] = s.enter_context(nc.sbuf_tensor(n, shape, dt))
            ctx.enter_context(nc.sbuf_tensor(name, [128, size], f32))
            return out

        RAW = [sb(f"raw{s}", [128, SLOT]) for s in range(2)]
        HI = [sb(f"hi{s}", [128, SLOT], f32r) for s in range(2)]
        LO = [sb(f"lo{s}", [128, SLOT], f32r) for s in range(2)]
        CST = sb("consts", [128, NCONST])
        X = sb("x_resident", [128, KT_, T])
        HH = sb("h_hi", [128, KT_ * T + 64], f32r)
        HL = sb("h_lo", [128, KT_ * T + 64], f32r)
        MID = sb("mid", [128, KT_, T])
        TS = sb("tmp", [128, 2, T])
        r = overlay("yg_region", 16 * T,
                    [("y_hi", [128, 8, T], f32r), ("y_lo", [128, 8, T], f32r)],
                    [("pad_a", [128, 4, T], f32), ("rows_a", [4, 4, T], f32),
                     ("pad_b", [128, 4, T], f32), ("rows_b", [4, 2, T], f32), ("c_out", [128, 4, 2, 129], f32)])
        YH, YL, RA, RB, COUT = r["y_hi"], r["y_lo"], r["rows_a"], r["rows_b"], r["c_out"]
        r = overlay("proj_region", 5 * 516 + 4 * T + 4 * T + 2 * 704,
                    [("v_tok", [128, 5, 4, 129], f32), ("mo_su", [128, 4, T], f32), ("wq", [128, 4, T], f32),
                     ("kall", [128, 2, 704], f32)],
                    [("ada", [128, 2, 8 * 512], f32)])
        VT, MO, WQ, KALL, ADA = r["v_tok"], r["mo_su"], r["wq"], r["kall"], r["ada"]
        r = overlay("tmp_region", 3072 + 128,
                    [("dmask", [128, T], f32), ("wdecay", [128, 1344], f32), ("ytmp", [128, T], f32),
                     ("kw", [128, 5, 128], f32)],
                    [("sm", [128, 2, 4, 256], f32), ("pt", [128, 2, 512], f32)],
                    [("sq", [128, 2, T], f32), ("acc", [128, T], f32), ("rstd", [128, T], f32)])
        DM, W, YT, KW, SM, PT, SQ, ACC, R = (r[n] for n in ("dmask", "wdecay", "ytmp", "kw", "sm", "pt",
                                                             "sq", "acc", "rstd"))
        VSW = sb("v_swa", [128, 5, 128])
        WST = sb("w_spatial_t", [128, 4, 128])
        C0N = sb("c0_n0", [128, 4, 129])
        KOUT = sb("k_out", [128, 2, 128])
        CV = sb("cache_v", [128, 128])
        BSP = sb("b_spatial", [1, 512])
        VCOL = sb("vcol", [128, 80])
        BIF = sb("b_if", [128, 8])
        SINK = sb("sink", [128, 8])
        IFT = sb("if_tok", [128, 5, 8])
        CS = sb("c_silu", [128, 8, 2])
        CC = sb("c_cols", [128, 16])
        MOD = sb("mod", [128, 6, 8, 2])
        SC = sb("scales", [128, 4, 8, 2])
        AS = sb("a_cols", [128, 5, 4])
        WSC = sb("ws_cols", [128, 5, 4])
        EMC = sb("em_cols", [128, 5, 4])
        DEN = sb("den", [128, 5])
        RC = sb("rstd_cols", [128, 5])
        WIN = sb("win", [4, 64])
        DEC = sb("decay", [128, 4])
        M0 = sb("m0", [4, 1])
        NML = sb("neg_m_last", [4, 2])
        MX = sb("mx", [128, 2, 5, 4])
        SCRATCH = sb("scratch", [128, 3])
        BN = sb("bn", [128, 6])
        MV = sb("mean_var", [128, 5, 2])
        LR = sb("ln_rstd", [128, 5])
        K_ = {n: CST[:, a:b] for n, (a, b) in CO.items()}
        IDN, ONES = K_["ident"], K_["ones"]
        SEL = K_["sel"].rearrange("p (h c) -> p h c", h=4)
        QK, SU, YTK = MID, MO, KW
        SV = VT[:, :, :, :].rearrange("p t h c -> p (t h c)")[:, 0:2560].rearrange("p (t c) -> p t c", t=5)
        OMID = MID
        LNG, LNB = MID[:, 6, 0:512], MID[:, 7, 0:512]
        WSP = MID[:, 0, 0:512].rearrange("p (g r) -> p g r", g=4)
        VROWS, CKR = MID[0:80, 1, 0:128], MID[:, 2, 0:128]
        XIO = ADA[:, :, :].rearrange("p a (b c) -> p (a b) c", c=1024)
        IG, BC, AR, NM = (RA[:, i, :] for i in range(4))
        EM, WR = RB[:, 0, :], RB[:, 1, :]
        LFT = TS[0:4, 0, :]

        PS = ctx.enter_context(nc.psum_tensor("ps", [128, UNITS, 1024], f32))

        def unit(name):
            return PS[:, G[name] % UNITS, :]

        def halves(name):
            return unit(name).rearrange("p (a c) -> p a c", a=2)[:, :, 0:HALF]

        def split2(ap):
            return ap.rearrange("p (a c) -> p a c", a=2)

        group_done = sem("group_done")
        unit_free = [sem(f"unit_free{u}") for u in range(UNITS)]
        raw_loaded = [sem(f"raw_loaded{s}") for s in range(2)]
        chunk_split, chunk_hi, chunk_used = sem("chunk_split"), sem("chunk_hi"), sem("chunk_used")
        ada_loaded = [sem(f"ada_loaded{s}") for s in range(2)]
        consts_loaded, x_loaded, param_loaded = sem("consts_loaded"), sem("x_loaded"), sem("param_loaded")
        kx_moved, out_done = sem("kx_moved"), sem("out_done")
        dve_step, act_step = sem("dve_step"), sem("act_step")
        init_done, cs_ready, x_in_t, x_out_t, x_out_copied = (sem(n) for n in (
            "init_done", "cs_ready", "x_in_t", "x_out_t", "x_out_copied"))

        rate = {}

        def event(name, per_layer, credit=0):
            s = sem(name)
            rate[id(s)] = (per_layer, credit)
            return s

        def nth(s, l, k=0):
            per, credit = rate[id(s)]
            return l * per + (k + (1 + credit))

        def before(s, l, k):
            return l * rate[id(s)][0] + (k + 1)

        x_ready = event("x_ready", 16)
        sqn_ready = event("sqn_ready", 16)
        sqn_used = event("sqn_used", 14)
        sqo_ready = event("sqo_ready", 16)
        acc_added = event("acc_added", 16, 2)
        merged2 = event("merged2", 8, 2)
        ms_ready = event("ms_ready", 5)
        rt_ready = event("rt_ready", 5)
        dg_ready = event("dg_ready", 4)
        hs_ready = event("hs_ready", 16)
        hh_ready = event("hh_ready", 24)
        hl_ready = event("hl_ready", 24)
        nabs_ready = event("nabs_ready", 1)
        sp_ready = event("sp_ready", 1)
        m_ready = event("m_ready", 1)
        rows_ready = event("rows_ready", 1)
        d_ready = event("d_ready", 4)
        w_ready = event("w_ready", 4)
        yh_ready = event("yh_ready", 8)
        yl_ready = event("yl_ready", 8)
        rope_ready = event("rope_ready", 5)
        ln_ready = event("ln_ready", 5)
        NS = len(SWA)
        mx_ready = event("mx_ready", NS)
        ex_ready = event("ex_ready", NS)
        pn_ready = event("pn_ready", NS)
        oh_ready = event("oh_ready", NS)
        gh_ready = event("gh_ready", 22)
        gl_ready = event("gl_ready", 22, 2)
        c_stored, o_stored, ln_loaded = sem("c_stored"), sem("o_stored"), sem("ln_loaded")

        def done_by(name):
            return chunk_used if name in CHUNK_OF else group_done

        def done(l, name, i=0):
            if name in CHUNK_OF:
                return l * NCH + (i + (CHUNK_OF[name] + 3))
            return l * NPLAIN + (i + (PLAIN[name] + 1))

        def unit_of(name):
            return unit_free[G[name] % UNITS]

        def empty(l, name, i=0):
            return l * PER_UNIT[G[name] % UNITS] + (i + (G[name] // UNITS + 1))

        def read(l, name, i=0):
            return l * PER_UNIT[G[name] % UNITS] + (i + (G[name] // UNITS + 2))

        def apart(a, b):
            return G[a] % UNITS != G[b] % UNITS

        def split_count(l, pos):
            return l * NCH + (pos + 3)

        def carry(eng, name=None):
            if eng is nc.tensor:
                pe_lead = unit(name)[0:32, 0:1]
                eng.matmul(pe_lead, ONES[:, 0:32], ONES[:, 0:1], start=True, stop=True)
            elif eng is nc.gpsimd:
                eng.tensor_tensor(SCRATCH[:, 0:1], ONES[:, 0:1], ONES[:, 0:1], ALU.mult)
            elif eng is nc.vector:
                eng.memset(SCRATCH[:, 1:2], 0.0)
            else:
                eng.activation(SCRATCH[:, 2:3], ONES[:, 0:1], ACT.Square)

        class Steps:

            def __init__(self, per_layer):
                self.per = per_layer

            def layer(self, l):
                self.base, self.n = l * self.per, 0

            def __call__(self):
                self.n += 1
                return 1

            def all(self):
                return self.base + self.n

            def end(self):
                assert self.n == self.per, (self.n, self.per)

        block = ctx.enter_context(nc.Block())

        @block.sync
        def _(sp):
            sp.dma_start(CST[:, :], A["consts"]).then_inc(consts_loaded, 16)
            for t in range(NTT):
                sp.dma_start(XIO[:, t, :], A["x_prompt"][0, t * 128:(t + 1) * 128, :]).then_inc(x_loaded, 16)
            sp.dma_start(XIO[0:64, NTT, :], A["x_sample"][0, :, :]).then_inc(x_loaded, 16)
            sp.dma_start(MID[0:8, 0, 0:128], A["c_prompt"].rearrange("b (k p) -> (b k) p", p=128)).then_inc(x_loaded, 16)
            sp.dma_start(MID[8:16, 0, 0:128], A["c_sample"].rearrange("b (k p) -> (b k) p", p=128)).then_inc(x_loaded, 16)
            with sp.Fori(0, DEPTH) as l:
                for_ada = A["w_ada"][ds(l, 1)].rearrange("l (k p) c -> p (l k) c", p=128)
                ada = [ADA[:, s, :].rearrange("p (k c) -> p k c", k=8) for s in range(2)]
                sp.wait_ge(x_ready, nth(x_ready, l, 7))
                for s in range(2):
                    sp.dma_start(ada[s], for_ada[:, :, s * 512:(s + 1) * 512]).then_inc(ada_loaded[s], 16)
                with sp.Fori(1, 6) as j:
                    for s in range(2):
                        sp.wait_ge(done_by(f"ada{2 * s + 1}"), done(l, f"ada{2 * s + 1}", (j - 1) * 4))
                        sp.dma_start(ada[s], for_ada[:, :, ds(j * 1024 + s * 512, 512)]).then_inc(ada_loaded[s], 16)

                def load(s, pos, dst, src):
                    sp.wait_ge(chunk_split, l * NCH + (pos + 1))
                    sp.dma_start(dst, src).then_inc(raw_loaded[s], 16)

                w_in = A["w_in"][ds(l, 1)].rearrange("l (k p) c -> p (l k) c", p=128)

                def cols(s, pos, src, c):
                    load(s, pos, RAW[s][:, 0:1024].rearrange("p (k c) -> p k c", k=8), src[:, :, ds(c, 128)])

                with sp.Fori(0, 4) as i:
                    for s in range(2):
                        cols(s, i * 2 + s, w_in, i * 256 + s * 128)
                r0 = RAW[0][:, :].rearrange("p (k c) -> p k c", k=8)
                load(0, P_WVIF, r0[:, :, 0:128], w_in[:, :, C_WV:C_WV + 128])
                sp.dma_start(r0[:, :, 128:136], w_in[:, :, C_IF:C_IF + 8]).then_inc(raw_loaded[0], 16)
                cols(1, P_WK, w_in, C_WK)
                for pos, c in ((P_V, C_V), (P_MO, C_MO), (P_WQ, C_WQ), (P_SU, C_SU), (P_SV, C_SV)):
                    with sp.Fori(0, 2) as i:
                        for s in range(2):
                            cols(s, i * 2 + (pos + s), w_in, i * 256 + (c + s * 128))
                for b, (nm, g, _) in enumerate(BRANCHES):
                    w_br = A[{"ml": "w_br_mlstm", "sg": "w_br_gmlp", "sw": "w_br_swa"}[nm]][ds(l, 1)] \
                        .rearrange("l (k p) c -> p (l k) c", p=128)
                    with sp.Fori(0, 2) as q:
                        for e in range(6):
                            pos = q * 6 + (P_BR + 12 * b + e)
                            if e % 3 < 2:
                                cols(e % 2, pos, w_in, q * 512 + (C_GL + g * D + (e // 3 * 2 + e % 3) * 128))
                            else:
                                load(e % 2, pos, RAW[e % 2][:, 0:1024].rearrange("p (k c) -> p k c", k=4),
                                     w_br[:, :, ds(q * 512 + e // 3 * 256, 256)])
                w_out = A["w_out"][ds(l, 1)].rearrange("l (k p) c -> p (l k) c", p=128)
                with sp.Fori(0, 4) as i:
                    for s in range(2):
                        cols(s, i * 2 + (P_WO + s), w_out, i * 256 + s * 128)
                w_fi = A["w_ffn_in"][ds(l, 1)].rearrange("l (k p) c -> p (l k) c", p=128)
                w_fo = A["w_ffn_out"][ds(l, 1)].rearrange("l (k p) c -> p (l k) c", p=128)
                pos, j0 = P_FFN, 0
                for nb in BLOCKS:
                    with sp.Fori(0, nb) as j:
                        for s in range(2):
                            cols(s, j * 2 + (pos + s), w_fi, j * 128 + (s * FFN + j0 * 128))
                    pos += 2 * nb
                    with sp.Fori(0, 4) as i:
                        for s in range(2):
                            load(s, i * 2 + (pos + s), RAW[s][:, 0:nb * 128].rearrange("p (k c) -> p k c", k=nb),
                                 w_fo[:, j0:j0 + nb, ds(i * 256 + s * 128, 128)])
                    pos += 8
                    j0 += nb
            for t in range(NTT + 1):
                sp.wait_ge(x_out_copied, t + 1)
                if t < NTT:
                    sp.dma_start(O["y_prompt"][0, t * 128:(t + 1) * 128, :], XIO[:, t, :]).then_inc(out_done, 16)
                else:
                    sp.dma_start(O["y_sample"][0, :, :], XIO[0:64, t, :]).then_inc(out_done, 16)
            sp.wait_ge(out_done, 16 * (NTT + 1))

        @block.gpsimd
        def _(pool):
            with pool.Fori(0, DEPTH) as l:
                def split(s, pos, size, loads, more=0):
                    pool.wait_ge(raw_loaded[s], l * (16 * RAW_LOADS[s]) + loads * 16 + (16 + more))
                    pool.wait_ge(chunk_used, l * NCH + (pos + 1))
                    carry(pool)
                    pool.tensor_copy(HI[s][:, 0:size], RAW[s][:, 0:size]).then_inc(chunk_hi, 1)
                    pool.wait_ge(chunk_hi, l * NCH + (pos + 1))
                    pool.tensor_tensor(LO[s][:, 0:size], RAW[s][:, 0:size], HI[s][:, 0:size].bitcast(f32),
                                       ALU.subtract).then_inc(chunk_split, 1)
                with pool.Fori(0, 4) as i:
                    for s in range(2):
                        split(s, i * 2 + s, 1024, i)
                split(0, P_WVIF, SLOT, 4, 16)
                split(1, P_WK, 1024, 4)
                tail = NCH - 8
                with pool.Fori(5, tail // 2) as i:
                    for s in range(2):
                        split(s, i * 2 + s, 1024, i, 16 * (s == 0))
                with pool.Fori(tail // 2, NCH // 2) as i:
                    for s in range(2):
                        split(s, i * 2 + s, BLOCKS[-1] * 128, i, 16 * (s == 0))

        @block.tensor
        def _(pe):
            pe.wait_ge(consts_loaded, 16)
            pe.wait_ge(x_loaded, 16 * 7)
            for t in range(NTT + 1):
                n = 128 if t < NTT else 64
                if t == NTT:
                    pe.wait_ge(init_done, 1)
                for k in range(8):
                    m = pe.transpose(PS[:, t % 4, k * 128:k * 128 + n], XIO[0:n, t, k * 128:(k + 1) * 128],
                                     IDN[0:n, 0:n])
                m.then_inc(x_in_t, 1)
            pe.wait_ge(init_done, 2)
            pe.transpose(PS[:, 1, 0:16], MID[0:16, 0, 0:128], IDN[0:16, 0:16]).then_inc(x_in_t, 1)

            with pe.Fori(0, DEPTH) as l:
                def feature_group(name, s, nk, w, c0, mh, ml, i=0, moving=None):
                    pe.wait_ge(unit_of(name), empty(l, name, i))
                    o = halves(name)
                    wh, wl = (x[s][:, 0:nk * w].rearrange("p (k c) -> p k c", k=nk) for x in (HI, LO))
                    for k in range(nk):
                        if moving is not None:
                            pe.wait_ge(moving[0], nth(moving[0], l, moving[1] + k))
                        for a, mv, first in ((wh, mh, True), (wh, ml, False), (wl, mh, False)):
                            for h in range(2):
                                m = pe.matmul(o[:, h, :], a[:, k, c0:c0 + 128], mv(k, h),
                                              start=(k == 0 and first), stop=(k == nk - 1 and a is wl))
                    m.then_inc(done_by(name), 1)

                def token_group(name, s, w):
                    pe.wait_ge(unit_of(name), empty(l, name))
                    wh, wl = (x[s][:, 0:8 * w].rearrange("p (k c) -> p k c", k=8) for x in (HI, LO))
                    per = 4 if w == 128 else 3
                    for t in range(NTT + 1):
                        c = t * w if t < per else 512 + (t - per) * w
                        for k in range(8):
                            for st, mv, first in ((HH, wh, True), (HH, wl, False), (HL, wh, False)):
                                m = pe.matmul(unit(name)[:, c:c + w], st[:, k * T + t * 128:k * T + t * 128 + 128],
                                              mv[:, k, :], start=(k == 0 and first), stop=(k == 7 and st is HL))
                    m.then_inc(done_by(name), 1)

                def hmov(x):
                    return lambda k, h: x[:, k * T + h * HALF:k * T + (h + 1) * HALF]

                HM = (hmov(HH), hmov(HL))

                def main(name, pos, s, i=0):
                    pe.wait_ge(chunk_split, split_count(l, pos))
                    feature_group(name, s, 8, 128, 0, *HM, i=i)

                def token_sums(name, k, sq, first, last):
                    for t in range(NTT + 1):
                        n = 128 if t < NTT else 64
                        m = pe.matmul(unit(name)[0:n, t:t + 1], sq[:, t * 128:t * 128 + n], ONES[:, 0:1],
                                      start=(first and t == 0), stop=last, skip_group_check=True)
                    return m

                def spread(name, which):
                    pe.wait_ge(unit_of(name), empty(l, name))
                    pe.wait_ge(dg_ready, nth(dg_ready, l, which))
                    pe.matmul(unit(name)[:, 0:512], ONES, R[:, 0:512], start=True, stop=True)
                    pe.matmul(unit(name)[:, 512:576], ONES[0:64, :], R[0:64, 512:576], start=True, stop=True).then_inc(done_by(name), 1)

                def norm(name, first, which):
                    pe.wait_ge(unit_of(name), empty(l, name))
                    for k in range(8):
                        pe.wait_ge(sqn_ready, nth(sqn_ready, l, first + k))
                        m = token_sums(name, k, SQ[:, k % 2, :], k == 0, k == 7)
                        if k < 7:
                            m.then_inc(sqn_used, 1)
                    m.then_inc(done_by(name), 1)
                    spread(name + "b", which)

                def post(name, which):
                    pe.wait_ge(unit_of(name), empty(l, name))
                    pe.wait_ge(acc_added, nth(acc_added, l, 8 * which + 7))
                    token_sums(name, 0, ACC[:, :], True, True).then_inc(done_by(name), 1)
                    spread(name + "b", 1 + 2 * which)

                pe.wait_ge(param_loaded, l * (16 * PARAM_DMAS) + 16 * PARAM_DMAS)
                pe.wait_ge(unit_of("par"), empty(l, "par"))
                pe.transpose(unit("par")[:, 0:80], VROWS, IDN[0:80, 0:80]).then_inc(done_by("par"), 1)
                pe.wait_ge(unit_of("wst"), empty(l, "wst"))
                for g in range(4):
                    m = pe.transpose(unit("wst")[:, g * 128:(g + 1) * 128], WSP[:, g, :], IDN)
                m.then_inc(done_by("wst"), 1)
                pe.wait_ge(cs_ready, 1)
                with pe.Fori(0, 6) as j:
                    for q in range(4):
                        nm = f"ada{q}"
                        s = q // 2
                        if q % 2 == 0:
                            pe.wait_ge(ada_loaded[s], l * (6 * 16) + j * 16 + 16)
                        pe.wait_ge(unit_of(nm), empty(l, nm, j))
                        wv = ADA[:, s, :].rearrange("p (k c) -> p k c", k=8)
                        for n in range(2):
                            c0 = (q % 2) * 256 + n * 128
                            for k in range(8):
                                m = pe.matmul(unit(nm)[:, 2 * n:2 * n + 2], wv[:, k, c0:c0 + 128], CS[:, k, :],
                                              start=(k == 0), stop=(k == 7))
                        m.then_inc(done_by(nm), 1)
                pe.wait_ge(unit_of("ckt"), empty(l, "ckt"))
                pe.transpose(unit("ckt")[:, 0:128], CKR, IDN).then_inc(done_by("ckt"), 1)
                norm("n1", 0, 0)
                with pe.Fori(0, 2) as i:
                    for e in range(4):
                        pe.wait_ge(chunk_split, split_count(l, i * 4 + e))
                        feature_group(f"qk{e}", e % 2, 8, 128, 0, *HM, i=i,
                                      moving=(hl_ready, 0) if e == 0 else None)

                pe.wait_ge(chunk_split, split_count(l, P_WVIF))
                token_group("wvif", 0, 136)
                main("wk", P_WK, 1)
                pe.wait_ge(unit_of("gt1"), empty(l, "gt1"))
                if apart("wvif", "gt1"):
                    pe.wait_ge(unit_of("wvif"), read(l, "wvif"))
                for c, o in ((0, 0), (4, 512)):
                    for t in range(NTT):
                        m = pe.transpose(unit("gt1")[0:4, o + t * 128:o + (t + 1) * 128], IFT[:, t, c:c + 4], IDN)
                m.then_inc(done_by("gt1"), 1)
                pe.wait_ge(unit_of("gt2"), empty(l, "gt2"))
                carry(pe, "gt2")
                for c, o in ((0, 0), (4, 512)):
                    m = pe.transpose(unit("gt2")[0:4, o:o + 64], IFT[0:64, 4, c:c + 4], IDN[0:64, 0:64])
                m.then_inc(done_by("gt2"), 1)

                def v_chunk(h):
                    pe.wait_ge(chunk_split, split_count(l, P_V + h))
                    token_group(f"v{h}", h % 2, 128)

                def key_transposes(h):
                    pe.wait_ge(unit_of(f"kt{h}"), empty(l, f"kt{h}"))
                    if h == 0:
                        if apart("qk7", "kt0"):
                            pe.wait_ge(unit_of("qk7"), read(l, "qk7"))
                    o = unit(f"kt{h}")
                    for t in range(NTT):
                        m = pe.transpose(o[:, t * 128:(t + 1) * 128], QK[:, 4 + h, t * 128:(t + 1) * 128], IDN)
                    m = pe.transpose(o[0:64, 512:640], QK[:, 4 + h, SEQ:T], IDN)
                    m.then_inc(done_by(f"kt{h}"), 1)

                def state(h):
                    pe.wait_ge(unit_of(f"cm{h}"), empty(l, f"cm{h}"))
                    if apart(f"kt{h}", f"cm{h}"):
                        pe.wait_ge(unit_of(f"kt{h}"), read(l, f"kt{h}"))
                    o = unit(f"cm{h}")
                    for t in range(NTT):
                        pe.matmul(o[:, 0:129], KW[:, t, :], VT[:, t, h, :], start=(t == 0), stop=(t == NTT - 1))
                    pe.matmul(o[:, 512:641], KW[0:64, 4, :], VT[0:64, 4, h, :], start=True, stop=True).then_inc(done_by(f"cm{h}"), 1)

                def scores(h):
                    n1, n2, n3 = _a(h)
                    pe.wait_ge(unit_of(n1), empty(l, n1))
                    pe.wait_ge(rows_ready, nth(rows_ready, l))
                    o = unit(n1)
                    pe.matmul(o[:, 0:512], SEL[0:4, h, :], NM[:, 0:512], start=True, stop=True)
                    pe.matmul(o[:, 512:576], SEL[0:4, h, :], NM[:, 512:576], start=True, stop=True)
                    pe.matmul(o[:, 576:640], SEL[0:4, h, :], WIN[:, :], start=True, stop=True).then_inc(done_by(n1), 1)
                    for nm, js in ((n2, (0, 1, 3)), (n3, (2, 4))):
                        pe.wait_ge(unit_of(nm), empty(l, nm))
                        base = 0 if nm is n2 else 1024
                        for j in js:
                            k0, k1 = (j * 128, j * 128 + 128) if j < 4 else (SEQ, T)
                            c = WOFF[j] - base
                            m = pe.matmul(unit(nm)[0:k1 - k0, c:c + (SEQ if j < 4 else T) - k0],
                                          QK[:, 4 + h, k0:k1], QK[:, h, k0:(SEQ if j < 4 else T)],
                                          start=True, stop=True)
                        m.then_inc(done_by(nm), 1)

                def outputs(h):
                    n1 = _b(h)[0][0]
                    pe.wait_ge(unit_of(n1), empty(l, n1))
                    if apart(_a(h)[2], n1):
                        pe.wait_ge(unit_of(_a(h)[2]), read(l, _a(h)[2]))
                    for t in range(NTT):
                        c = t * 129 if t < 3 else 512
                        for j in range(t + 1):
                            w0 = WOFF[j] + 128 * (t - j)
                            pe.matmul(unit(n1)[:, c:c + 129], W[:, w0:w0 + 128], VT[:, j, h, :],
                                      start=(j == 0), stop=(j == t))
                    o = unit(n1)[0:64, 641:770]
                    pe.matmul(o, W[0:64, 1280:1344], VT[0:64, 4, h, :], start=True, stop=False)
                    pe.matmul(o, DM[:, 512:576], C0N[:, h, :], start=False, stop=True).then_inc(done_by(n1), 1)

                def back(h):
                    nm = _b(h)[1][0]
                    pe.wait_ge(unit_of(nm), empty(l, nm))
                    if apart(_b(h)[0][0], nm):
                        pe.wait_ge(unit_of(_b(h)[0][0]), read(l, _b(h)[0][0]))
                    for t in range(NTT):
                        pe.transpose(unit(nm)[:, t * 128:(t + 1) * 128], YTK[:, t, :], IDN)
                    pe.transpose(unit(nm)[:, 512:576], YTK[0:64, 4, :], IDN[0:64, 0:64]).then_inc(done_by(nm), 1)

                v_chunk(0)
                pe.wait_ge(unit_of("gt3"), empty(l, "gt3"))
                pe.wait_ge(rows_ready, nth(rows_ready, l))
                carry(pe, "gt3")
                o = unit("gt3")
                for x, c in ((AR, 0), (WR, 20), (EM, 44)):
                    for t in range(NTT + 1):
                        n = 128 if t < NTT else 64
                        pe.transpose(o[0:n, c + 4 * t:c + 4 * t + 4], x[:, t * 128:t * 128 + n], IDN[0:4, 0:4])
                for h in range(4):
                    m = pe.matmul(o[:, 40 + h:41 + h], SEL[0:4, h, :], WIN[:, 63:64], start=True, stop=True)
                m.then_inc(done_by("gt3"), 1)
                v_chunk(1)
                key_transposes(0)
                v_chunk(2)
                state(0)
                key_transposes(1)
                v_chunk(3)
                state(1)
                key_transposes(2)
                main("mo0", P_MO, 0)
                state(2)
                key_transposes(3)
                main("mo1", P_MO + 1, 1)
                state(3)
                scores(0)
                main("mo2", P_MO + 2, 0)
                outputs(0)
                main("mo3", P_MO + 3, 1)
                back(0)
                scores(1)
                main("wq0", P_WQ, 0)
                outputs(1)
                main("wq1", P_WQ + 1, 1)
                back(1)
                scores(2)
                main("wq2", P_WQ + 2, 0)
                outputs(2)
                main("wq3", P_WQ + 3, 1)
                back(2)
                scores(3)
                main("su0", P_SU, 0)
                outputs(3)

                def rope(i):
                    nm = f"r{i}"
                    pe.wait_ge(unit_of(nm), empty(l, nm))
                    if i == 4:
                        if apart("wk", nm):
                            pe.wait_ge(unit_of("wk"), read(l, "wk"))
                        src = KALL[:, 0, 0:T]
                    else:
                        if apart(f"wq{i}", nm):
                            pe.wait_ge(unit_of(f"wq{i}"), read(l, f"wq{i}"))
                        src = WQ[:, i, :]
                    for h in range(2):
                        m = pe.matmul(halves(nm)[:, h, :], K_["perm"], src[:, h * HALF:(h + 1) * HALF],
                                      start=True, stop=True)
                    m.then_inc(done_by(nm), 1)

                main("su1", P_SU + 1, 1)
                back(3)
                rope(4)
                rope(0)
                main("su2", P_SU + 2, 0)
                rope(1)
                rope(2)
                main("su3", P_SU + 3, 1)
                rope(3)
                pe.wait_ge(unit_of("ko"), empty(l, "ko"))
                pe.wait_ge(rope_ready, nth(rope_ready, l, 0))
                pe.transpose(unit("ko")[:, 0:128], KALL[:, 0, SEQ - 128:SEQ], IDN)
                pe.transpose(unit("ko")[0:64, 128:256], KALL[:, 0, SEQ:T], IDN).then_inc(done_by("ko"), 1)

                def keys(t):
                    return (0, 128) if t == 0 else ((SEQ, 704) if t == NTT else (128 * (t - 1), 128 * (t + 1)))

                def sw_scores(i):
                    t, g = SWA[i]
                    nm = f"sc{i}"
                    pe.wait_ge(unit_of(nm), empty(l, nm))
                    if i == 0:
                        pe.wait_ge(rope_ready, nth(rope_ready, l, 4))
                        pe.wait_ge(kx_moved, l * 32 + 32)
                    if SWA[i][0] == NTT:
                        carry(pe, nm)
                    n = 128 if t < NTT else 64
                    k0, k1 = keys(t)
                    for r_ in range(4):
                        h = 4 * g + r_
                        b = 64 * (h % 2)
                        c = (2 * (h % 2) + r_ // 2) * 256
                        m = pe.matmul(unit(nm)[0:n, c:c + k1 - k0],
                                      WQ[b:b + 64, h // 2, t * 128:t * 128 + n],
                                      KALL[b:b + 64, 0 if g == h % 2 else 1, k0:k1], start=True, stop=True)
                    m.then_inc(done_by(nm), 1)

                def sw_transposes(i):
                    t, g = SWA[i]
                    nm = f"tp{i}"
                    pe.wait_ge(unit_of(nm), empty(l, nm))
                    pe.wait_ge(pn_ready, nth(pn_ready, l, i))
                    if SWA[i][0] == NTT:
                        carry(pe, nm)
                    n = 128 if t < NTT else 64
                    o = unit(nm).rearrange("p (a r c) -> p a r c", a=2, r=4)
                    for a, (c0, c1) in enumerate(((0, 128), (128, 256))[:1 if t == 0 else 2]
                                                 if t < NTT else ((0, 64), (64, 192))):
                        for r_ in range(4):
                            m = pe.transpose(o[0:c1 - c0, a, r_, 0:n], SM[0:n, i % 2, r_, c0:c1], IDN[0:n, 0:n])
                    m.then_inc(done_by(nm), 1)

                def sw_output(i):
                    t, g = SWA[i]
                    nm = f"pv{i}"
                    pe.wait_ge(unit_of(nm), empty(l, nm))
                    if apart(f"tp{i}", nm):
                        pe.wait_ge(unit_of(f"tp{i}"), read(l, f"tp{i}"))
                    if SWA[i][0] == NTT:
                        carry(pe, nm)
                    n = 128 if t < NTT else 64
                    p = PT[:, :, :].rearrange("p a (r c) -> p a r c", r=4)
                    v = VSW[:, :, g * 64:(g + 1) * 64]
                    if t == 0:
                        parts = [(v[:, 0, :], 0, 128)]
                    elif t < NTT:
                        parts = [(v[:, t - 1, :], 0, 128), (v[:, t, :], 1, 128)]
                    else:
                        parts = [(v[0:64, 4, :], 0, 64), (CV[:, g * 64:(g + 1) * 64], 1, 128)]
                    for odd in range(2):
                        o = unit(nm)[64 * odd:64 * odd + 64, 0:2 * n].rearrange("p (r c) -> p r c", r=2)
                        for x, (st, a, kk) in enumerate(parts):
                            m = pe.matmul(o, st, p[0:kk, a, 2 * odd:2 * odd + 2, 0:n], start=(x == 0),
                                          stop=(x == len(parts) - 1))
                    m.then_inc(done_by(nm), 1)

                def slot(i):
                    if 0 <= i - 2 < NS:
                        sw_output(i - 2)
                    if 0 <= i - 1 < NS:
                        sw_transposes(i - 1)
                    if i < NS:
                        sw_scores(i)

                for i in range(4):
                    pe.wait_ge(chunk_split, split_count(l, P_SV + i))
                    token_group(f"sv{i}", i % 2, 128)
                    slot(i)

                def ymov(x, st):
                    return lambda k, h: x[:, st * 4 + k, h * HALF:(h + 1) * HALF]

                def spatial(g):
                    nm = f"z{g}"
                    pe.wait_ge(unit_of(nm), empty(l, nm))
                    pe.wait_ge(ln_ready, nth(ln_ready, l, 4))
                    o = unit(nm)
                    for t in range(NTT + 1):
                        n = 128 if t < NTT else 64
                        pe.matmul(o[:, t * 128:t * 128 + n], SV[0:n, t, g * 128:(g + 1) * 128], WST[0:n, g, 0:n],
                                  start=True, stop=False)
                        m = pe.matmul(o[:, t * 128:t * 128 + n], ONES[0:1, :], BSP[0:1, g * 128:g * 128 + n],
                                      start=False, stop=True)
                    m.then_inc(done_by(nm), 1)

                def branch(b, n, pos, s, i=0):
                    pe.wait_ge(chunk_split, split_count(l, pos))
                    st = BRANCHES[b][2]
                    for e in range(2):
                        feature_group(f"br{b}_{n + e}", s, 4, 256, e * 128, ymov(YH, st), ymov(YL, st), i=i)

                x = 4
                for n in range(0, 8, 2):
                    pos = P_BR + 3 * (n // 2)
                    for e in range(2):
                        main(f"g0_{n + e}", pos + e, (pos + e) % 2)
                        slot(x)
                        x += 1
                    if n == 0:
                        pe.wait_ge(yl_ready, nth(yl_ready, l, 3))
                    branch(0, n, pos + 2, pos % 2)
                    slot(x)
                    x += 1
                for n in range(0, 8, 2):
                    pos = P_BR + 12 + 3 * (n // 2)
                    for e in range(2):
                        main(f"g1_{n + e}", pos + e, (pos + e) % 2)
                    spatial(n // 2)
                    if n == 0:
                        if apart(f"pv{NS - 1}", "br1_0"):
                            pe.wait_ge(unit_of(f"pv{NS - 1}"), read(l, f"pv{NS - 1}"))
                    branch(1, n, pos + 2, pos % 2)
                with pe.Fori(0, 2) as q:
                    for n in range(0, 4, 2):
                        e0 = 3 * (n // 2)
                        for e in range(2):
                            main(f"g2_{n + e}", q * 6 + (P_BR + 24 + e0 + e), (e0 + e) % 2, i=q * 2)
                        if n == 0:
                            pe.wait_ge(yl_ready, nth(yl_ready, l, 7))
                        branch(2, n, q * 6 + (P_BR + 24 + e0 + 2), e0 % 2, i=q * 2)
                with pe.Fori(0, 2) as i:
                    for e in range(4):
                        pe.wait_ge(chunk_split, split_count(l, i * 4 + (P_WO + e)))
                        feature_group(f"wo{e}", e % 2, 8, 128, 0, *HM, i=i,
                                      moving=(hl_ready, 8) if e == 0 else None)
                post("p1", 0)
                norm("n2", 8, 2)
                pos, j0 = P_FFN, 0
                for c, nb in enumerate(BLOCKS):
                    with pe.Fori(0, nb // 2) as i:
                        for e in range(4):
                            pe.wait_ge(chunk_split, split_count(l, i * 4 + (pos + e)))
                            feature_group(
                                f"fi{c}_{e}", e % 2, 8, 128, 0, *HM, i=i,
                                moving=(hl_ready, 16) if (c, e) == (0, 0) else None)
                    pos += 2 * nb
                    gm = (lambda k, h: YH[:, k, h * HALF:(h + 1) * HALF], lambda k, h: YL[:, k, h * HALF:(h + 1) * HALF])
                    with pe.Fori(0, 2) as i:
                        for e in range(4):
                            pe.wait_ge(chunk_split, split_count(l, i * 4 + (pos + e)))
                            feature_group(
                                f"fo{c}_{e}", e % 2, nb, 128, 0, *gm, i=i,
                                moving=(gl_ready, j0) if e == 0 else None)
                    pos += 8
                    j0 += nb
                post("p2", 1)

            pe.wait_ge(x_ready, nth(x_ready, DEPTH, 7))
            for t in range(NTT + 1):
                n = 128 if t < NTT else 64
                if t == NTT:
                    pe.wait_ge(x_out_copied, 1)
                for k in range(8):
                    m = pe.transpose(PS[0:n, t % 4, k * 128:(k + 1) * 128], X[:, k, t * 128:t * 128 + n], IDN)
                m.then_inc(x_out_t, 1)

        @block.scalar
        def _(act):
            step = Steps(ACT_STEPS)
            act.wait_ge(init_done, 6)
            for b in range(2):
                m = act.activation(CS[:, :, b], CC[:, 8 * b:8 * b + 8], ACT.Silu)
            m.then_inc(cs_ready, 1)

            with act.Fori(0, DEPTH) as l:
                step.layer(l)

                def par(dst, src, **how):
                    act.dma_start(dst, src, **how).then_inc(param_loaded, 16)

                def row(name):
                    return A[name][ds(l, 1)]

                act.wait_ge(x_ready, nth(x_ready, l, 7))
                par(VROWS[0:48, :], row("b_ada").rearrange("l (k p) -> (l k) p", p=128))
                for i, nm in enumerate(("g_pre_mix", "g_post_mix", "g_pre_ffn", "g_post_ffn")):
                    par(VROWS[48 + 8 * i:56 + 8 * i, :], row(nm).rearrange("l (k p) -> (l k) p", p=128))
                par(WSP, row("w_spatial").rearrange("l g p r -> p (l g) r"))
                par(CKR, row("cache_swa_k").rearrange("l b k g d -> (l b k) (g d)"))
                par(CV[:, :], row("cache_swa_v").rearrange("l b k g d -> (l b k) (g d)"))
                par(BSP[:, :], row("b_spatial").rearrange("l g p -> l (g p)"))
                par(BIF[:, 0:4], row("b_igate").to_broadcast([128, 4]))
                par(BIF[:, 4:8], row("b_fgate").to_broadcast([128, 4]))
                par(SINK[:, :], row("swa_sinks").to_broadcast([128, 8]))
                par(C0N[:, :, 0:128], row("state_mlstm_C").rearrange("l b h d e -> d (l b h) e"))
                par(C0N[:, :, 128:129], row("state_mlstm_n").rearrange("l b h (d o) -> d (l b h) o", o=1),
                    allow_slow_non_contiguous=True)
                par(M0[:, :], row("state_mlstm_m").rearrange("l b (h o) -> (l b h) o", o=1))

                def cols(x, k):
                    return x[:, k * T:(k + 1) * T]

                def squares(first):
                    for k in range(8):
                        act.wait_ge(x_ready, nth(x_ready, l, first + k))
                        if k >= 2:
                            act.wait_ge(sqn_used, nth(sqn_used, l, (7 if first else 0) + k - 2))
                        act.activation(SQ[:, k % 2, :], X[:, k, :], ACT.Square).then_inc(sqn_ready, 1)

                def roots(which, src, dst):
                    act.wait_ge(ms_ready, nth(ms_ready, l, which))
                    act.activation(dst, src, ACT.Sqrt).then_inc(rt_ready, 1)

                def h_hi(first, part):
                    for k in range(8):
                        act.wait_ge(hs_ready, nth(hs_ready, l, first + k))
                        h = cols(HH, k)
                        act.activation(h[:, 0:SEQ], TS[:, k % 2, 0:SEQ], ACT.Identity, bias=MOD[:, part, k, 0:1])
                        act.activation(h[:, SEQ:T], TS[:, k % 2, SEQ:T], ACT.Identity, bias=MOD[:, part, k, 1:2]) \
                           .then_inc(hh_ready, 1)

                squares(0)
                roots(0, RC[:, :], RC[:, :])
                h_hi(0, 0)

                with act.Fori(0, 2) as i:
                    for e in range(4):
                        act.wait_ge(done_by(f"qk{e}"), done(l, f"qk{e}", i * 4))
                        act.activation(QK[:, ds(i * 4 + e, 1), :].rearrange("p o (a c) -> p (o a) c", a=2),
                                            halves(f"qk{e}"), ACT.Copy).then_inc(unit_of(f"qk{e}"), 1)

                def tile(name, dst, func=ACT.Copy, scale=1.0, i=0, c=0):
                    act.wait_ge(done_by(name), done(l, name, c))
                    act.activation(split2(dst), halves(name), func, scale=scale).then_inc(unit_of(name), 1)

                tile("wk", KALL[:, 0, 0:T])
                act.wait_ge(nabs_ready, nth(nabs_ready, l))
                act.activation(LFT, WR, ACT.Exp).then_inc(act_step, step())
                act.wait_ge(act_step, step.all())
                act.activation(WR, LFT, ACT.Ln, bias=1.0).then_inc(sp_ready, 1)
                act.wait_ge(m_ready, nth(m_ready, l))
                act.activation(EM, IG, ACT.Exp, scale=-1.0)
                for j, (a, b) in enumerate(((0, SEQ), (SEQ, T))):
                    act.activation(WR[:, a:b], AR[:, a:b], ACT.Exp, bias=NML[:, j:j + 1])
                act.activation(WIN[:, :], NM[:, SEQ:T], ACT.Exp, bias=M0[:, :]).then_inc(rows_ready, 1)
                for nm, c in (("m_prompt", SEQ - 1), ("m_sample", T - 1)):
                    act.dma_start(O[nm][ds(l, 1)].rearrange("l b (h o) -> (l b h) o", o=1), IG[:, c:c + 1]) \
                       .then_inc(c_stored, 16)

                def store_state(h):
                    act.wait_ge(unit_of(f"cm{h}"), read(l, f"cm{h}"))
                    for j, w in enumerate(("prompt", "sample")):
                        act.dma_start(O[f"C_{w}"][ds(l, 1), 0, h].rearrange("l d e -> (l d) e"), COUT[:, h, j, 0:128]) \
                           .then_inc(c_stored, 16)
                        act.dma_start(O[f"n_{w}"][ds(l, 1), 0, h].rearrange("l (d o) -> (l d) o", o=1),
                                      COUT[:, h, j, 128:129]).then_inc(c_stored, 16)

                def decay(h):
                    n1 = _a(h)[0]
                    if h == 0:
                        act.wait_ge(unit_of("gt3"), read(l, "gt3"))
                    act.wait_ge(d_ready, nth(d_ready, l, h))
                    for j in range(3):
                        m = act.activation(W[:, WOFF[j] + 128:WOFF[j] + SEQ - 128 * j],
                                           unit(n1)[:, 128 * (j + 1):SEQ], ACT.Exp, bias=AS[:, j, h:h + 1])
                    m.then_inc(unit_of(n1), 1)
                    for j in range(4):
                        act.activation(W[:, WOFF[j]:WOFF[j] + 128], DM[:, 128 * j:128 * j + 128], ACT.Exp,
                                       bias=AS[:, j, h:h + 1])
                    act.activation(W[0:64, 1280:1344], W[0:64, 1280:1344], ACT.Exp, bias=AS[0:64, 4, h:h + 1]) \
                       .then_inc(w_ready, 1)

                def y_hi(i, src):
                    act.activation(YH[:, i % 4, :], src, ACT.Copy).then_inc(yh_ready, 1)

                def head_hi(h):
                    act.wait_ge(unit_of(_b(h)[1][0]), read(l, _b(h)[1][0]))
                    y_hi(h, YT[:, :])

                tile("mo0", MO[:, 0, :], ACT.Tanh, 0.5)
                store_state(0)
                store_state(1)
                tile("mo1", MO[:, 1, :], ACT.Tanh, 0.5)
                store_state(2)
                decay(0)
                tile("mo2", MO[:, 2, :], ACT.Tanh, 0.5)
                store_state(3)
                tile("mo3", MO[:, 3, :], ACT.Tanh, 0.5)
                head_hi(0)
                decay(1)
                tile("wq0", WQ[:, 0, :])
                tile("wq1", WQ[:, 1, :])
                head_hi(1)
                decay(2)
                tile("wq2", WQ[:, 2, :])
                tile("wq3", WQ[:, 3, :])
                head_hi(2)
                decay(3)
                tile("su0", SU[:, 0, :])
                tile("su1", SU[:, 1, :])
                head_hi(3)
                act.wait_ge(unit_of(_a(3)[2]), read(l, _a(3)[2]))
                for dst, nm in ((LNG, "ln_v_g"), (LNB, "ln_v_b")):
                    act.dma_start(dst, row(nm).to_broadcast([128, 512])).then_inc(ln_loaded, 16)
                act.wait_ge(rope_ready, nth(rope_ready, l, 0))
                act.wait_ge(unit_of("ckt"), read(l, "ckt"))
                act.dma_start(KALL[0:64, 1, :], KALL[64:128, 0, :]).then_inc(kx_moved, 16)
                act.dma_start(KALL[64:128, 1, :], KALL[0:64, 0, :]).then_inc(kx_moved, 16)
                tile("su2", SU[:, 2, :])
                tile("su3", SU[:, 3, :])
                act.wait_ge(unit_of("ko"), read(l, "ko"))
                for nm, src in (("k_prompt", KOUT[:, 0, :]), ("k_sample", KOUT[0:64, 1, :]),
                                ("v_prompt", VSW[:, NTT - 1, :]), ("v_sample", VSW[0:64, NTT, :])):
                    act.dma_start(O[nm][ds(l, 1)].rearrange("l b k g d -> (l b k) (g d)"), src).then_inc(o_stored, 16)
                act.wait_ge(c_stored, l * (16 * C_STORES) + 16 * C_STORES)

                def sw_hi(i):
                    t, g = SWA[i]
                    n = 128 if t < NTT else 64
                    act.wait_ge(done_by(f"pv{i}"), done(l, f"pv{i}"))
                    act.activation(YH[:, 4 + 2 * g:6 + 2 * g, t * 128:t * 128 + n],
                                   unit(f"pv{i}")[:, 0:2 * n].rearrange("p (r c) -> p r c", r=2), ACT.Copy) \
                       .then_inc(oh_ready, 1)

                def sw_pt(i):
                    t, g = SWA[i]
                    nm = f"tp{i}"
                    act.wait_ge(done_by(nm), done(l, nm))
                    if t == 0:
                        m = act.activation(PT[:, 0, :], unit(nm)[:, 0:512], ACT.Copy)
                    elif t < NTT:
                        m = act.activation(PT[:, :, :], unit(nm).rearrange("p (a c) -> p a c", a=2), ACT.Copy)
                    else:
                        for a, kk in ((0, 64), (1, 128)):
                            m = act.activation(PT[0:kk, a, :].rearrange("p (r c) -> p r c", r=4)[:, :, 0:64],
                                               unit(nm)[0:kk, a * 512:(a + 1) * 512]
                                               .rearrange("p (r c) -> p r c", r=4)[:, :, 0:64], ACT.Copy)
                    m.then_inc(unit_of(nm), 1)

                def sw_exp(i):
                    t, g = SWA[i]
                    n = 128 if t < NTT else 64
                    kw = 128 if t == 0 else (192 if t == NTT else 256)
                    act.wait_ge(mx_ready, nth(mx_ready, l, i))
                    for r_ in range(4):
                        x = SM[0:n, i % 2, r_, 0:kw]
                        act.activation(x, x, ACT.Exp, bias=MX[0:n, i % 2, 1, r_:r_ + 1],
                                       accum_out=MX[0:n, i % 2, 2, r_:r_ + 1])
                    act.activation(MX[0:n, i % 2, 3, :], MX[0:n, i % 2, 3, :], ACT.Exp).then_inc(ex_ready, 1)

                def slot(i):
                    if 0 <= i - 2 < NS:
                        sw_hi(i - 2)
                    if 0 <= i - 1 < NS:
                        sw_pt(i - 1)
                    if i < NS:
                        sw_exp(i)

                for i in range(4):
                    slot(i)

                def gate(b, n, c=0, q=0):
                    if n >= 2:
                        act.wait_ge(unit_of(f"br{b}_{n - 2}"), read(l, f"br{b}_{n - 2}", q))
                    elif b > 0 and b < 2:
                        act.wait_ge(unit_of(f"br{b - 1}_{n + 6}"), read(l, f"br{b - 1}_{n + 6}"))
                    tile(f"g{b}_{n}", TS[:, n % 2, :], ACT.Tanh, 0.5, c=c)

                x = 4
                for n in range(0, 8, 2):
                    for e in range(2):
                        gate(0, n + e)
                        slot(x)
                        x += 1
                    if n == 0:
                        roots(1, LR[:, :], LR[:, :])
                    slot(x)
                    x += 1
                act.wait_ge(ln_ready, nth(ln_ready, l, 4))
                act.dma_start(O["gmlp_v_sample"][ds(l, 1)].rearrange("l b t c -> (l b t) c"), SV[0:64, NTT, :]) \
                   .then_inc(o_stored, 16)
                for n in range(0, 8, 2):
                    gate(1, n)
                    gate(1, n + 1)
                    g = n // 2
                    act.wait_ge(unit_of(f"z{g}"), read(l, f"z{g}"))
                    y_hi(4 + g, WQ[:, 2 + g % 2, :])
                for n in range(2):
                    act.wait_ge(unit_of(f"br1_{n + 6}"), read(l, f"br1_{n + 6}"))
                with act.Fori(0, 2) as q:
                    for n in range(4):
                        act.wait_ge(merged2, before(merged2, l, q * 4 + n))
                        tile(f"g2_{n}", TS[:, n % 2, :], ACT.Tanh, 0.5, c=q * 6)
                for k in range(8):
                    act.wait_ge(merged2, nth(merged2, l, k))
                    act.activation(cols(HH, k), MID[:, k, :], ACT.Copy, scale=0.5).then_inc(hh_ready, 1)

                def o_tile(name, c, n, which):
                    o = OMID[:, ds(n, 1), :].rearrange("p o c -> p (o c)")
                    act.wait_ge(done_by(name), done(l, name, c))
                    act.activation(OMID[:, ds(n, 1), :].rearrange("p o (a c) -> p (o a) c", a=2),
                                        halves(name), ACT.Copy).then_inc(unit_of(name), 1)
                    return o

                with act.Fori(0, 2) as i:
                    for e in range(4):
                        o = o_tile(f"wo{e}", i * 4, i * 4 + e, 0)
                        act.wait_ge(unit_of(f"wo{e}"), read(l, f"wo{e}", i))
                        act.wait_ge(acc_added, before(acc_added, l, i * 4 + e))
                        carry(act)
                        act.activation(SQ[:, e % 2, :], o, ACT.Square).then_inc(sqo_ready, 1)
                roots(2, RC[:, :], RC[:, :])
                squares(8)
                roots(3, RC[:, :], RC[:, :])
                h_hi(8, 3)

                j0, pos = 0, 0
                for c, nb in enumerate(BLOCKS):
                    with act.Fori(0, nb // 2) as i:
                        for e in range(2):
                            act.wait_ge(gl_ready, before(gl_ready, l, i * 2 + (j0 + e)))
                            tile(f"fi{c}_{2 * e}", WQ[:, e, :], ACT.Silu, c=i * 4)
                            g_tmp = TS[:, e, :]
                            act.wait_ge(unit_of(f"fi{c}_{2 * e + 1}"), read(l, f"fi{c}_{2 * e + 1}", i))
                            act.activation(YH[:, ds(i * 2 + e, 1), :].rearrange("p o c -> p (o c)"), g_tmp, ACT.Copy) \
                               .then_inc(gh_ready, 1)
                    if c == 0:
                        with act.Fori(0, 2) as i:
                            for e in range(4):
                                o_tile(f"fo0_{e}", i * 4, i * 4 + e, 1)
                    if c == len(BLOCKS) - 1:
                        with act.Fori(0, 2) as i:
                            for e in range(4):
                                act.wait_ge(unit_of(f"fo{c}_{e}"), read(l, f"fo{c}_{e}", i))
                                act.wait_ge(acc_added, before(acc_added, l, i * 4 + (8 + e)))
                                carry(act)
                                act.activation(SQ[:, e % 2, :],
                                               OMID[:, ds(i * 4 + e, 1), :].rearrange("p o c -> p (o c)"), ACT.Square) \
                                   .then_inc(sqo_ready, 1)
                    j0 += nb
                roots(4, RC[:, :], RC[:, :])
                act.wait_ge(o_stored, l * (16 * O_STORES) + 16 * O_STORES)
                step.end()

        @block.vector
        def _(dve):
            step = Steps(DVE_STEPS)
            RNG = ((0, SEQ, 0), (SEQ, T, 1))
            dve.memset(HH[:, KT_ * T:].bitcast(f32), 0.0).then_inc(chunk_split, 2)
            dve.memset(HL[:, KT_ * T:].bitcast(f32), 0.0).then_inc(chunk_used, 2)
            for t in range(NTT + 1):
                n = 128 if t < NTT else 64
                dve.wait_ge(x_in_t, t + 1)
                dve.tensor_copy(X[:, :, t * 128:t * 128 + n],
                                PS[:, t % 4, :].rearrange("p (k c) -> p k c", k=8)[:, :, 0:n]).then_inc(init_done, 1)
            dve.wait_ge(x_in_t, NTT + 2)
            dve.tensor_copy(CC[:, :], PS[:, 1, 0:16]).then_inc(init_done, 1)
            dve.wait_ge(init_done, NTT + 2)
            for u in range(UNITS):
                dve.memset(LR[:, u:u + 1], 1.0).then_inc(unit_free[u], 1)
            dve.memset(LR[:, 4:5], 1.0).then_inc(x_ready, 8)
            for i, ring in enumerate((acc_added, gl_ready, merged2)):
                dve.memset(BN[:, i:i + 1], 0.0).then_inc(ring, 2)

            with dve.Fori(0, DEPTH) as l:
                step.layer(l)

                def cols(x, k):
                    return x[:, k * T:(k + 1) * T]

                def tt(out, a, b, op):
                    return dve.tensor_tensor(out, a, b, op)

                def bc(ap, shape):
                    return ap.unsqueeze(len(shape) - 1).to_broadcast(shape)

                dve.wait_ge(done_by("par"), done(l, "par"))
                dve.tensor_copy(VCOL[:, :], unit("par")[:, 0:80]).then_inc(unit_of("par"), 1)
                dve.wait_ge(done_by("wst"), done(l, "wst"))
                dve.scalar_tensor_tensor(WST[:, :, :], K_["mneg"].unsqueeze(1).to_broadcast([128, 4, 128]), 0.0,
                                              unit("wst")[:, 0:512].rearrange("p (g c) -> p g c", g=4),
                                              ALU.is_ge, ALU.mult).then_inc(unit_of("wst"), 1)
                dve.wait_ge(unit_of("par"), read(l, "par"))
                carry(dve)
                with dve.Fori(0, 6) as j:
                    for q in range(4):
                        dve.wait_ge(done_by(f"ada{q}"), done(l, f"ada{q}", j * 4))
                        tt(MOD[:, ds(j, 1), 2 * q:2 * q + 2, :].rearrange("p o a b -> p (o a) b"),
                                unit(f"ada{q}")[:, 0:4].rearrange("p (a b) -> p a b", a=2),
                                bc(VCOL[:, ds(j * 8 + 2 * q, 2)], [128, 2, 2]), ALU.add).then_inc(unit_of(f"ada{q}"), 1)
                dve.wait_ge(done_by("ckt"), done(l, "ckt"))
                dve.tensor_copy(KALL[:, 0, T:704], unit("ckt")[:, 0:128]).then_inc(unit_of("ckt"), 1)
                dve.memset(VT[:, :, :, 128:129], 1.0).then_inc(dve_step, step())
                dve.wait_ge(unit_of("ada3"), read(l, "ada3", 5))
                for i, (part, c, plus) in enumerate(((1, 48, 1.0), (2, 56, 0.0), (4, 64, 1.0), (5, 72, 0.0))):
                    dve.scalar_tensor_tensor(SC[:, i, :, :], MOD[:, part, :, :], plus,
                                                  bc(VCOL[:, c:c + 8], [128, 8, 2]), ALU.add, ALU.mult).then_inc(dve_step, step())
                dve.wait_ge(dve_step, step.all())

                def norm_tail(name, which, col=None):
                    dve.wait_ge(done_by(name), done(l, name))
                    for a, b, n in ((0, 4, 128), (4, 5, 64)):
                        m = dve.tensor_scalar(RC[0:n, a:b], unit(name)[0:n, a:b], 1.0 / D, EPS, ALU.mult, ALU.add)
                        if n == 128:
                            m.then_inc(dve_step, step())
                    m.then_inc(unit_of(name), 1)
                    dve.wait_ge(unit_of(name), read(l, name))
                    dve.tensor_scalar(RC[64:128, 4:5], RC[64:128, 3:4], 1.0, None, ALU.mult) \
                       .then_inc(ms_ready, 1)
                    dve.wait_ge(rt_ready, nth(rt_ready, l, which))
                    dve.reciprocal(RC[:, :], RC[:, :]).then_inc(dve_step, step())
                    dve.wait_ge(dve_step, step.all())
                    tt(R[:, 0:512].rearrange("p (t c) -> p t c", t=4),
                            IDN.unsqueeze(1).to_broadcast([128, 4, 128]), bc(RC[:, 0:4], [128, 4, 128]), ALU.mult).then_inc(dve_step, step())
                    dve.tensor_scalar(R[0:64, 512:576], IDN[0:64, 0:64], RC[0:64, 4:5], None, ALU.mult) \
                       .then_inc(dg_ready, 1)
                    dve.wait_ge(done_by(name + "b"), done(l, name + "b"))
                    dve.tensor_copy(R[:, :], unit(name + "b")[:, 0:T]).then_inc(unit_of(name + "b"), 1)
                    dve.wait_ge(unit_of(name + "b"), read(l, name + "b"))

                def pre_norm(name, which, first, sc, sh):
                    norm_tail(name, which)

                    def lo(k):
                        dve.wait_ge(hh_ready, nth(hh_ready, l, (0 if first == 0 else 16) + k))
                        for a, b, j in RNG:
                            m = dve.scalar_tensor_tensor(cols(HL, k)[:, a:b], TS[:, k % 2, a:b], MOD[:, sh, k, j:j + 1],
                                                         cols(HH, k)[:, a:b].bitcast(f32), ALU.add, ALU.subtract)
                        m.then_inc(hl_ready, 1)
                    for k in range(8):
                        if k >= 2:
                            dve.wait_ge(hl_ready, nth(hl_ready, l, (0 if first == 0 else 16) + k - 2))
                        for a, b, j in RNG:
                            m = dve.scalar_tensor_tensor(TS[:, k % 2, a:b], X[:, k, a:b], SC[:, sc, k, j:j + 1],
                                                         R[:, a:b], ALU.mult, ALU.mult)
                        m.then_inc(hs_ready, 1)
                        if k:
                            lo(k - 1)
                    lo(7)

                def post_norm(name, which, first, sc):
                    norm_tail(name, which)
                    for k in range(8):
                        for a, b, j in RNG:
                            dve.scalar_tensor_tensor(TS[:, k % 2, a:b], OMID[:, k, a:b], SC[:, sc, k, j:j + 1],
                                                          R[:, a:b], ALU.mult, ALU.mult).then_inc(dve_step, step())
                        dve.wait_ge(dve_step, step.all())
                        tt(X[:, k, :], X[:, k, :], TS[:, k % 2, :], ALU.add).then_inc(x_ready, 1)

                pre_norm("n1", 0, 0, 0, 0)
                dve.wait_ge(done_by("wvif"), done(l, "wvif"))
                for t0, t1, c in ((0, 3, 0), (3, 5, 512)):
                    o = unit("wvif")[:, c:c + 136 * (t1 - t0)].rearrange("p (t c) -> p t c", c=136)
                    dve.tensor_copy(VSW[:, t0:t1, :], o[:, :, 0:128]).then_inc(dve_step, step())
                    m = tt(IFT[:, t0:t1, :], o[:, :, 128:136], BIF[:, :].unsqueeze(1).to_broadcast([128, t1 - t0, 8]),
                           ALU.add)
                    if t0 == 0:
                        m.then_inc(dve_step, step())
                m.then_inc(unit_of("wvif"), 1)
                dve.wait_ge(done_by("gt1"), done(l, "gt1"))
                dve.tensor_copy(IG[:, 0:512], unit("gt1")[0:4, 0:512]).then_inc(dve_step, step())
                dve.tensor_copy(EM[:, 0:512], unit("gt1")[0:4, 512:1024]).then_inc(unit_of("gt1"), 1)
                dve.wait_ge(done_by("gt2"), done(l, "gt2"))
                dve.tensor_copy(IG[:, 512:576], unit("gt2")[0:4, 0:64]).then_inc(dve_step, step())
                dve.tensor_copy(EM[:, 512:576], unit("gt2")[0:4, 512:576]).then_inc(unit_of("gt2"), 1)
                dve.wait_ge(unit_of("gt1"), read(l, "gt1"))
                dve.wait_ge(unit_of("gt2"), read(l, "gt2"))
                dve.scalar_tensor_tensor(WR, EM, -1.0, EM, ALU.mult, ALU.min).then_inc(nabs_ready, 1)
                dve.wait_ge(sp_ready, nth(sp_ready, l))
                dve.scalar_tensor_tensor(LFT, EM, 0.0, WR, ALU.min, ALU.subtract).then_inc(dve_step, step())
                dve.wait_ge(dve_step, step.all())
                for a, b in ((0, SEQ), (SEQ, T)):
                    dve.tensor_tensor_scan(BC[:, a:b], ONES[0:4, 0:1].to_broadcast([4, b - a]), LFT[:, a:b],
                                                0.0, ALU.mult, ALU.add).then_inc(dve_step, step())
                dve.wait_ge(dve_step, step.all())
                tt(AR, IG, BC, ALU.subtract).then_inc(dve_step, step())
                dve.wait_ge(dve_step, step.all())
                dve.tensor_tensor_scan(IG[:, 0:SEQ], AR[:, 0:SEQ], AR[:, 0:SEQ], 0.0, ALU.max, ALU.max).then_inc(dve_step, step())
                dve.tensor_tensor_scan(IG[:, SEQ:T], AR[:, SEQ:T], AR[:, SEQ:T], M0[:, 0:1], ALU.max, ALU.max).then_inc(dve_step, step())
                dve.wait_ge(dve_step, step.all())
                dve.tensor_scalar(NM, IG, -1.0, None, ALU.mult).then_inc(dve_step, step())
                dve.wait_ge(dve_step, step.all())
                tt(IG, IG, BC, ALU.add).then_inc(dve_step, step())
                for j, c in enumerate((SEQ - 1, T - 1)):
                    m = dve.tensor_copy(NML[:, j:j + 1], NM[:, c:c + 1])
                m.then_inc(m_ready, 1)

                def v_copy(h):
                    dve.wait_ge(done_by(f"v{h}"), done(l, f"v{h}"))
                    dve.tensor_copy(VT[:, :, h, 0:128],
                                         unit(f"v{h}")[:, 0:640].rearrange("p (t c) -> p t c", t=5)).then_inc(unit_of(f"v{h}"), 1)

                def weigh_keys(h):
                    nm = f"kt{h}"
                    dve.wait_ge(done_by(nm), done(l, nm))
                    tt(KW[:, 0:4, :], unit(nm)[:, 0:512].rearrange("p (t c) -> p t c", t=4),
                            bc(WSC[:, 0:4, h], [128, 4, 128]), ALU.mult).then_inc(dve_step, step())
                    dve.tensor_scalar(KW[0:64, 4, :], unit(nm)[0:64, 512:640], WSC[0:64, 4, h:h + 1], None,
                                           ALU.mult).then_inc(unit_of(nm), 1)

                def new_state(h):
                    nm = f"cm{h}"
                    dve.wait_ge(done_by(nm), done(l, nm))
                    dve.tensor_copy(COUT[:, h, 0, :], unit(nm)[:, 0:129]).then_inc(dve_step, step())
                    dve.scalar_tensor_tensor(COUT[:, h, 1, :], C0N[:, h, :], DEC[:, h:h + 1],
                                                  unit(nm)[:, 512:641], ALU.mult, ALU.add).then_inc(unit_of(nm), 1)

                v_copy(0)
                dve.wait_ge(done_by("gt3"), done(l, "gt3"))
                o = unit("gt3")
                for dst, c, f in ((AS, 0, 1.0), (WSC, 20, ML_SCALE), (EMC, 44, 1.0)):
                    dve.tensor_scalar(dst[:, 0:4, :], o[:, c:c + 16].rearrange("p (t h) -> p t h", t=4), f, None,
                                           ALU.mult).then_inc(dve_step, step())
                    dve.tensor_scalar(dst[0:64, 4, :], o[0:64, c + 16:c + 20], f, None, ALU.mult).then_inc(dve_step, step())
                dve.tensor_copy(DEC[:, :], o[:, 40:44]).then_inc(unit_of("gt3"), 1)
                dve.wait_ge(unit_of("gt3"), read(l, "gt3"))
                v_copy(1)
                weigh_keys(0)
                v_copy(2)
                new_state(0)
                weigh_keys(1)
                v_copy(3)
                new_state(1)
                weigh_keys(2)
                new_state(2)
                weigh_keys(3)
                new_state(3)

                def exponents(h):
                    nm = _a(h)[0]
                    dve.wait_ge(done_by(nm), done(l, nm))
                    o = unit(nm)
                    tt(DM[:, 0:512].rearrange("p (t c) -> p t c", t=4),
                            o[:, 0:512].rearrange("p (t c) -> p t c", t=4),
                            K_["mneg"].unsqueeze(1).to_broadcast([128, 4, 128]), ALU.add).then_inc(dve_step, step())
                    tt(W[0:64, 1280:1344], o[0:64, 512:576], K_["mneg"][0:64, 0:64], ALU.add).then_inc(dve_step, step())
                    tt(DM[:, 512:576], QK[:, h, SEQ:T], o[:, 576:640], ALU.mult).then_inc(d_ready, 1)

                def weigh_scores(h):
                    _, n2, n3 = _a(h)
                    dve.wait_ge(w_ready, nth(w_ready, l, h))
                    dve.wait_ge(done_by(n2), done(l, n2))
                    dve.scalar_tensor_tensor(W[:, 0:1024], unit(n2), ML_SCALE, W[:, 0:1024], ALU.mult, ALU.mult).then_inc(unit_of(n2), 1)
                    dve.wait_ge(done_by(n3), done(l, n3))
                    dve.scalar_tensor_tensor(W[:, 1024:1280], unit(n3)[:, 0:256], ML_SCALE, W[:, 1024:1280],
                                                  ALU.mult, ALU.mult).then_inc(dve_step, step())
                    dve.scalar_tensor_tensor(W[0:64, 1280:1344], unit(n3)[0:64, 256:320], ML_SCALE,
                                                  W[0:64, 1280:1344], ALU.mult, ALU.mult).then_inc(unit_of(n3), 1)

                def normalise(h):
                    nm = _b(h)[0][0]
                    dve.wait_ge(done_by(nm), done(l, nm))
                    o3 = unit(nm)[:, 0:387].rearrange("p (t c) -> p t c", t=3)
                    o4, o5 = unit(nm)[:, 512:641], unit(nm)[0:64, 641:770]
                    dve.tensor_copy(DEN[:, 0:3], o3[:, :, 128]).then_inc(dve_step, step())
                    dve.tensor_copy(DEN[:, 3:4], o4[:, 128:129]).then_inc(dve_step, step())
                    dve.tensor_copy(DEN[0:64, 4:5], o5[:, 128:129]).then_inc(dve_step, step())
                    dve.wait_ge(dve_step, step.all())
                    for n, a, b in ((128, 0, 4), (64, 4, 5)):
                        dve.scalar_tensor_tensor(EMC[0:n, a:b, h], DEN[0:n, a:b], -1.0, EMC[0:n, a:b, h],
                                                      ALU.mult, ALU.max).then_inc(dve_step, step())
                    dve.wait_ge(dve_step, step.all())
                    for n, a, b in ((128, 0, 4), (64, 4, 5)):
                        tt(DEN[0:n, a:b], DEN[0:n, a:b], EMC[0:n, a:b, h], ALU.max).then_inc(dve_step, step())
                    dve.wait_ge(dve_step, step.all())
                    for n, a, b in ((128, 0, 4), (64, 4, 5)):
                        dve.reciprocal(DEN[0:n, a:b], DEN[0:n, a:b]).then_inc(dve_step, step())
                    dve.wait_ge(dve_step, step.all())
                    dve.scalar_tensor_tensor(YTK[:, 0:3, :], o3[:, :, 0:128], 0.5, bc(DEN[:, 0:3], [128, 3, 128]),
                                                  ALU.mult, ALU.mult).then_inc(dve_step, step())
                    dve.tensor_scalar(YTK[:, 3, :], o4[:, 0:128], DEN[:, 3:4], 0.5, ALU.mult, ALU.mult).then_inc(dve_step, step())
                    dve.tensor_scalar(YTK[0:64, 4, :], o5[:, 0:128], DEN[0:64, 4:5], 0.5, ALU.mult, ALU.mult).then_inc(unit_of(nm), 1)
                    dve.wait_ge(unit_of(nm), read(l, nm))

                def gate_head(h):
                    nm = _b(h)[1][0]
                    dve.wait_ge(done_by(nm), done(l, nm))
                    dve.wait_ge(unit_of(f"mo{h}"), read(l, f"mo{h}"))
                    dve.scalar_tensor_tensor(YT[:, :], MO[:, h, :], 1.0, unit(nm)[:, 0:T], ALU.add, ALU.mult).then_inc(unit_of(nm), 1)

                def y_lo(i, src):
                    dve.wait_ge(yh_ready, nth(yh_ready, l, i))
                    tt(YL[:, i % 4, :], src, YH[:, i % 4, :].bitcast(f32), ALU.subtract).then_inc(yl_ready, 1)

                exponents(0)
                weigh_scores(0)
                for h in range(4):
                    normalise(h)
                    if h < 3:
                        gate_head(h)
                        exponents(h + 1)
                        y_lo(h, YT[:, :])
                        weigh_scores(h + 1)
                gate_head(3)
                y_lo(3, YT[:, :])

                def rope(i):
                    nm = f"r{i}"
                    raw = KALL[:, 0, 0:T] if i == 4 else WQ[:, i, :]
                    dve.wait_ge(unit_of("wk" if i == 4 else f"wq{i}"), read(l, "wk" if i == 4 else f"wq{i}"))
                    tt(TS[:, 0, :], raw, K_["cos"], ALU.mult).then_inc(dve_step, step())
                    dve.wait_ge(done_by(nm), done(l, nm))
                    tt(split2(TS[:, 1, :]), halves(nm), split2(K_["sin"]), ALU.mult).then_inc(unit_of(nm), 1)
                    dve.wait_ge(dve_step, step.all())
                    dve.wait_ge(unit_of(nm), read(l, nm))
                    tt(raw, TS[:, 0, :], TS[:, 1, :], ALU.add).then_inc(rope_ready, 1)

                for j, i in enumerate((4, 0, 1, 2, 3)):
                    if j:
                        dve.wait_ge(rope_ready, nth(rope_ready, l, j - 1))
                    rope(i)
                dve.wait_ge(done_by("ko"), done(l, "ko"))
                dve.tensor_copy(KOUT[:, 0, :], unit("ko")[:, 0:128]).then_inc(dve_step, step())
                dve.tensor_copy(KOUT[0:64, 1, :], unit("ko")[0:64, 128:256]).then_inc(unit_of("ko"), 1)
                dve.wait_ge(c_stored, l * (16 * C_STORES) + 16 * C_STORES)

                def sw_lo(i):
                    t, g = SWA[i]
                    n = 128 if t < NTT else 64
                    dve.wait_ge(oh_ready, nth(oh_ready, l, i))
                    y = (slice(None), slice(4 + 2 * g, 6 + 2 * g), slice(t * 128, t * 128 + n))
                    tt(YL[y], unit(f"pv{i}")[:, 0:2 * n].rearrange("p (r c) -> p r c", r=2),
                            YH[y].bitcast(f32), ALU.subtract).then_inc(unit_of(f"pv{i}"), 1)

                def sw_max(i):
                    t, g = SWA[i]
                    nm = f"sc{i}"
                    n = 128 if t < NTT else 64
                    kw = 128 if t == 0 else (192 if t == NTT else 256)
                    dve.wait_ge(done_by(nm), done(l, nm))
                    o = unit(nm).rearrange("p (r c) -> p r c", r=4)[0:n, :, 0:kw]
                    s = SM[0:n, i % 2, :, 0:kw]
                    if t == NTT:
                        dve.tensor_scalar(s, o, SW_SCALE, None, ALU.mult).then_inc(unit_of(nm), 1)
                    else:
                        dve.scalar_tensor_tensor(s, o, SW_SCALE, K_["m1"][:, 256 - kw:].unsqueeze(1)
                                                      .to_broadcast([128, 4, kw]), ALU.mult, ALU.add).then_inc(unit_of(nm), 1)
                    dve.wait_ge(unit_of(nm), read(l, nm))
                    mx = [MX[0:n, i % 2, j, :] for j in range(5)]
                    sink = SINK[0:n, 4 * g:4 * g + 4].rearrange("p (r o) -> p o r", o=2)
                    dve.tensor_reduce(mx[0], s, AX.X, ALU.max).then_inc(dve_step, step())
                    dve.wait_ge(dve_step, step.all())
                    m2 = mx[0].rearrange("p (o r) -> p o r", o=2)
                    tt(m2, m2, sink, ALU.max).then_inc(dve_step, step())
                    dve.wait_ge(dve_step, step.all())
                    dve.tensor_scalar(mx[1], mx[0], -1.0, None, ALU.mult).then_inc(dve_step, step())
                    tt(mx[3].rearrange("p (o r) -> p o r", o=2), sink, m2, ALU.subtract).then_inc(mx_ready, 1)

                def sw_norm(i):
                    t, g = SWA[i]
                    n = 128 if t < NTT else 64
                    kw = 128 if t == 0 else (192 if t == NTT else 256)
                    s = SM[0:n, i % 2, :, 0:kw]
                    mx = [MX[0:n, i % 2, j, :] for j in range(5)]
                    dve.wait_ge(ex_ready, nth(ex_ready, l, i))
                    tt(mx[4], mx[2], mx[3], ALU.add).then_inc(dve_step, step())
                    dve.wait_ge(dve_step, step.all())
                    dve.reciprocal(mx[4], mx[4]).then_inc(dve_step, step())
                    dve.wait_ge(dve_step, step.all())
                    tt(s, s, bc(mx[4], [n, 4, kw]), ALU.mult).then_inc(pn_ready, 1)

                def slot(i, between=None):
                    if 0 <= i - 2 < NS:
                        sw_lo(i - 2)
                    if i < NS:
                        sw_max(i)
                    if between is not None:
                        between()
                    if i < NS:
                        sw_norm(i)

                for i in range(4):
                    dve.wait_ge(done_by(f"sv{i}"), done(l, f"sv{i}"))
                    dve.tensor_copy(SV[:, :, i * 128:(i + 1) * 128],
                                         unit(f"sv{i}")[:, 0:640].rearrange("p (t c) -> p t c", t=5)).then_inc(unit_of(f"sv{i}"), 1)
                    slot(i)

                def ln_stats():
                    dve.wait_ge(unit_of("sv3"), read(l, "sv3"))
                    for t in range(NTT + 1):
                        n = 128 if t < NTT else 64
                        dve.wait_ge(dve_step, step.all())
                        dve.bn_stats(BN[0:n, :], SV[0:n, t, :]).then_inc(dve_step, step())
                        dve.wait_ge(dve_step, step.all())
                        carry(dve)
                        dve.bn_aggr(MV[0:n, t, :], BN[0:n, :]).then_inc(dve_step, step())
                    dve.wait_ge(dve_step, step.all())
                    dve.tensor_scalar(LR[:, 0:4], MV[:, 0:4, 1], EPS, None, ALU.add).then_inc(dve_step, step())
                    dve.tensor_scalar(LR[0:64, 4:5], MV[0:64, 4, 1:2], EPS, None, ALU.add).then_inc(ms_ready, 1)

                def ln_root():
                    dve.wait_ge(ln_loaded, l * 32 + 32)
                    dve.wait_ge(rt_ready, nth(rt_ready, l, 1))
                    dve.reciprocal(LR[:, :], LR[:, :]).then_inc(dve_step, step())

                def ln_apply(t):
                    n = 128 if t < NTT else 64
                    v = SV[0:n, t, :]
                    dve.wait_ge(dve_step, step.all())
                    dve.tensor_scalar(v, v, MV[0:n, t, 0:1], LR[0:n, t:t + 1], ALU.subtract, ALU.mult).then_inc(dve_step, step())
                    dve.wait_ge(dve_step, step.all())
                    tt(v, v, LNG[0:n], ALU.mult).then_inc(dve_step, step())
                    dve.wait_ge(dve_step, step.all())
                    tt(v, v, LNB[0:n], ALU.add).then_inc(ln_ready, 1)

                def merge(b, n, q=0, tile=None):
                    nm, tile = f"br{b}_{n}", n if tile is None else tile
                    dve.wait_ge(unit_of(f"g{b}_{n}"), read(l, f"g{b}_{n}", q * 2))
                    dve.wait_ge(done_by(nm), done(l, nm, q * (6 if nm in CHUNK_OF else 2)))
                    s = split2(TS[:, n % 2, :])
                    m = MID[:, ds(tile, 1), :].rearrange("p o (a c) -> p (o a) c", a=2)
                    if b == 0:
                        dve.scalar_tensor_tensor(m, s, 1.0, halves(nm), ALU.add, ALU.mult).then_inc(unit_of(nm), 1)
                        return
                    w = WQ[:, n % 2, :]
                    dve.scalar_tensor_tensor(split2(w), s, 1.0, halves(nm), ALU.add, ALU.mult).then_inc(unit_of(nm), 1)
                    dve.wait_ge(unit_of(nm), read(l, nm, q * 2))
                    ins = tt(m, m, split2(w), ALU.add)
                    if b == 2:
                        ins.then_inc(merged2, 1)
                    else:
                        ins.then_inc(dve_step, step())

                x = 4
                for n in range(0, 8, 2):
                    for e in range(2):
                        slot(x, ln_stats if x == 4 else (lambda: ln_apply(x - 7)) if 7 <= x < 12 else None)
                        x += 1
                    merge(0, n)
                    merge(0, n + 1)
                    if n == 0:
                        ln_root()
                    slot(x, (lambda: ln_apply(x - 7)) if 7 <= x < 12 else None)
                    x += 1
                for n in range(0, 8, 2):
                    g = n // 2
                    nm = f"z{g}"
                    dve.wait_ge(done_by(nm), done(l, nm))
                    dve.wait_ge(unit_of(f"su{g}"), read(l, f"su{g}"))
                    tt(WQ[:, 2 + g % 2, :], SU[:, g, :], unit(nm)[:, 0:T], ALU.mult).then_inc(unit_of(nm), 1)
                    dve.wait_ge(unit_of(nm), read(l, nm))
                    y_lo(4 + g, WQ[:, 2 + g % 2, :])
                    for e in range(2):
                        merge(1, n + e)

                with dve.Fori(0, 2) as q:
                    for n in range(4):
                        merge(2, n, q, q * 4 + n)
                dve.wait_ge(done_by("g2_3"), done(l, "g2_3", 6))
                for k in range(8):
                    dve.wait_ge(hh_ready, nth(hh_ready, l, 8 + k))
                    dve.scalar_tensor_tensor(cols(HL, k), MID[:, k, :], 0.5, cols(HH, k).bitcast(f32),
                                             ALU.mult, ALU.subtract).then_inc(hl_ready, 1)

                def add_tile(c, e, i):
                    o = OMID[:, ds(i * 4 + e, 1), :].rearrange("p o (a c) -> p (o a) c", a=2)
                    dve.wait_ge(unit_of(f"fo{c - 1}_{e}"), read(l, f"fo{c - 1}_{e}", i))
                    dve.wait_ge(done_by(f"fo{c}_{e}"), done(l, f"fo{c}_{e}", i * 4))
                    tt(o, o, halves(f"fo{c}_{e}"), ALU.add).then_inc(unit_of(f"fo{c}_{e}"), 1)

                def add_squares(which):
                    with dve.Fori(0, 2) as i:
                        for e in range(4):
                            if which == 1:
                                add_tile(len(BLOCKS) - 1, e, i)
                            dve.wait_ge(sqo_ready, nth(sqo_ready, l, i * 4 + (8 * which + e)))
                            dve.wait_ge(acc_added, nth(acc_added, l, i * 4 + (8 * which + e - 1)))
                            tt(ACC[:, :], ACC[:, :], SQ[:, e % 2, :], ALU.add).then_inc(acc_added, 1)

                dve.memset(ACC[:, :], 0.0).then_inc(dve_step, step())
                dve.wait_ge(dve_step, step.all())
                carry(dve)
                add_squares(0)
                post_norm("p1", 2, 8, 1)
                pre_norm("n2", 3, 8, 2, 3)
                j0 = 0
                for c, nb in enumerate(BLOCKS):
                    with dve.Fori(0, nb // 2) as i:
                        for e in range(2):
                            gate_nm, up = f"fi{c}_{2 * e}", f"fi{c}_{2 * e + 1}"
                            dve.wait_ge(unit_of(gate_nm), read(l, gate_nm, i))
                            dve.wait_ge(done_by(up), done(l, up, i * 4))
                            tt(split2(TS[:, e, :]), split2(WQ[:, e, :]), halves(up), ALU.mult).then_inc(unit_of(up), 1)
                            dve.wait_ge(gh_ready, nth(gh_ready, l, i * 2 + (j0 + e)))
                            y = ds(i * 2 + e, 1)
                            tt(YL[:, y, :].rearrange("p o c -> p (o c)"), TS[:, e, :],
                               YH[:, y, :].bitcast(f32).rearrange("p o c -> p (o c)"),
                               ALU.subtract).then_inc(gl_ready, 1)
                    j0 += nb
                    if c == 1:
                        with dve.Fori(0, 2) as i:
                            for e in range(4):
                                add_tile(1, e, i)
                    if c == 2:
                        dve.memset(ACC[:, :], 0.0).then_inc(dve_step, step())
                        dve.wait_ge(dve_step, step.all())
                        carry(dve)
                        add_squares(1)
                dve.wait_ge(o_stored, l * (16 * O_STORES) + 16 * O_STORES)
                post_norm("p2", 4, 16, 3)
                step.end()

            for t in range(NTT + 1):
                n = 128 if t < NTT else 64
                dve.wait_ge(x_out_t, t + 1)
                dve.tensor_copy(XIO[0:n, t, :], PS[0:n, t % 4, :]).then_inc(x_out_copied, 1)


_INS = ["x_prompt", "x_sample", "c_prompt", "c_sample", "state_mlstm_C", "state_mlstm_n", "state_mlstm_m",
        "cache_swa_k", "cache_swa_v", "w_ada", "b_ada", "g_pre_mix", "g_post_mix", "g_pre_ffn", "g_post_ffn",
        "w_in", "b_igate", "b_fgate", "ln_v_g", "ln_v_b", "w_spatial", "b_spatial", "swa_sinks",
        "w_br_mlstm", "w_br_gmlp", "w_br_swa", "w_out", "w_ffn_in", "w_ffn_out"]
_OUTS = [("y_prompt", (1, SEQ, D)), ("y_sample", (1, DSEQ, D)),
         ("C_prompt", (DEPTH, 1, MLH, 128, 128)), ("n_prompt", (DEPTH, 1, MLH, 128)), ("m_prompt", (DEPTH, 1, MLH)),
         ("k_prompt", (DEPTH, 1, 128, 2, 64)), ("v_prompt", (DEPTH, 1, 128, 2, 64)),
         ("C_sample", (DEPTH, 1, MLH, 128, 128)), ("n_sample", (DEPTH, 1, MLH, 128)), ("m_sample", (DEPTH, 1, MLH)),
         ("k_sample", (DEPTH, 1, DSEQ, 2, 64)), ("v_sample", (DEPTH, 1, DSEQ, 2, 64)),
         ("gmlp_v_sample", (DEPTH, 1, DSEQ, 512))]


def kernel(**inputs):
    import numpy as _np
    import concourse.bacc as _bacc
    from concourse import mybir as _mybir
    from concourse.bass_utils import run_bass_kernel_spmd as _run

    nc = _bacc.Bacc("TRN2", target_bir_lowering=False, num_devices=1)
    arrays, ins, outs = {}, {}, {}
    for name in _INS:
        a = _np.ascontiguousarray(inputs[name])
        arrays[f"in_{name}"] = a
        ins[name] = nc.dram_tensor(f"in_{name}", a.shape, _mybir.dt.from_np(a.dtype), kind="ExternalInput").ap()
    arrays["in_consts"] = constants()
    ins["consts"] = nc.dram_tensor("in_consts", (128, NCONST), _mybir.dt.float32, kind="ExternalInput").ap()
    for name, shape in _OUTS:
        outs[name] = nc.dram_tensor(f"out_{name}", shape, _mybir.dt.float32, kind="ExternalOutput").ap()
    build(nc, ins, outs)
    r = _run(nc, [arrays], core_ids=[0])
    return tuple(r.results[0][f"out_{name}"] for name, _ in _OUTS)
```

```python
import numpy as np
import concourse.bass as bass
from concourse import mybir
from contextlib import ExitStack

DEPTH, D, SEQ, DSEQ, PAST = 2, 1024, 512, 64, 128
T = SEQ + DSEQ
HALF = T // 2
KT_ = D // 128
MLH, SGG, SWH, SWD = 4, 4, 8, 64
FFN = 2816
EPS = 1e-6
NTT = SEQ // 128
C_Q, C_K, C_V, C_MO, C_IF, C_SU, C_SV, C_WQ, C_WK, C_WV, C_GL = (
    0, 512, 1024, 1536, 2048, 2056, 2568, 3080, 3592, 3720, 3848)
BLOCKS = (8, 8, 6)
SLOT = 8 * 136
NEG = -1.0e30
ML_SCALE, SW_SCALE = 128 ** -0.5, 64 ** -0.5
WOFF = {0: 0, 1: 512, 3: 896, 2: 1024, 4: 1280}

CO = {}
_at = 0
for _n, _w in (("ident", 128), ("perm", 128), ("mneg", 128), ("ones", 128), ("cos", T),
               ("sin", T), ("m1", 256), ("sel", 512)):
    CO[_n] = (_at, _at + _w)
    _at += _w
NCONST = _at


def constants():
    c = np.zeros((128, NCONST), np.float32)

    def put(n, a):
        c[:a.shape[0], CO[n][0]:CO[n][1]] = a
    p = np.arange(128)
    put("ident", np.eye(128, dtype=np.float32))
    swap = np.where(p % 64 < 32, p + 32, p - 32)
    perm = np.zeros((128, 128), np.float32)
    perm[swap, p] = 1.0
    put("perm", perm)
    put("mneg", np.where(p[:, None] <= p[None, :], 0.0, NEG).astype(np.float32))
    put("ones", np.ones((128, 128), np.float32))
    pos = np.concatenate([np.arange(SEQ), PAST + np.arange(DSEQ)]).astype(np.float32)
    inv = (np.float32(10000.0) ** (-np.arange(32, dtype=np.float32) / np.float32(32))).astype(np.float32)
    ang = (inv[p % 32][:, None] * pos[None, :]).astype(np.float32)
    put("cos", np.cos(ang))
    put("sin", np.sin(ang) * np.where(p % 64 < 32, -1.0, 1.0)[:, None].astype(np.float32))
    k = np.arange(256)
    late = p[:, None] >= 64
    put("m1", np.where((late & (k[None] < 64)) | (~late & (k[None] >= 192)), NEG, 0.0).astype(np.float32))
    sel = np.zeros((128, 4, 128), np.float32)
    for h in range(4):
        sel[h, h] = 1.0
    put("sel", sel.reshape(128, 512))
    return c


SWA = [(t, g) for t in range(NTT + 1) for g in range(2)]
ORDER = ["ada0", "ada1", "n1", "n1b", "par", "wst"] + [f"ada{i}" for i in range(2, 24)] 
ORDER += ["ckt"] + [f"qk{i}" for i in range(8)]
ORDER += ["wvif", "wk", "gt1", "gt2", "v0", "gt3", "v1", "vt0", "kt0", "v2", "vt1", "cm0", "kt1", "v3", "vt2",
          "cm1", "kt2", "mo0", "vt3", "cm2", "kt3", "mo1", "cm3"]


def _a(h):
    return [f"a1_{h}", f"a2_{h}", f"a3_{h}"]


def _b(h):
    return [f"b1_{h}"], [f"b2_{h}"]


def swa_slot(i):
    return (["pv%d" % (i - 2)] if 0 <= i - 2 < len(SWA) else []) + \
        (["tp%d" % (i - 1)] if 0 <= i - 1 < len(SWA) else []) + (["sc%d" % i] if i < len(SWA) else [])


ORDER += _a(0) + ["mo2"] + _b(0)[0] + ["mo3"] + _b(0)[1] + _a(1) + ["wq0"] + _b(1)[0] + ["wq1"] + _b(1)[1] \
    + _a(2) + ["wq2"] + _b(2)[0] + ["wq3"] + _b(2)[1] + _a(3) + ["su0"] + _b(3)[0] + ["su1"] + _b(3)[1] \
    + ["r4", "r0", "su2", "r1", "r2", "su3", "r3", "ko"]
for _i in range(4):
    ORDER += [f"sv{_i}"] + ([f"svt{_i - 1}"] if _i else []) + swa_slot(_i)
BRANCHES = (("ml", 0, 0), ("sw", 2, 1), ("sg", 1, 0))
_s = 4
for _b_, (_nm, _g, _set) in enumerate(BRANCHES):
    for _n in range(0, 8, 2):
        for _e in (f"g{_b_}_{_n}", f"g{_b_}_{_n + 1}"):
            ORDER.append(_e)
            if (_b_, _n, _e[-1]) == (0, 0, "0"):
                ORDER.append("svt3")
            if _b_ == 0:
                ORDER += swa_slot(_s)
                _s += 1
        if _b_ == 1:
            ORDER.append(f"z{_n // 2}")
        ORDER += [f"br{_b_}_{_n}", f"br{_b_}_{_n + 1}"]
        if _b_ == 0:
            ORDER += swa_slot(_s)
            _s += 1
ORDER += [f"wo{i}" for i in range(8)] + ["p1", "p1b", "n2", "n2b"]
for _c, _nb in enumerate(BLOCKS):
    ORDER += [f"fi{_c}_{i}" for i in range(2 * _nb)] + [f"fo{_c}_{i}" for i in range(8)]
ORDER += ["p2", "p2b"]
G = {n: i for i, n in enumerate(ORDER)}
NG = len(ORDER)
assert len(G) == NG
UNITS = 4
PER_UNIT = [sum(1 for i in range(NG) if i % UNITS == u) for u in range(UNITS)]

P_QK, P_WVIF, P_WK, P_V, P_MO, P_WQ, P_SU, P_SV, P_BR = 0, 8, 9, 10, 14, 18, 22, 26, 30
P_WO = P_BR + 36
P_FFN = P_WO + 8
NCH = P_FFN + sum(2 * b + 8 for b in BLOCKS)
assert NCH % 2 == 0

CHUNK_OF = {}
CHUNK_OF.update({f"qk{i}": i for i in range(8)})
CHUNK_OF.update({"wvif": P_WVIF, "wk": P_WK})
for _i in range(4):
    CHUNK_OF.update({f"v{_i}": P_V + _i, f"mo{_i}": P_MO + _i, f"wq{_i}": P_WQ + _i, f"su{_i}": P_SU + _i,
                     f"sv{_i}": P_SV + _i})
for _b_ in range(3):
    for _n in range(8):
        _p = P_BR + 12 * _b_ + 3 * (_n // 2)
        CHUNK_OF[f"g{_b_}_{_n}"] = _p + _n % 2
        if _n % 2:
            CHUNK_OF[f"br{_b_}_{_n}"] = _p + 2
CHUNK_OF.update({f"wo{i}": P_WO + i for i in range(8)})
_p = P_FFN
for _c, _nb in enumerate(BLOCKS):
    CHUNK_OF.update({f"fi{_c}_{i}": _p + i for i in range(2 * _nb)})
    _p += 2 * _nb
    CHUNK_OF.update({f"fo{_c}_{i}": _p + i for i in range(8)})
    _p += 8
assert sorted(CHUNK_OF.values()) == list(range(NCH))
_plain = [n for n in ORDER if n not in CHUNK_OF]
PLAIN = {n: i for i, n in enumerate(_plain)}
NPLAIN = len(_plain)
RAW_LOADS = [NCH // 2 + 1, NCH // 2]
PARAM_DMAS = 15
ACT_STEPS, DVE_STEPS = 1, 227
C_STORES, O_STORES = 18, 5


def build(nc, A, O):
    f32, f32r = mybir.dt.float32, mybir.dt.float32r
    ALU, ACT, AX = mybir.AluOpType, mybir.ActivationFunctionType, mybir.AxisListType
    ds = bass.ds
    ctx = ExitStack()
    with ctx:
        def sb(name, shape, dt=f32):
            return ctx.enter_context(nc.sbuf_tensor(name, shape, dt))

        def sem(name):
            return ctx.enter_context(nc.semaphore(name))

        def overlay(name, size, *uses):
            out = {}
            for use in uses:
                with ExitStack() as s:
                    for n, shape, dt in use:
                        out[n] = s.enter_context(nc.sbuf_tensor(n, shape, dt))
            ctx.enter_context(nc.sbuf_tensor(name, [128, size], f32))
            return out

        RAW = [sb(f"raw{s}", [128, SLOT]) for s in range(2)]
        HI = [sb(f"hi{s}", [128, SLOT], f32r) for s in range(2)]
        LO = [sb(f"lo{s}", [128, SLOT], f32r) for s in range(2)]
        CST = sb("consts", [128, NCONST])
        X = sb("x_resident", [128, KT_, T])
        HH = sb("h_hi", [128, KT_ * T + 64], f32r)
        HL = sb("h_lo", [128, KT_ * T + 64], f32r)
        MID = sb("mid", [128, KT_, T])
        TS = sb("tmp", [128, 2, T])
        r = overlay("yg_region", 16 * T,
                    [("y_hi", [128, 8, T], f32r), ("y_lo", [128, 8, T], f32r)],
                    [("pad_a", [128, 4, T], f32), ("rows_a", [4, 4, T], f32),
                     ("pad_b", [128, 4, T], f32), ("rows_b", [4, 2, T], f32), ("c_out", [128, 4, 2, 129], f32)],
                    [("x_io", [128, NTT + 1, D], f32)])
        YH, YL, RA, RB, COUT, XIO = (r[n] for n in ("y_hi", "y_lo", "rows_a", "rows_b", "c_out", "x_io"))
        r = overlay("proj_region", 5 * 516 + 4 * T + 4 * T + 2 * 704,
                    [("v_tok", [128, 5, 4, 129], f32), ("mo_su", [128, 4, T], f32), ("wq", [128, 4, T], f32),
                     ("kall", [128, 2, 704], f32)],
                    [("ada", [128, 2, 8 * 512], f32)])
        VT, MO, WQ, KALL, ADA = r["v_tok"], r["mo_su"], r["wq"], r["kall"], r["ada"]
        r = overlay("tmp_region", 3072 + 128,
                    [("dmask", [128, T], f32), ("wdecay", [128, 1344], f32), ("ytmp", [128, T], f32),
                     ("kw", [128, 5, 128], f32)],
                    [("sm", [128, 2, 4, 256], f32), ("pt", [128, 2, 512], f32)],
                    [("sq", [128, 2, T], f32), ("acc", [128, T], f32), ("rstd", [128, T], f32)])
        DM, W, YT, KW, SM, PT, SQ, ACC, R = (r[n] for n in ("dmask", "wdecay", "ytmp", "kw", "sm", "pt",
                                                             "sq", "acc", "rstd"))
        VSW = sb("v_swa", [128, 5, 128])
        WST = sb("w_spatial_t", [128, 4, 128])
        C0N = sb("c0_n0", [128, 4, 129])
        KOUT = sb("k_out", [128, 2, 128])
        CV = sb("cache_v", [128, 128])
        BSP = sb("b_spatial", [1, 512])
        VCOL = sb("vcol", [128, 80])
        BIF = sb("b_if", [128, 8])
        SINK = sb("sink", [128, 8])
        IFT = sb("if_tok", [128, 5, 8])
        CS = sb("c_silu", [128, 8, 32])
        CC = sb("c_cols", [128, 16])
        MOD = sb("mod", [128, 6, 8, 2])
        SC = sb("scales", [128, 4, 8, 2])
        AS = sb("a_cols", [128, 5, 4])
        WSC = sb("ws_cols", [128, 5, 4])
        EMC = sb("em_cols", [128, 5, 4])
        DEN = sb("den", [128, 5])
        RC = sb("rstd_cols", [128, 5])
        WIN = sb("win", [4, 64])
        DEC = sb("decay", [128, 4])
        M0 = sb("m0", [4, 1])
        NML = sb("neg_m_last", [4, 2])
        MX = sb("mx", [128, 2, 5, 4])
        SCRATCH = sb("scratch", [128, 3])
        BN = sb("bn", [128, 6])
        MV = sb("mean_var", [128, 5, 2])
        LR = sb("ln_rstd", [128, 5])
        K_ = {n: CST[:, a:b] for n, (a, b) in CO.items()}
        IDN, ONES = K_["ident"], K_["ones"]
        SEL = K_["sel"].rearrange("p (h c) -> p h c", h=4)
        QK, SU, YTK = MID, MO, KW
        SV = VT[:, :, :, :].rearrange("p t h c -> p (t h c)")[:, 0:2560].rearrange("p (t c) -> p t c", t=5)
        OMID = MID
        LNG, LNB = MID[:, 6, 0:512], MID[:, 7, 0:512]
        WSP = MID[:, 0, 0:512].rearrange("p (g r) -> p g r", g=4)
        VROWS, CKR = MID[0:80, 1, 0:128], MID[:, 2, 0:128]
        IG, BC, AR, NM = (RA[:, i, :] for i in range(4))
        EM, WR = RB[:, 0, :], RB[:, 1, :]
        LFT = TS[0:4, 0, :]

        PS = ctx.enter_context(nc.psum_tensor("ps", [128, UNITS, 1024], f32))

        def unit(name):
            return PS[:, G[name] % UNITS, :]

        def halves(name):
            return unit(name).rearrange("p (a c) -> p a c", a=2)[:, :, 0:HALF]

        def split2(ap):
            return ap.rearrange("p (a c) -> p a c", a=2)

        group_done = sem("group_done")
        unit_free = [sem(f"unit_free{u}") for u in range(UNITS)]
        raw_loaded = [sem(f"raw_loaded{s}") for s in range(2)]
        chunk_split, chunk_hi, chunk_used = sem("chunk_split"), sem("chunk_hi"), sem("chunk_used")
        ada_loaded = [sem(f"ada_loaded{s}") for s in range(2)]
        consts_loaded, x_loaded, param_loaded = sem("consts_loaded"), sem("x_loaded"), sem("param_loaded")
        kx_moved, out_done = sem("kx_moved"), sem("out_done")
        dve_step, act_step = sem("dve_step"), sem("act_step")
        init_done, cs_ready, x_in_t, x_out_t, x_out_copied = (sem(n) for n in (
            "init_done", "cs_ready", "x_in_t", "x_out_t", "x_out_copied"))

        rate = {}

        def event(name, per_layer, credit=0):
            s = sem(name)
            rate[id(s)] = (per_layer, credit)
            return s

        def nth(s, l, k=0):
            per, credit = rate[id(s)]
            return l * per + (k + (1 + credit))

        def before(s, l, k):
            return l * rate[id(s)][0] + (k + 1)

        proj_free = event("proj_free", 1, 1)
        x_ready = event("x_ready", 16)
        sqn_ready = event("sqn_ready", 16)
        sqn_used = event("sqn_used", 14)
        sqo_ready = event("sqo_ready", 16)
        acc_added = event("acc_added", 16, 2)
        merged2 = event("merged2", 8, 2)
        ms_ready = event("ms_ready", 5)
        rt_ready = event("rt_ready", 5)
        dg_ready = event("dg_ready", 4)
        hs_ready = event("hs_ready", 16)
        hh_ready = event("hh_ready", 24)
        hl_ready = event("hl_ready", 24)
        nabs_ready = event("nabs_ready", 1)
        sp_ready = event("sp_ready", 1)
        m_ready = event("m_ready", 1)
        rows_ready = event("rows_ready", 1)
        d_ready = event("d_ready", 4)
        w_ready = event("w_ready", 4)
        yh_ready = event("yh_ready", 8)
        yl_ready = event("yl_ready", 8)
        rope_ready = event("rope_ready", 5)
        ln_ready = event("ln_ready", 5)
        NS = len(SWA)
        mx_ready = event("mx_ready", NS)
        ex_ready = event("ex_ready", NS)
        pn_ready = event("pn_ready", NS)
        oh_ready = event("oh_ready", NS)
        gh_ready = event("gh_ready", 22)
        gl_ready = event("gl_ready", 22, 2)
        c_stored, o_stored, ln_loaded = sem("c_stored"), sem("o_stored"), sem("ln_loaded")

        def done_by(name):
            return chunk_used if name in CHUNK_OF else group_done

        def done(l, name, i=0):
            if name in CHUNK_OF:
                return l * NCH + (i + (CHUNK_OF[name] + 3))
            return l * NPLAIN + (i + (PLAIN[name] + 1))

        def unit_of(name):
            return unit_free[G[name] % UNITS]

        def empty(l, name, i=0):
            return l * PER_UNIT[G[name] % UNITS] + (i + (G[name] // UNITS + 1))

        def read(l, name, i=0):
            return l * PER_UNIT[G[name] % UNITS] + (i + (G[name] // UNITS + 2))

        def apart(a, b):
            return G[a] % UNITS != G[b] % UNITS

        def split_count(l, pos):
            return l * NCH + (pos + 3)

        def carry(eng, name=None):
            if eng is nc.tensor:
                pe_lead = unit(name)[0:32, 0:1]
                eng.matmul(pe_lead, ONES[:, 0:32], ONES[:, 0:1], start=True, stop=True)
            elif eng is nc.vector:
                eng.memset(SCRATCH[:, 1:2], 0.0)
            else:
                eng.activation(SCRATCH[:, 2:3], ONES[:, 0:1], ACT.Square)

        class Steps:

            def __init__(self, per_layer):
                self.per = per_layer

            def layer(self, l):
                self.base, self.n = l * self.per, 0

            def __call__(self):
                self.n += 1
                return 1

            def all(self):
                return self.base + self.n

            def end(self):
                assert self.n == self.per, (self.n, self.per)

        block = ctx.enter_context(nc.Block())

        @block.sync
        def _(sp):
            sp.dma_start(CST[:, :], A["consts"]).then_inc(consts_loaded, 16)
            for t in range(NTT):
                sp.dma_start(XIO[:, t, :], A["x_prompt"][0, t * 128:(t + 1) * 128, :]).then_inc(x_loaded, 16)
            sp.dma_start(XIO[0:64, NTT, :], A["x_sample"][0, :, :]).then_inc(x_loaded, 16)
            sp.dma_start(MID[0:8, 0, 0:128], A["c_prompt"].rearrange("b (k p) -> (b k) p", p=128)) \
              .then_inc(x_loaded, 16)
            sp.dma_start(MID[8:16, 0, 0:128], A["c_sample"].rearrange("b (k p) -> (b k) p", p=128)) \
              .then_inc(x_loaded, 16)
            with sp.Fori(0, DEPTH) as l:
                for_ada = A["w_ada"][ds(l, 1)].rearrange("l (k p) c -> p (l k) c", p=128)
                ada = [ADA[:, s, :].rearrange("p (k c) -> p k c", k=8) for s in range(2)]
                sp.wait_ge(proj_free, before(proj_free, l, 0))
                for s in range(2):
                    sp.dma_start(ada[s], for_ada[:, :, s * 512:(s + 1) * 512]).then_inc(ada_loaded[s], 16)

                def par(dst, src, **how):
                    sp.dma_start(dst, src, **how).then_inc(param_loaded, 16)

                def row(name):
                    return A[name][ds(l, 1)]

                sp.wait_ge(x_ready, nth(x_ready, l, 7))
                par(VROWS[0:48, :], row("b_ada").rearrange("l (k p) -> (l k) p", p=128))
                for i, nm in enumerate(("g_pre_mix", "g_post_mix", "g_pre_ffn", "g_post_ffn")):
                    par(VROWS[48 + 8 * i:56 + 8 * i, :], row(nm).rearrange("l (k p) -> (l k) p", p=128))
                par(WSP, row("w_spatial").rearrange("l g p r -> p (l g) r"))
                par(CKR, row("cache_swa_k").rearrange("l b k g d -> (l b k) (g d)"))
                par(CV[:, :], row("cache_swa_v").rearrange("l b k g d -> (l b k) (g d)"))
                par(BSP[:, :], row("b_spatial").rearrange("l g p -> l (g p)"))
                par(BIF[:, 0:4], row("b_igate").to_broadcast([128, 4]))
                par(BIF[:, 4:8], row("b_fgate").to_broadcast([128, 4]))
                par(SINK[:, :], row("swa_sinks").to_broadcast([128, 8]))
                par(C0N[:, :, 0:128], row("state_mlstm_C").rearrange("l b h d e -> d (l b h) e"))
                par(C0N[:, :, 128:129], row("state_mlstm_n").rearrange("l b h (d o) -> d (l b h) o", o=1),
                    allow_slow_non_contiguous=True)
                par(M0[:, :], row("state_mlstm_m").rearrange("l b (h o) -> (l b h) o", o=1))

                for s in range(2):
                    sp.wait_ge(done_by(f"ada{s}"), done(l, f"ada{s}"))
                    sp.dma_start(ada[s], for_ada[:, :, 1024 + s * 512:1536 + s * 512]) \
                       .then_inc(ada_loaded[s], 16)
                with sp.Fori(2, 6) as j:
                    for s in range(2):
                        sp.wait_ge(done_by(f"ada{4 + s}"), done(l, f"ada{4 + s}", (j - 2) * 4))
                        sp.dma_start(ada[s], for_ada[:, :, ds(j * 1024 + s * 512, 512)]) \
                           .then_inc(ada_loaded[s], 16)

                def load(s, pos, dst, src):
                    sp.wait_ge(chunk_split, l * NCH + (pos + 1))
                    sp.dma_start(dst, src).then_inc(raw_loaded[s], 16)

                w_in = A["w_in"][ds(l, 1)].rearrange("l (k p) c -> p (l k) c", p=128)

                def cols(s, pos, src, c):
                    load(s, pos, RAW[s][:, 0:1024].rearrange("p (k c) -> p k c", k=8), src[:, :, ds(c, 128)])

                with sp.Fori(0, 4) as i:
                    for s in range(2):
                        cols(s, i * 2 + s, w_in, i * 256 + s * 128)
                r0 = RAW[0][:, :].rearrange("p (k c) -> p k c", k=8)
                load(0, P_WVIF, r0[:, :, 0:128], w_in[:, :, C_WV:C_WV + 128])
                sp.dma_start(r0[:, :, 128:136], w_in[:, :, C_IF:C_IF + 8]).then_inc(raw_loaded[0], 16)
                cols(1, P_WK, w_in, C_WK)
                for pos, c in ((P_V, C_V), (P_MO, C_MO), (P_WQ, C_WQ), (P_SU, C_SU), (P_SV, C_SV)):
                    with sp.Fori(0, 2) as i:
                        for s in range(2):
                            cols(s, i * 2 + (pos + s), w_in, i * 256 + (c + s * 128))
                for b, (nm, g, _) in enumerate(BRANCHES):
                    w_br = A[{"ml": "w_br_mlstm", "sg": "w_br_gmlp", "sw": "w_br_swa"}[nm]][ds(l, 1)] \
                        .rearrange("l (k p) c -> p (l k) c", p=128)
                    with sp.Fori(0, 2) as q:
                        for e in range(6):
                            pos = q * 6 + (P_BR + 12 * b + e)
                            if e % 3 < 2:
                                cols(e % 2, pos, w_in, q * 512 + (C_GL + g * D + (e // 3 * 2 + e % 3) * 128))
                            else:
                                load(e % 2, pos, RAW[e % 2][:, 0:1024].rearrange("p (k c) -> p k c", k=4),
                                     w_br[:, :, ds(q * 512 + e // 3 * 256, 256)])
                w_out = A["w_out"][ds(l, 1)].rearrange("l (k p) c -> p (l k) c", p=128)
                with sp.Fori(0, 4) as i:
                    for s in range(2):
                        cols(s, i * 2 + (P_WO + s), w_out, i * 256 + s * 128)
                w_fi = A["w_ffn_in"][ds(l, 1)].rearrange("l (k p) c -> p (l k) c", p=128)
                w_fo = A["w_ffn_out"][ds(l, 1)].rearrange("l (k p) c -> p (l k) c", p=128)
                pos, j0 = P_FFN, 0
                for nb in BLOCKS:
                    with sp.Fori(0, nb) as j:
                        for s in range(2):
                            cols(s, j * 2 + (pos + s), w_fi, j * 128 + (s * FFN + j0 * 128))
                    pos += 2 * nb
                    with sp.Fori(0, 4) as i:
                        for s in range(2):
                            load(s, i * 2 + (pos + s), RAW[s][:, 0:nb * 128].rearrange("p (k c) -> p k c", k=nb),
                                 w_fo[:, j0:j0 + nb, ds(i * 256 + s * 128, 128)])
                    pos += 8
                    j0 += nb
            for t in range(NTT + 1):
                sp.wait_ge(x_out_copied, t + 1)
                if t < NTT:
                    sp.dma_start(O["y_prompt"][0, t * 128:(t + 1) * 128, :], XIO[:, t, :]) \
                       .then_inc(out_done, 16)
                else:
                    sp.dma_start(O["y_sample"][0, :, :], XIO[0:64, t, :]).then_inc(out_done, 16)
            sp.wait_ge(out_done, 16 * (NTT + 1))

        @block.gpsimd
        def _(pool):
            pool.wait_ge(consts_loaded, 16)
            with pool.Fori(0, DEPTH) as l:
                def split(s, pos, size, loads, more=0):
                    pool.wait_ge(raw_loaded[s], l * (16 * RAW_LOADS[s]) + loads * 16 + (16 + more))
                    pool.wait_ge(chunk_used, l * NCH + (pos + 1))
                    pool.tensor_tensor(HI[s][:, 0:size], RAW[s][:, 0:size],
                                       ONES[:, 0:1].to_broadcast([128, size]), ALU.mult).then_inc(chunk_hi, 1)
                    pool.wait_ge(chunk_hi, l * NCH + (pos + 1))
                    pool.tensor_tensor(LO[s][:, 0:size], RAW[s][:, 0:size], HI[s][:, 0:size].bitcast(f32),
                                       ALU.subtract).then_inc(chunk_split, 1)
                with pool.Fori(0, 4) as i:
                    for s in range(2):
                        split(s, i * 2 + s, 1024, i)
                split(0, P_WVIF, SLOT, 4, 16)
                split(1, P_WK, 1024, 4)
                tail = NCH - 8
                with pool.Fori(5, tail // 2) as i:
                    for s in range(2):
                        split(s, i * 2 + s, 1024, i, 16 * (s == 0))
                with pool.Fori(tail // 2, NCH // 2) as i:
                    for s in range(2):
                        split(s, i * 2 + s, BLOCKS[-1] * 128, i, 16 * (s == 0))

        @block.tensor
        def _(pe):
            pe.wait_ge(consts_loaded, 16)
            pe.wait_ge(x_loaded, 16 * (NTT + 3))
            for t in range(NTT + 1):
                n = 128 if t < NTT else 64
                if t == NTT:
                    pe.wait_ge(init_done, 2)
                for k in range(8):
                    m = pe.transpose(PS[:, t % 4, k * 128:k * 128 + n], XIO[0:n, t, k * 128:(k + 1) * 128],
                                     IDN[0:n, 0:n])
                m.then_inc(x_in_t, 1)
            pe.wait_ge(init_done, 3)
            pe.transpose(PS[:, 1, 0:16], MID[0:16, 0, 0:128], IDN[0:16, 0:16]).then_inc(x_in_t, 1)

            with pe.Fori(0, DEPTH) as l:
                def feature_group(name, s, nk, w, c0, mh, ml, i=0, moving=None, pos=None):
                    if pos is None:
                        pe.wait_ge(unit_of(name), empty(l, name, i))
                    o = halves(name)
                    wh, wl = (x[s][:, 0:nk * w].rearrange("p (k c) -> p k c", k=nk) for x in (HI, LO))
                    for k in range(nk):
                        if moving is not None:
                            pe.wait_ge(moving[0], nth(moving[0], l, moving[1] + k))
                        if k == nk - 1 and pos is not None:
                            follower = ORDER[G[name] + 1]
                            pe.wait_ge(chunk_split, split_count(l, pos + 1))
                            pe.wait_ge(unit_of(follower), empty(l, follower, i))
                        for a, mv, first in ((wh, mh, True), (wh, ml, False), (wl, mh, False)):
                            for h in range(2):
                                m = pe.matmul(o[:, h, :], a[:, k, c0:c0 + 128], mv(k, h),
                                              start=(k == 0 and first), stop=(k == nk - 1 and a is wl))
                    m.then_inc(done_by(name), 1)

                def run_begins(name, pos):
                    pe.wait_ge(chunk_split, split_count(l, pos))
                    pe.wait_ge(unit_of(name), empty(l, name))
                    carry(pe, name)

                def token_group(name, s, w):
                    pe.wait_ge(unit_of(name), empty(l, name))
                    wh, wl = (x[s][:, 0:8 * w].rearrange("p (k c) -> p k c", k=8) for x in (HI, LO))
                    per = 512 // w
                    for t in range(NTT + 1):
                        c = t * w if t < per else 512 + (t - per) * w
                        for k in range(8):
                            for st, mv, first in ((HH, wh, True), (HH, wl, False), (HL, wh, False)):
                                m = pe.matmul(unit(name)[:, c:c + w], st[:, k * T + t * 128:k * T + t * 128 + 128],
                                              mv[:, k, :], start=(k == 0 and first), stop=(k == 7 and st is HL))
                    m.then_inc(done_by(name), 1)

                def hmov(x):
                    return lambda k, h: x[:, k * T + h * HALF:k * T + (h + 1) * HALF]

                HM = (hmov(HH), hmov(HL))

                def main(name, pos, s, i=0):
                    pe.wait_ge(chunk_split, split_count(l, pos))
                    feature_group(name, s, 8, 128, 0, *HM, i=i)

                def token_sums(name, k, sq, first, last):
                    for t in range(NTT + 1):
                        n = 128 if t < NTT else 64
                        m = pe.matmul(unit(name)[0:n, t:t + 1], sq[:, t * 128:t * 128 + n], ONES[:, 0:1],
                                      start=(first and t == 0), stop=last, skip_group_check=True)
                    return m

                def spread(name, which):
                    pe.wait_ge(unit_of(name), empty(l, name))
                    pe.wait_ge(dg_ready, nth(dg_ready, l, which))
                    pe.matmul(unit(name)[:, 0:512], ONES, R[:, 0:512], start=True, stop=True)
                    pe.matmul(unit(name)[:, 512:576], ONES[0:64, :], R[0:64, 512:576], start=True, stop=True) \
                       .then_inc(done_by(name), 1)

                def norm(name, first, which):
                    pe.wait_ge(unit_of(name), empty(l, name))
                    for k in range(8):
                        pe.wait_ge(sqn_ready, nth(sqn_ready, l, first + k))
                        m = token_sums(name, k, SQ[:, k % 2, :], k == 0, k == 7)
                        if k < 7:
                            m.then_inc(sqn_used, 1)
                    m.then_inc(done_by(name), 1)
                    spread(name + "b", which)

                def post(name, which):
                    pe.wait_ge(unit_of(name), empty(l, name))
                    pe.wait_ge(acc_added, nth(acc_added, l, 8 * which + 7))
                    token_sums(name, 0, ACC[:, :], True, True).then_inc(done_by(name), 1)
                    spread(name + "b", 1 + 2 * which)

                def modulate(nm, s, j, i=0):
                    pe.wait_ge(ada_loaded[s], l * (6 * 16) + (j * 16 + 16))
                    pe.wait_ge(unit_of(nm), empty(l, nm, i))
                    wv = ADA[:, s, :].rearrange("p (k c) -> p k c", k=8)
                    for k in range(8):
                        for x in range(4):
                            m = pe.matmul(unit(nm)[32 * x:32 * x + 32, 0:128], CS[:, k, :],
                                          wv[:, k, x * 128:(x + 1) * 128], start=(k == 0), stop=(k == 7))
                    m.then_inc(done_by(nm), 1)

                def modulation_back(nm, source, s, i=0):
                    pe.wait_ge(unit_of(nm), empty(l, nm, i))
                    if apart(source, nm):
                        pe.wait_ge(unit_of(source), read(l, source, i))
                    pe.transpose(unit(nm)[:, 0:128], TS[:, s, 0:128], IDN).then_inc(done_by(nm), 1)

                pe.wait_ge(cs_ready, 1)
                for s in range(2):
                    modulate(f"ada{s}", s, 0)
                norm("n1", 0, 0)
                pe.wait_ge(param_loaded, l * (16 * PARAM_DMAS) + 16 * PARAM_DMAS)
                pe.wait_ge(unit_of("par"), empty(l, "par"))
                pe.transpose(unit("par")[:, 0:80], VROWS, IDN[0:80, 0:80]).then_inc(done_by("par"), 1)
                pe.wait_ge(unit_of("wst"), empty(l, "wst"))
                for g in range(4):
                    m = pe.transpose(unit("wst")[:, g * 128:(g + 1) * 128], WSP[:, g, :], IDN)
                m.then_inc(done_by("wst"), 1)
                for s in range(2):
                    modulation_back(f"ada{2 + s}", f"ada{s}", s)
                with pe.Fori(0, 5) as i:
                    for s in range(2):
                        modulate(f"ada{4 + s}", s, i + 1, i)
                    for s in range(2):
                        modulation_back(f"ada{6 + s}", f"ada{4 + s}", s, i)
                pe.wait_ge(unit_of("ckt"), empty(l, "ckt"))
                pe.transpose(unit("ckt")[:, 0:128], CKR, IDN).then_inc(done_by("ckt"), 1)
                run_begins("qk0", P_QK)
                with pe.Fori(0, 2) as i:
                    for e in range(4):
                        feature_group(f"qk{e}", e % 2, 8, 128, 0, *HM, i=i,
                                      moving=(hl_ready, 0) if e == 0 else None, pos=i * 4 + e)

                pe.wait_ge(chunk_split, split_count(l, P_WVIF))
                token_group("wvif", 0, 136)
                main("wk", P_WK, 1)
                pe.wait_ge(unit_of("gt1"), empty(l, "gt1"))
                if apart("wvif", "gt1"):
                    pe.wait_ge(unit_of("wvif"), read(l, "wvif"))
                for c, o in ((0, 0), (4, 512)):
                    for t in range(NTT):
                        m = pe.transpose(unit("gt1")[0:4, o + t * 128:o + (t + 1) * 128], IFT[:, t, c:c + 4], IDN)
                m.then_inc(done_by("gt1"), 1)
                pe.wait_ge(unit_of("gt2"), empty(l, "gt2"))
                carry(pe, "gt2")
                for c, o in ((0, 0), (4, 512)):
                    m = pe.transpose(unit("gt2")[0:4, o:o + 64], IFT[0:64, 4, c:c + 4], IDN[0:64, 0:64])
                m.then_inc(done_by("gt2"), 1)

                def v_chunk(h):
                    main(f"v{h}", P_V + h, h % 2)

                def to_tokens(name, source, s):
                    pe.wait_ge(unit_of(name), empty(l, name))
                    if apart(source, name):
                        pe.wait_ge(unit_of(source), read(l, source))
                    o = unit(name)
                    for t in range(NTT):
                        pe.transpose(o[:, t * 128:(t + 1) * 128], TS[:, s, t * 128:(t + 1) * 128], IDN)
                    pe.transpose(o[0:64, 512:640], TS[:, s, SEQ:T], IDN).then_inc(done_by(name), 1)

                def key_transposes(h):
                    pe.wait_ge(unit_of(f"kt{h}"), empty(l, f"kt{h}"))
                    if h == 0:
                        if apart("qk7", "kt0"):
                            pe.wait_ge(unit_of("qk7"), read(l, "qk7"))
                    o = unit(f"kt{h}")
                    for t in range(NTT):
                        m = pe.transpose(o[:, t * 128:(t + 1) * 128], QK[:, 4 + h, t * 128:(t + 1) * 128], IDN)
                    m = pe.transpose(o[0:64, 512:640], QK[:, 4 + h, SEQ:T], IDN)
                    m.then_inc(done_by(f"kt{h}"), 1)

                def state(h):
                    pe.wait_ge(unit_of(f"cm{h}"), empty(l, f"cm{h}"))
                    if apart(f"kt{h}", f"cm{h}"):
                        pe.wait_ge(unit_of(f"kt{h}"), read(l, f"kt{h}"))
                    o = unit(f"cm{h}")
                    for t in range(NTT):
                        pe.matmul(o[:, 0:129], KW[:, t, :], VT[:, t, h, :], start=(t == 0), stop=(t == NTT - 1))
                    pe.matmul(o[:, 512:641], KW[0:64, 4, :], VT[0:64, 4, h, :], start=True, stop=True) \
                       .then_inc(done_by(f"cm{h}"), 1)

                def scores(h):
                    n1, n2, n3 = _a(h)
                    pe.wait_ge(unit_of(n1), empty(l, n1))
                    pe.wait_ge(rows_ready, nth(rows_ready, l))
                    o = unit(n1)
                    pe.matmul(o[:, 0:512], SEL[0:4, h, :], NM[:, 0:512], start=True, stop=True)
                    pe.matmul(o[:, 512:576], SEL[0:4, h, :], NM[:, 512:576], start=True, stop=True)
                    pe.matmul(o[:, 576:640], SEL[0:4, h, :], WIN[:, :], start=True, stop=True) \
                       .then_inc(done_by(n1), 1)
                    for nm, js in ((n2, (0, 1, 3)), (n3, (2, 4))):
                        pe.wait_ge(unit_of(nm), empty(l, nm))
                        base = 0 if nm is n2 else 1024
                        for j in js:
                            k0, k1 = (j * 128, j * 128 + 128) if j < 4 else (SEQ, T)
                            c = WOFF[j] - base
                            m = pe.matmul(unit(nm)[0:k1 - k0, c:c + (SEQ if j < 4 else T) - k0],
                                          QK[:, 4 + h, k0:k1], QK[:, h, k0:(SEQ if j < 4 else T)],
                                          start=True, stop=True)
                        m.then_inc(done_by(nm), 1)

                def outputs(h):
                    n1 = _b(h)[0][0]
                    pe.wait_ge(unit_of(n1), empty(l, n1))
                    if apart(_a(h)[2], n1):
                        pe.wait_ge(unit_of(_a(h)[2]), read(l, _a(h)[2]))
                    for t in range(NTT):
                        c = t * 129 if t < 3 else 512
                        for j in range(t + 1):
                            w0 = WOFF[j] + 128 * (t - j)
                            pe.matmul(unit(n1)[:, c:c + 129], W[:, w0:w0 + 128], VT[:, j, h, :],
                                      start=(j == 0), stop=(j == t))
                    o = unit(n1)[0:64, 641:770]
                    pe.matmul(o, W[0:64, 1280:1344], VT[0:64, 4, h, :], start=True, stop=False)
                    pe.matmul(o, DM[:, 512:576], C0N[:, h, :], start=False, stop=True).then_inc(done_by(n1), 1)

                def back(h):
                    nm = _b(h)[1][0]
                    pe.wait_ge(unit_of(nm), empty(l, nm))
                    if apart(_b(h)[0][0], nm):
                        pe.wait_ge(unit_of(_b(h)[0][0]), read(l, _b(h)[0][0]))
                    for t in range(NTT):
                        pe.transpose(unit(nm)[:, t * 128:(t + 1) * 128], YTK[:, t, :], IDN)
                    pe.transpose(unit(nm)[:, 512:576], YTK[0:64, 4, :], IDN[0:64, 0:64]) \
                       .then_inc(done_by(nm), 1)

                v_chunk(0)
                pe.wait_ge(unit_of("gt3"), empty(l, "gt3"))
                pe.wait_ge(rows_ready, nth(rows_ready, l))
                carry(pe, "gt3")
                o = unit("gt3")
                for x, c in ((AR, 0), (WR, 20), (EM, 44)):
                    for t in range(NTT + 1):
                        n = 128 if t < NTT else 64
                        pe.transpose(o[0:n, c + 4 * t:c + 4 * t + 4], x[:, t * 128:t * 128 + n], IDN[0:4, 0:4])
                for h in range(4):
                    m = pe.matmul(o[:, 40 + h:41 + h], SEL[0:4, h, :], WIN[:, 63:64], start=True, stop=True)
                m.then_inc(done_by("gt3"), 1)
                v_chunk(1)
                to_tokens("vt0", "v0", 1)
                key_transposes(0)
                v_chunk(2)
                to_tokens("vt1", "v1", 0)
                state(0)
                key_transposes(1)
                v_chunk(3)
                to_tokens("vt2", "v2", 1)
                state(1)
                key_transposes(2)
                main("mo0", P_MO, 0)
                to_tokens("vt3", "v3", 0)
                state(2)
                key_transposes(3)
                main("mo1", P_MO + 1, 1)
                state(3)
                scores(0)
                main("mo2", P_MO + 2, 0)
                outputs(0)
                main("mo3", P_MO + 3, 1)
                back(0)
                scores(1)
                main("wq0", P_WQ, 0)
                outputs(1)
                main("wq1", P_WQ + 1, 1)
                back(1)
                scores(2)
                main("wq2", P_WQ + 2, 0)
                outputs(2)
                main("wq3", P_WQ + 3, 1)
                back(2)
                scores(3)
                main("su0", P_SU, 0)
                outputs(3)

                def rope(i):
                    nm = f"r{i}"
                    pe.wait_ge(unit_of(nm), empty(l, nm))
                    if i == 4:
                        if apart("wk", nm):
                            pe.wait_ge(unit_of("wk"), read(l, "wk"))
                        src = KALL[:, 0, 0:T]
                    else:
                        if apart(f"wq{i}", nm):
                            pe.wait_ge(unit_of(f"wq{i}"), read(l, f"wq{i}"))
                        src = WQ[:, i, :]
                    for h in range(2):
                        m = pe.matmul(halves(nm)[:, h, :], K_["perm"], src[:, h * HALF:(h + 1) * HALF],
                                      start=True, stop=True)
                    m.then_inc(done_by(nm), 1)

                main("su1", P_SU + 1, 1)
                back(3)
                rope(4)
                rope(0)
                main("su2", P_SU + 2, 0)
                rope(1)
                rope(2)
                main("su3", P_SU + 3, 1)
                rope(3)
                pe.wait_ge(unit_of("ko"), empty(l, "ko"))
                pe.wait_ge(rope_ready, nth(rope_ready, l, 0))
                pe.transpose(unit("ko")[:, 0:128], KALL[:, 0, SEQ - 128:SEQ], IDN)
                pe.transpose(unit("ko")[0:64, 128:256], KALL[:, 0, SEQ:T], IDN).then_inc(done_by("ko"), 1)

                def keys(t):
                    return (0, 128) if t == 0 else ((SEQ, 704) if t == NTT else (128 * (t - 1), 128 * (t + 1)))

                def sw_scores(i):
                    t, g = SWA[i]
                    nm = f"sc{i}"
                    pe.wait_ge(unit_of(nm), empty(l, nm))
                    if i == 0:
                        pe.wait_ge(rope_ready, nth(rope_ready, l, 4))
                        pe.wait_ge(kx_moved, l * 32 + 32)
                    if SWA[i][0] == NTT:
                        carry(pe, nm)
                    n = 128 if t < NTT else 64
                    k0, k1 = keys(t)
                    for r_ in range(4):
                        h = 4 * g + r_
                        b = 64 * (h % 2)
                        c = (2 * (h % 2) + r_ // 2) * 256
                        m = pe.matmul(unit(nm)[0:n, c:c + k1 - k0],
                                      WQ[b:b + 64, h // 2, t * 128:t * 128 + n],
                                      KALL[b:b + 64, 0 if g == h % 2 else 1, k0:k1], start=True, stop=True)
                    m.then_inc(done_by(nm), 1)

                def sw_transposes(i):
                    t, g = SWA[i]
                    nm = f"tp{i}"
                    pe.wait_ge(unit_of(nm), empty(l, nm))
                    pe.wait_ge(pn_ready, nth(pn_ready, l, i))
                    if SWA[i][0] == NTT:
                        carry(pe, nm)
                    n = 128 if t < NTT else 64
                    o = unit(nm).rearrange("p (a r c) -> p a r c", a=2, r=4)
                    for a, (c0, c1) in enumerate(((0, 128), (128, 256))[:1 if t == 0 else 2]
                                                 if t < NTT else ((0, 64), (64, 192))):
                        for r_ in range(4):
                            m = pe.transpose(o[0:c1 - c0, a, r_, 0:n], SM[0:n, i % 2, r_, c0:c1], IDN[0:n, 0:n])
                    m.then_inc(done_by(nm), 1)

                def sw_output(i):
                    t, g = SWA[i]
                    nm = f"pv{i}"
                    pe.wait_ge(unit_of(nm), empty(l, nm))
                    if apart(f"tp{i}", nm):
                        pe.wait_ge(unit_of(f"tp{i}"), read(l, f"tp{i}"))
                    if SWA[i][0] == NTT:
                        carry(pe, nm)
                    n = 128 if t < NTT else 64
                    p = PT[:, :, :].rearrange("p a (r c) -> p a r c", r=4)
                    v = VSW[:, :, g * 64:(g + 1) * 64]
                    if t == 0:
                        parts = [(v[:, 0, :], 0, 128)]
                    elif t < NTT:
                        parts = [(v[:, t - 1, :], 0, 128), (v[:, t, :], 1, 128)]
                    else:
                        parts = [(v[0:64, 4, :], 0, 64), (CV[:, g * 64:(g + 1) * 64], 1, 128)]
                    for odd in range(2):
                        o = unit(nm)[64 * odd:64 * odd + 64, 0:2 * n].rearrange("p (r c) -> p r c", r=2)
                        for x, (st, a, kk) in enumerate(parts):
                            m = pe.matmul(o, st, p[0:kk, a, 2 * odd:2 * odd + 2, 0:n], start=(x == 0),
                                          stop=(x == len(parts) - 1))
                    m.then_inc(done_by(nm), 1)

                def slot(i):
                    if 0 <= i - 2 < NS:
                        sw_output(i - 2)
                    if 0 <= i - 1 < NS:
                        sw_transposes(i - 1)
                    if i < NS:
                        sw_scores(i)

                for i in range(4):
                    main(f"sv{i}", P_SV + i, i % 2)
                    if i:
                        to_tokens(f"svt{i - 1}", f"sv{i - 1}", (i - 1) % 2)
                    slot(i)

                def ymov(x, st):
                    return lambda k, h: x[:, st * 4 + k, h * HALF:(h + 1) * HALF]

                def spatial(g):
                    nm = f"z{g}"
                    pe.wait_ge(unit_of(nm), empty(l, nm))
                    pe.wait_ge(ln_ready, nth(ln_ready, l, 4))
                    o = unit(nm)
                    for t in range(NTT + 1):
                        n = 128 if t < NTT else 64
                        pe.matmul(o[:, t * 128:t * 128 + n], SV[0:n, t, g * 128:(g + 1) * 128], WST[0:n, g, 0:n],
                                  start=True, stop=False)
                        m = pe.matmul(o[:, t * 128:t * 128 + n], ONES[0:1, :], BSP[0:1, g * 128:g * 128 + n],
                                      start=False, stop=True)
                    m.then_inc(done_by(nm), 1)

                def branch(b, n, pos, s, i=0):
                    pe.wait_ge(chunk_split, split_count(l, pos))
                    st = BRANCHES[b][2]
                    for e in range(2):
                        feature_group(f"br{b}_{n + e}", s, 4, 256, e * 128, ymov(YH, st), ymov(YL, st), i=i)

                x = 4
                for n in range(0, 8, 2):
                    pos = P_BR + 3 * (n // 2)
                    for e in range(2):
                        main(f"g0_{n + e}", pos + e, (pos + e) % 2)
                        if n + e == 0:
                            to_tokens("svt3", "sv3", 1)
                        slot(x)
                        x += 1
                    if n == 0:
                        pe.wait_ge(yl_ready, nth(yl_ready, l, 3))
                    branch(0, n, pos + 2, pos % 2)
                    slot(x)
                    x += 1
                for n in range(0, 8, 2):
                    pos = P_BR + 12 + 3 * (n // 2)
                    for e in range(2):
                        main(f"g1_{n + e}", pos + e, (pos + e) % 2)
                    spatial(n // 2)
                    if n == 0:
                        if apart(f"pv{NS - 1}", "br1_0"):
                            pe.wait_ge(unit_of(f"pv{NS - 1}"), read(l, f"pv{NS - 1}"))
                    branch(1, n, pos + 2, pos % 2)
                with pe.Fori(0, 2) as q:
                    for n in range(0, 4, 2):
                        e0 = 3 * (n // 2)
                        for e in range(2):
                            main(f"g2_{n + e}", q * 6 + (P_BR + 24 + e0 + e), (e0 + e) % 2, i=q * 2)
                        if n == 0:
                            pe.wait_ge(yl_ready, nth(yl_ready, l, 7))
                        branch(2, n, q * 6 + (P_BR + 24 + e0 + 2), e0 % 2, i=q * 2)
                run_begins("wo0", P_WO)
                with pe.Fori(0, 2) as i:
                    for e in range(4):
                        feature_group(f"wo{e}", e % 2, 8, 128, 0, *HM, i=i,
                                      moving=(hl_ready, 8) if e == 0 else None, pos=i * 4 + (P_WO + e))
                post("p1", 0)
                norm("n2", 8, 2)
                pos, j0 = P_FFN, 0
                run_begins("fi0_0", pos)
                for c, nb in enumerate(BLOCKS):
                    with pe.Fori(0, nb // 2) as i:
                        for e in range(4):
                            feature_group(
                                f"fi{c}_{e}", e % 2, 8, 128, 0, *HM, i=i,
                                moving=(hl_ready, 16) if (c, e) == (0, 0) else None, pos=i * 4 + (pos + e))
                    pos += 2 * nb
                    gm = tuple((lambda k, h, y=y: y[:, k, h * HALF:(h + 1) * HALF]) for y in (YH, YL))
                    more = c < len(BLOCKS) - 1
                    with pe.Fori(0, 2) as i:
                        for e in range(4):
                            if not more:
                                pe.wait_ge(chunk_split, split_count(l, i * 4 + (pos + e)))
                            feature_group(
                                f"fo{c}_{e}", e % 2, nb, 128, 0, *gm, i=i,
                                moving=(gl_ready, j0) if e == 0 else None, pos=i * 4 + (pos + e) if more else None)
                    pos += 8
                    j0 += nb
                post("p2", 1)

            pe.wait_ge(x_ready, nth(x_ready, DEPTH, 7))
            for t in range(NTT + 1):
                n = 128 if t < NTT else 64
                if t == NTT:
                    pe.wait_ge(x_out_copied, 1)
                for k in range(8):
                    m = pe.transpose(PS[0:n, t % 4, k * 128:(k + 1) * 128], X[:, k, t * 128:t * 128 + n], IDN)
                m.then_inc(x_out_t, 1)

        @block.scalar
        def _(act):
            step = Steps(ACT_STEPS)
            act.wait_ge(init_done, 7)
            for b in range(2):
                m = act.activation(CS[:, :, b], CC[:, 8 * b:8 * b + 8], ACT.Silu)
            m.then_inc(cs_ready, 1)

            with act.Fori(0, DEPTH) as l:
                step.layer(l)

                def row(name):
                    return A[name][ds(l, 1)]

                def cols(x, k):
                    return x[:, k * T:(k + 1) * T]

                def squares(first):
                    for k in range(8):
                        act.wait_ge(x_ready, nth(x_ready, l, first + k))
                        if k >= 2:
                            act.wait_ge(sqn_used, nth(sqn_used, l, (7 if first else 0) + k - 2))
                        act.activation(SQ[:, k % 2, :], X[:, k, :], ACT.Square).then_inc(sqn_ready, 1)

                def roots(which, src, dst):
                    act.wait_ge(ms_ready, nth(ms_ready, l, which))
                    act.activation(dst, src, ACT.Sqrt).then_inc(rt_ready, 1)

                def h_hi(first, part):
                    for k in range(8):
                        act.wait_ge(hs_ready, nth(hs_ready, l, first + k))
                        h = cols(HH, k)
                        act.activation(h[:, 0:SEQ], TS[:, k % 2, 0:SEQ], ACT.Identity, bias=MOD[:, part, k, 0:1])
                        act.activation(h[:, SEQ:T], TS[:, k % 2, SEQ:T], ACT.Identity, bias=MOD[:, part, k, 1:2]) \
                           .then_inc(hh_ready, 1)

                squares(0)
                roots(0, RC[:, :], RC[:, :])
                def modulation_tile(nm, s, i=0):
                    act.wait_ge(done_by(nm), done(l, nm, i))
                    act.activation(TS[:, s, 0:128], unit(nm)[:, 0:128], ACT.Copy).then_inc(unit_of(nm), 1)

                for s in range(2):
                    modulation_tile(f"ada{s}", s)
                with act.Fori(0, 5) as i:
                    for s in range(2):
                        modulation_tile(f"ada{4 + s}", s, i * 4)
                h_hi(0, 0)

                with act.Fori(0, 2) as i:
                    for e in range(4):
                        act.wait_ge(done_by(f"qk{e}"), done(l, f"qk{e}", i * 4))
                        act.activation(QK[:, ds(i * 4 + e, 1), :].rearrange("p o (a c) -> p (o a) c", a=2),
                                            halves(f"qk{e}"), ACT.Copy).then_inc(unit_of(f"qk{e}"), 1)

                def tile(name, dst, func=ACT.Copy, scale=1.0, c=0):
                    act.wait_ge(done_by(name), done(l, name, c))
                    act.activation(split2(dst), halves(name), func, scale=scale).then_inc(unit_of(name), 1)

                tile("wk", KALL[:, 0, 0:T])
                act.wait_ge(nabs_ready, nth(nabs_ready, l))
                act.activation(LFT, WR, ACT.Exp).then_inc(act_step, step())
                act.wait_ge(act_step, step.all())
                act.activation(WR, LFT, ACT.Ln, bias=1.0).then_inc(sp_ready, 1)
                act.wait_ge(m_ready, nth(m_ready, l))
                act.activation(EM, IG, ACT.Exp, scale=-1.0)
                for j, (a, b) in enumerate(((0, SEQ), (SEQ, T))):
                    act.activation(WR[:, a:b], AR[:, a:b], ACT.Exp, bias=NML[:, j:j + 1])
                act.activation(WIN[:, :], NM[:, SEQ:T], ACT.Exp, bias=M0[:, :]).then_inc(rows_ready, 1)
                for nm, c in (("m_prompt", SEQ - 1), ("m_sample", T - 1)):
                    act.dma_start(O[nm][ds(l, 1)].rearrange("l b (h o) -> (l b h) o", o=1), IG[:, c:c + 1]) \
                       .then_inc(c_stored, 16)

                for h in range(4):
                    if h >= 2:
                        act.wait_ge(done_by(f"vt{h - 2}"), done(l, f"vt{h - 2}"))
                    tile(f"v{h}", TS[:, (h + 1) % 2, :])

                def store_state(h):
                    act.wait_ge(unit_of(f"cm{h}"), read(l, f"cm{h}"))
                    for j, w in enumerate(("prompt", "sample")):
                        act.dma_start(O[f"C_{w}"][ds(l, 1), 0, h].rearrange("l d e -> (l d) e"), COUT[:, h, j, 0:128]) \
                           .then_inc(c_stored, 16)
                        act.dma_start(O[f"n_{w}"][ds(l, 1), 0, h].rearrange("l (d o) -> (l d) o", o=1),
                                      COUT[:, h, j, 128:129]).then_inc(c_stored, 16)

                def decay(h):
                    n1 = _a(h)[0]
                    if h == 0:
                        act.wait_ge(unit_of("gt3"), read(l, "gt3"))
                    act.wait_ge(d_ready, nth(d_ready, l, h))
                    for j in range(3):
                        m = act.activation(W[:, WOFF[j] + 128:WOFF[j] + SEQ - 128 * j],
                                           unit(n1)[:, 128 * (j + 1):SEQ], ACT.Exp, bias=AS[:, j, h:h + 1])
                    m.then_inc(unit_of(n1), 1)
                    for j in range(4):
                        act.activation(W[:, WOFF[j]:WOFF[j] + 128], DM[:, 128 * j:128 * j + 128], ACT.Exp,
                                       bias=AS[:, j, h:h + 1])
                    act.activation(W[0:64, 1280:1344], W[0:64, 1280:1344], ACT.Exp, bias=AS[0:64, 4, h:h + 1]) \
                       .then_inc(w_ready, 1)

                def y_hi(i, src):
                    act.activation(YH[:, i % 4, :], src, ACT.Copy).then_inc(yh_ready, 1)

                def head_hi(h):
                    act.wait_ge(unit_of(_b(h)[1][0]), read(l, _b(h)[1][0]))
                    y_hi(h, YT[:, :])

                tile("mo0", MO[:, 0, :], ACT.Tanh, 0.5)
                store_state(0)
                store_state(1)
                tile("mo1", MO[:, 1, :], ACT.Tanh, 0.5)
                store_state(2)
                decay(0)
                tile("mo2", MO[:, 2, :], ACT.Tanh, 0.5)
                store_state(3)
                tile("mo3", MO[:, 3, :], ACT.Tanh, 0.5)
                head_hi(0)
                decay(1)
                tile("wq0", WQ[:, 0, :])
                tile("wq1", WQ[:, 1, :])
                head_hi(1)
                decay(2)
                tile("wq2", WQ[:, 2, :])
                tile("wq3", WQ[:, 3, :])
                head_hi(2)
                decay(3)
                tile("su0", SU[:, 0, :])
                tile("su1", SU[:, 1, :])
                head_hi(3)
                act.wait_ge(unit_of(_a(3)[2]), read(l, _a(3)[2]))
                for dst, nm in ((LNG, "ln_v_g"), (LNB, "ln_v_b")):
                    act.dma_start(dst, row(nm).to_broadcast([128, 512])).then_inc(ln_loaded, 16)
                act.wait_ge(rope_ready, nth(rope_ready, l, 0))
                act.wait_ge(unit_of("ckt"), read(l, "ckt"))
                act.dma_start(KALL[0:64, 1, :], KALL[64:128, 0, :]).then_inc(kx_moved, 16)
                act.dma_start(KALL[64:128, 1, :], KALL[0:64, 0, :]).then_inc(kx_moved, 16)
                tile("su2", SU[:, 2, :])
                tile("su3", SU[:, 3, :])
                act.wait_ge(unit_of("ko"), read(l, "ko"))
                for nm, src in (("k_prompt", KOUT[:, 0, :]), ("k_sample", KOUT[0:64, 1, :]),
                                ("v_prompt", VSW[:, NTT - 1, :]), ("v_sample", VSW[0:64, NTT, :])):
                    act.dma_start(O[nm][ds(l, 1)].rearrange("l b k g d -> (l b k) (g d)"), src) \
                       .then_inc(o_stored, 16)
                act.wait_ge(c_stored, l * (16 * C_STORES) + 16 * C_STORES)

                def sw_hi(i):
                    t, g = SWA[i]
                    n = 128 if t < NTT else 64
                    act.wait_ge(done_by(f"pv{i}"), done(l, f"pv{i}"))
                    act.activation(YH[:, 4 + 2 * g:6 + 2 * g, t * 128:t * 128 + n],
                                   unit(f"pv{i}")[:, 0:2 * n].rearrange("p (r c) -> p r c", r=2), ACT.Copy) \
                       .then_inc(oh_ready, 1)

                def sw_pt(i):
                    t, g = SWA[i]
                    nm = f"tp{i}"
                    act.wait_ge(done_by(nm), done(l, nm))
                    if t == 0:
                        m = act.activation(PT[:, 0, :], unit(nm)[:, 0:512], ACT.Copy)
                    elif t < NTT:
                        m = act.activation(PT[:, :, :], unit(nm).rearrange("p (a c) -> p a c", a=2), ACT.Copy)
                    else:
                        for a, kk in ((0, 64), (1, 128)):
                            m = act.activation(PT[0:kk, a, :].rearrange("p (r c) -> p r c", r=4)[:, :, 0:64],
                                               unit(nm)[0:kk, a * 512:(a + 1) * 512]
                                               .rearrange("p (r c) -> p r c", r=4)[:, :, 0:64], ACT.Copy)
                    m.then_inc(unit_of(nm), 1)

                def sw_exp(i):
                    t, g = SWA[i]
                    n = 128 if t < NTT else 64
                    kw = 128 if t == 0 else (192 if t == NTT else 256)
                    act.wait_ge(mx_ready, nth(mx_ready, l, i))
                    for r_ in range(4):
                        x = SM[0:n, i % 2, r_, 0:kw]
                        act.activation(x, x, ACT.Exp, bias=MX[0:n, i % 2, 1, r_:r_ + 1],
                                       accum_out=MX[0:n, i % 2, 2, r_:r_ + 1])
                    act.activation(MX[0:n, i % 2, 3, :], MX[0:n, i % 2, 3, :], ACT.Exp).then_inc(ex_ready, 1)

                def slot(i):
                    if 0 <= i - 2 < NS:
                        sw_hi(i - 2)
                    if 0 <= i - 1 < NS:
                        sw_pt(i - 1)
                    if i < NS:
                        sw_exp(i)

                act.wait_ge(rope_ready, nth(rope_ready, l, 4))
                for i in range(4):
                    if i >= 2:
                        act.wait_ge(done_by(f"svt{i - 2}"), done(l, f"svt{i - 2}"))
                    tile(f"sv{i}", TS[:, i % 2, :])
                    slot(i)

                def gate(b, n, c=0, q=0):
                    if b == 0 and n < 2:
                        act.wait_ge(done_by(f"svt{n + 2}"), done(l, f"svt{n + 2}"))
                    if n >= 2:
                        act.wait_ge(unit_of(f"br{b}_{n - 2}"), read(l, f"br{b}_{n - 2}", q))
                    elif b > 0 and b < 2:
                        act.wait_ge(unit_of(f"br{b - 1}_{n + 6}"), read(l, f"br{b - 1}_{n + 6}"))
                    tile(f"g{b}_{n}", TS[:, n % 2, :], ACT.Tanh, 0.5, c=c)

                x = 4
                for n in range(0, 8, 2):
                    for e in range(2):
                        gate(0, n + e)
                        slot(x)
                        x += 1
                    if n == 0:
                        roots(1, LR[:, :], LR[:, :])
                    slot(x)
                    x += 1
                act.wait_ge(ln_ready, nth(ln_ready, l, 4))
                act.dma_start(O["gmlp_v_sample"][ds(l, 1)].rearrange("l b t c -> (l b t) c"), SV[0:64, NTT, :]) \
                   .then_inc(o_stored, 16)
                for n in range(0, 8, 2):
                    gate(1, n)
                    gate(1, n + 1)
                    g = n // 2
                    act.wait_ge(unit_of(f"z{g}"), read(l, f"z{g}"))
                    y_hi(4 + g, WQ[:, 2 + g % 2, :])
                for n in range(2):
                    act.wait_ge(unit_of(f"br1_{n + 6}"), read(l, f"br1_{n + 6}"))
                with act.Fori(0, 2) as q:
                    for n in range(4):
                        act.wait_ge(merged2, before(merged2, l, q * 4 + n))
                        tile(f"g2_{n}", TS[:, n % 2, :], ACT.Tanh, 0.5, c=q * 6)
                for k in range(8):
                    act.wait_ge(merged2, nth(merged2, l, k))
                    act.activation(cols(HH, k), MID[:, k, :], ACT.Copy, scale=0.5).then_inc(hh_ready, 1)

                def o_tile(name, c, n):
                    o = OMID[:, ds(n, 1), :].rearrange("p o c -> p (o c)")
                    act.wait_ge(done_by(name), done(l, name, c))
                    act.activation(OMID[:, ds(n, 1), :].rearrange("p o (a c) -> p (o a) c", a=2),
                                        halves(name), ACT.Copy).then_inc(unit_of(name), 1)
                    return o

                with act.Fori(0, 2) as i:
                    for e in range(4):
                        o = o_tile(f"wo{e}", i * 4, i * 4 + e)
                        act.wait_ge(unit_of(f"wo{e}"), read(l, f"wo{e}", i))
                        act.wait_ge(acc_added, before(acc_added, l, i * 4 + e))
                        carry(act)
                        act.activation(SQ[:, e % 2, :], o, ACT.Square).then_inc(sqo_ready, 1)
                roots(2, RC[:, :], RC[:, :])
                squares(8)
                roots(3, RC[:, :], RC[:, :])
                h_hi(8, 3)

                j0, pos = 0, 0
                for c, nb in enumerate(BLOCKS):
                    with act.Fori(0, nb // 2) as i:
                        for e in range(2):
                            act.wait_ge(gl_ready, before(gl_ready, l, i * 2 + (j0 + e)))
                            tile(f"fi{c}_{2 * e}", WQ[:, e, :], ACT.Silu, c=i * 4)
                            g_tmp = TS[:, e, :]
                            act.wait_ge(unit_of(f"fi{c}_{2 * e + 1}"), read(l, f"fi{c}_{2 * e + 1}", i))
                            act.activation(YH[:, ds(i * 2 + e, 1), :].rearrange("p o c -> p (o c)"), g_tmp, ACT.Copy) \
                               .then_inc(gh_ready, 1)
                    if c == 0:
                        with act.Fori(0, 2) as i:
                            for e in range(4):
                                o_tile(f"fo0_{e}", i * 4, i * 4 + e)
                    if c == len(BLOCKS) - 1:
                        with act.Fori(0, 2) as i:
                            for e in range(4):
                                act.wait_ge(unit_of(f"fo{c}_{e}"), read(l, f"fo{c}_{e}", i))
                                act.wait_ge(acc_added, before(acc_added, l, i * 4 + (8 + e)))
                                carry(act)
                                act.activation(SQ[:, e % 2, :],
                                               OMID[:, ds(i * 4 + e, 1), :].rearrange("p o c -> p (o c)"), ACT.Square) \
                                   .then_inc(sqo_ready, 1)
                    j0 += nb
                roots(4, RC[:, :], RC[:, :])
                act.wait_ge(o_stored, l * (16 * O_STORES) + 16 * O_STORES)
                step.end()

        @block.vector
        def _(dve):
            step = Steps(DVE_STEPS)
            RNG = ((0, SEQ, 0), (SEQ, T, 1))
            dve.memset(HH[:, KT_ * T:].bitcast(f32), 0.0).then_inc(chunk_split, 2)
            dve.memset(HL[:, KT_ * T:].bitcast(f32), 0.0).then_inc(chunk_used, 2)
            dve.memset(RC[:, :], 1.0).then_inc(proj_free, 1)
            dve.memset(CS[:, :, :], 0.0).then_inc(init_done, 1)
            for t in range(NTT + 1):
                n = 128 if t < NTT else 64
                dve.wait_ge(x_in_t, t + 1)
                dve.tensor_copy(X[:, :, t * 128:t * 128 + n],
                                PS[:, t % 4, :].rearrange("p (k c) -> p k c", k=8)[:, :, 0:n]) \
                                   .then_inc(init_done, 1)
            dve.wait_ge(x_in_t, NTT + 2)
            dve.tensor_copy(CC[:, :], PS[:, 1, 0:16]).then_inc(init_done, 1)
            dve.wait_ge(init_done, NTT + 3)
            for u in range(UNITS):
                dve.memset(LR[:, u:u + 1], 1.0).then_inc(unit_free[u], 1)
            dve.memset(LR[:, 4:5], 1.0).then_inc(x_ready, 8)
            for i, ring in enumerate((acc_added, gl_ready, merged2)):
                dve.memset(BN[:, i:i + 1], 0.0).then_inc(ring, 2)

            with dve.Fori(0, DEPTH) as l:
                step.layer(l)

                def cols(x, k):
                    return x[:, k * T:(k + 1) * T]

                def tt(out, a, b, op):
                    return dve.tensor_tensor(out, a, b, op)

                def bc(ap, shape):
                    return ap.unsqueeze(len(shape) - 1).to_broadcast(shape)

                def norm_tail(name, which):
                    dve.wait_ge(done_by(name), done(l, name))
                    for a, b, n in ((0, 4, 128), (4, 5, 64)):
                        m = dve.tensor_scalar(RC[0:n, a:b], unit(name)[0:n, a:b], 1.0 / D, EPS, ALU.mult, ALU.add)
                        if n == 128:
                            m.then_inc(dve_step, step())
                    m.then_inc(unit_of(name), 1)
                    dve.wait_ge(unit_of(name), read(l, name))
                    dve.tensor_scalar(RC[64:128, 4:5], RC[64:128, 3:4], 1.0, None, ALU.mult) \
                       .then_inc(ms_ready, 1)
                    dve.wait_ge(rt_ready, nth(rt_ready, l, which))
                    dve.reciprocal(RC[:, :], RC[:, :]).then_inc(dve_step, step())
                    dve.wait_ge(dve_step, step.all())
                    tt(R[:, 0:512].rearrange("p (t c) -> p t c", t=4),
                            IDN.unsqueeze(1).to_broadcast([128, 4, 128]), bc(RC[:, 0:4], [128, 4, 128]), ALU.mult) \
                               .then_inc(dve_step, step())
                    dve.tensor_scalar(R[0:64, 512:576], IDN[0:64, 0:64], RC[0:64, 4:5], None, ALU.mult) \
                       .then_inc(dg_ready, 1)
                    dve.wait_ge(done_by(name + "b"), done(l, name + "b"))
                    dve.tensor_copy(R[:, :], unit(name + "b")[:, 0:T]).then_inc(unit_of(name + "b"), 1)
                    dve.wait_ge(unit_of(name + "b"), read(l, name + "b"))

                norm_tail("n1", 0)
                dve.wait_ge(done_by("par"), done(l, "par"))
                dve.tensor_copy(VCOL[:, :], unit("par")[:, 0:80]).then_inc(unit_of("par"), 1)
                dve.wait_ge(done_by("wst"), done(l, "wst"))
                dve.scalar_tensor_tensor(WST[:, :, :], K_["mneg"].unsqueeze(1).to_broadcast([128, 4, 128]), 0.0,
                                              unit("wst")[:, 0:512].rearrange("p (g c) -> p g c", g=4),
                                              ALU.is_ge, ALU.mult).then_inc(unit_of("wst"), 1)
                dve.wait_ge(unit_of("par"), read(l, "par"))

                def modulation_part(nm, s, j, i=0):
                    dve.wait_ge(done_by(nm), done(l, nm, i))
                    tt(MOD[:, ds(j, 1), 4 * s:4 * s + 4, :].rearrange("p o a b -> p (o a) b"),
                       unit(nm)[:, 0:128].rearrange("p (a b) -> p a b", b=32)[:, :, 0:2],
                       bc(VCOL[:, ds(j * 8 + 4 * s, 4)], [128, 4, 2]), ALU.add).then_inc(unit_of(nm), 1)

                for s in range(2):
                    modulation_part(f"ada{2 + s}", s, 0)
                with dve.Fori(0, 5) as i:
                    for s in range(2):
                        modulation_part(f"ada{6 + s}", s, i + 1, i * 4)
                dve.wait_ge(done_by("ckt"), done(l, "ckt"))
                dve.tensor_copy(KALL[:, 0, T:704], unit("ckt")[:, 0:128]).then_inc(unit_of("ckt"), 1)
                dve.memset(VT[:, :, :, 128:129], 1.0).then_inc(dve_step, step())
                dve.wait_ge(unit_of("ada23"), read(l, "ada23"))
                for i, (part, c, plus) in enumerate(((1, 48, 1.0), (2, 56, 0.0), (4, 64, 1.0), (5, 72, 0.0))):
                    dve.scalar_tensor_tensor(SC[:, i, :, :], MOD[:, part, :, :], plus,
                                                  bc(VCOL[:, c:c + 8], [128, 8, 2]), ALU.add, ALU.mult) \
                                                     .then_inc(dve_step, step())
                dve.wait_ge(dve_step, step.all())

                def pre_norm(first, sc, sh):
                    def lo(k):
                        dve.wait_ge(hh_ready, nth(hh_ready, l, (0 if first == 0 else 16) + k))
                        for a, b, j in RNG:
                            m = dve.scalar_tensor_tensor(cols(HL, k)[:, a:b], TS[:, k % 2, a:b], MOD[:, sh, k, j:j + 1],
                                                         cols(HH, k)[:, a:b].bitcast(f32), ALU.add, ALU.subtract)
                        m.then_inc(hl_ready, 1)
                    for k in range(8):
                        if k >= 2:
                            dve.wait_ge(hl_ready, nth(hl_ready, l, (0 if first == 0 else 16) + k - 2))
                        for a, b, j in RNG:
                            m = dve.scalar_tensor_tensor(TS[:, k % 2, a:b], X[:, k, a:b], SC[:, sc, k, j:j + 1],
                                                         R[:, a:b], ALU.mult, ALU.mult)
                        m.then_inc(hs_ready, 1)
                        if k:
                            lo(k - 1)
                    lo(7)

                def post_norm(name, which, sc):
                    norm_tail(name, which)
                    for k in range(8):
                        for a, b, j in RNG:
                            dve.scalar_tensor_tensor(TS[:, k % 2, a:b], OMID[:, k, a:b], SC[:, sc, k, j:j + 1],
                                                          R[:, a:b], ALU.mult, ALU.mult) \
                                                             .then_inc(dve_step, step())
                        dve.wait_ge(dve_step, step.all())
                        tt(X[:, k, :], X[:, k, :], TS[:, k % 2, :], ALU.add).then_inc(x_ready, 1)

                pre_norm(0, 0, 0)
                dve.wait_ge(done_by("wvif"), done(l, "wvif"))
                for t0, t1, c in ((0, 3, 0), (3, 5, 512)):
                    o = unit("wvif")[:, c:c + 136 * (t1 - t0)].rearrange("p (t c) -> p t c", c=136)
                    dve.tensor_copy(VSW[:, t0:t1, :], o[:, :, 0:128]).then_inc(dve_step, step())
                    m = tt(IFT[:, t0:t1, :], o[:, :, 128:136], BIF[:, :].unsqueeze(1).to_broadcast([128, t1 - t0, 8]),
                           ALU.add)
                    if t0 == 0:
                        m.then_inc(dve_step, step())
                m.then_inc(unit_of("wvif"), 1)
                dve.wait_ge(done_by("gt1"), done(l, "gt1"))
                dve.tensor_copy(IG[:, 0:512], unit("gt1")[0:4, 0:512]).then_inc(dve_step, step())
                dve.tensor_copy(EM[:, 0:512], unit("gt1")[0:4, 512:1024]).then_inc(unit_of("gt1"), 1)
                dve.wait_ge(done_by("gt2"), done(l, "gt2"))
                dve.tensor_copy(IG[:, 512:576], unit("gt2")[0:4, 0:64]).then_inc(dve_step, step())
                dve.tensor_copy(EM[:, 512:576], unit("gt2")[0:4, 512:576]).then_inc(unit_of("gt2"), 1)
                dve.wait_ge(unit_of("gt1"), read(l, "gt1"))
                dve.wait_ge(unit_of("gt2"), read(l, "gt2"))
                dve.scalar_tensor_tensor(WR, EM, -1.0, EM, ALU.mult, ALU.min).then_inc(nabs_ready, 1)
                dve.wait_ge(sp_ready, nth(sp_ready, l))
                dve.scalar_tensor_tensor(LFT, EM, 0.0, WR, ALU.min, ALU.subtract).then_inc(dve_step, step())
                dve.wait_ge(dve_step, step.all())
                for a, b in ((0, SEQ), (SEQ, T)):
                    dve.tensor_tensor_scan(BC[:, a:b], ONES[0:4, 0:1].to_broadcast([4, b - a]), LFT[:, a:b],
                                                0.0, ALU.mult, ALU.add).then_inc(dve_step, step())
                dve.wait_ge(dve_step, step.all())
                tt(AR, IG, BC, ALU.subtract).then_inc(dve_step, step())
                dve.wait_ge(dve_step, step.all())
                dve.tensor_tensor_scan(IG[:, 0:SEQ], AR[:, 0:SEQ], AR[:, 0:SEQ], 0.0, ALU.max, ALU.max) \
                   .then_inc(dve_step, step())
                dve.tensor_tensor_scan(IG[:, SEQ:T], AR[:, SEQ:T], AR[:, SEQ:T], M0[:, 0:1], ALU.max, ALU.max) \
                   .then_inc(dve_step, step())
                dve.wait_ge(dve_step, step.all())
                dve.tensor_scalar(NM, IG, -1.0, None, ALU.mult).then_inc(dve_step, step())
                dve.wait_ge(dve_step, step.all())
                tt(IG, IG, BC, ALU.add).then_inc(dve_step, step())
                for j, c in enumerate((SEQ - 1, T - 1)):
                    m = dve.tensor_copy(NML[:, j:j + 1], NM[:, c:c + 1])
                m.then_inc(m_ready, 1)

                def v_copy(h):
                    dve.wait_ge(done_by(f"vt{h}"), done(l, f"vt{h}"))
                    dve.tensor_copy(VT[:, 0:4, h, 0:128], unit(f"vt{h}")[:, 0:512].rearrange("p (t c) -> p t c", t=4)) \
                       .then_inc(dve_step, step())
                    dve.tensor_copy(VT[0:64, 4, h, 0:128], unit(f"vt{h}")[0:64, 512:640]) \
                       .then_inc(unit_of(f"vt{h}"), 1)

                def weigh_keys(h):
                    nm = f"kt{h}"
                    dve.wait_ge(done_by(nm), done(l, nm))
                    tt(KW[:, 0:4, :], unit(nm)[:, 0:512].rearrange("p (t c) -> p t c", t=4),
                            bc(WSC[:, 0:4, h], [128, 4, 128]), ALU.mult).then_inc(dve_step, step())
                    dve.tensor_scalar(KW[0:64, 4, :], unit(nm)[0:64, 512:640], WSC[0:64, 4, h:h + 1], None,
                                           ALU.mult).then_inc(unit_of(nm), 1)

                def new_state(h):
                    nm = f"cm{h}"
                    dve.wait_ge(done_by(nm), done(l, nm))
                    dve.tensor_copy(COUT[:, h, 0, :], unit(nm)[:, 0:129]).then_inc(dve_step, step())
                    dve.scalar_tensor_tensor(COUT[:, h, 1, :], C0N[:, h, :], DEC[:, h:h + 1],
                                                  unit(nm)[:, 512:641], ALU.mult, ALU.add) \
                                                     .then_inc(unit_of(nm), 1)

                dve.wait_ge(done_by("gt3"), done(l, "gt3"))
                o = unit("gt3")
                for dst, c, f in ((AS, 0, 1.0), (WSC, 20, ML_SCALE), (EMC, 44, 1.0)):
                    dve.tensor_scalar(dst[:, 0:4, :], o[:, c:c + 16].rearrange("p (t h) -> p t h", t=4), f, None,
                                           ALU.mult).then_inc(dve_step, step())
                    dve.tensor_scalar(dst[0:64, 4, :], o[0:64, c + 16:c + 20], f, None, ALU.mult) \
                       .then_inc(dve_step, step())
                dve.tensor_copy(DEC[:, :], o[:, 40:44]).then_inc(unit_of("gt3"), 1)
                dve.wait_ge(unit_of("gt3"), read(l, "gt3"))
                v_copy(0)
                weigh_keys(0)
                v_copy(1)
                new_state(0)
                weigh_keys(1)
                v_copy(2)
                new_state(1)
                weigh_keys(2)
                v_copy(3)
                new_state(2)
                weigh_keys(3)
                new_state(3)

                def exponents(h):
                    nm = _a(h)[0]
                    dve.wait_ge(done_by(nm), done(l, nm))
                    o = unit(nm)
                    tt(DM[:, 0:512].rearrange("p (t c) -> p t c", t=4),
                            o[:, 0:512].rearrange("p (t c) -> p t c", t=4),
                            K_["mneg"].unsqueeze(1).to_broadcast([128, 4, 128]), ALU.add) \
                               .then_inc(dve_step, step())
                    tt(W[0:64, 1280:1344], o[0:64, 512:576], K_["mneg"][0:64, 0:64], ALU.add) \
                       .then_inc(dve_step, step())
                    tt(DM[:, 512:576], QK[:, h, SEQ:T], o[:, 576:640], ALU.mult).then_inc(d_ready, 1)

                def weigh_scores(h):
                    _, n2, n3 = _a(h)
                    dve.wait_ge(w_ready, nth(w_ready, l, h))
                    dve.wait_ge(done_by(n2), done(l, n2))
                    dve.scalar_tensor_tensor(W[:, 0:1024], unit(n2), ML_SCALE, W[:, 0:1024], ALU.mult, ALU.mult) \
                       .then_inc(unit_of(n2), 1)
                    dve.wait_ge(done_by(n3), done(l, n3))
                    dve.scalar_tensor_tensor(W[:, 1024:1280], unit(n3)[:, 0:256], ML_SCALE, W[:, 1024:1280],
                                                  ALU.mult, ALU.mult).then_inc(dve_step, step())
                    dve.scalar_tensor_tensor(W[0:64, 1280:1344], unit(n3)[0:64, 256:320], ML_SCALE,
                                                  W[0:64, 1280:1344], ALU.mult, ALU.mult) \
                                                     .then_inc(unit_of(n3), 1)

                def normalise(h):
                    nm = _b(h)[0][0]
                    dve.wait_ge(done_by(nm), done(l, nm))
                    o3 = unit(nm)[:, 0:387].rearrange("p (t c) -> p t c", t=3)
                    o4, o5 = unit(nm)[:, 512:641], unit(nm)[0:64, 641:770]
                    dve.tensor_copy(DEN[:, 0:3], o3[:, :, 128]).then_inc(dve_step, step())
                    dve.tensor_copy(DEN[:, 3:4], o4[:, 128:129]).then_inc(dve_step, step())
                    dve.tensor_copy(DEN[0:64, 4:5], o5[:, 128:129]).then_inc(dve_step, step())
                    dve.wait_ge(dve_step, step.all())
                    for n, a, b in ((128, 0, 4), (64, 4, 5)):
                        dve.scalar_tensor_tensor(EMC[0:n, a:b, h], DEN[0:n, a:b], -1.0, EMC[0:n, a:b, h],
                                                      ALU.mult, ALU.max).then_inc(dve_step, step())
                    dve.wait_ge(dve_step, step.all())
                    for n, a, b in ((128, 0, 4), (64, 4, 5)):
                        tt(DEN[0:n, a:b], DEN[0:n, a:b], EMC[0:n, a:b, h], ALU.max).then_inc(dve_step, step())
                    dve.wait_ge(dve_step, step.all())
                    for n, a, b in ((128, 0, 4), (64, 4, 5)):
                        dve.reciprocal(DEN[0:n, a:b], DEN[0:n, a:b]).then_inc(dve_step, step())
                    dve.wait_ge(dve_step, step.all())
                    dve.scalar_tensor_tensor(YTK[:, 0:3, :], o3[:, :, 0:128], 0.5, bc(DEN[:, 0:3], [128, 3, 128]),
                                                  ALU.mult, ALU.mult).then_inc(dve_step, step())
                    dve.tensor_scalar(YTK[:, 3, :], o4[:, 0:128], DEN[:, 3:4], 0.5, ALU.mult, ALU.mult) \
                       .then_inc(dve_step, step())
                    dve.tensor_scalar(YTK[0:64, 4, :], o5[:, 0:128], DEN[0:64, 4:5], 0.5, ALU.mult, ALU.mult) \
                       .then_inc(unit_of(nm), 1)
                    dve.wait_ge(unit_of(nm), read(l, nm))

                def gate_head(h):
                    nm = _b(h)[1][0]
                    dve.wait_ge(done_by(nm), done(l, nm))
                    dve.wait_ge(unit_of(f"mo{h}"), read(l, f"mo{h}"))
                    dve.scalar_tensor_tensor(YT[:, :], MO[:, h, :], 1.0, unit(nm)[:, 0:T], ALU.add, ALU.mult) \
                       .then_inc(unit_of(nm), 1)

                def y_lo(i, src):
                    dve.wait_ge(yh_ready, nth(yh_ready, l, i))
                    tt(YL[:, i % 4, :], src, YH[:, i % 4, :].bitcast(f32), ALU.subtract).then_inc(yl_ready, 1)

                exponents(0)
                weigh_scores(0)
                for h in range(4):
                    normalise(h)
                    if h < 3:
                        gate_head(h)
                        exponents(h + 1)
                        y_lo(h, YT[:, :])
                        weigh_scores(h + 1)
                gate_head(3)
                y_lo(3, YT[:, :])

                def rope(i):
                    nm = f"r{i}"
                    raw = KALL[:, 0, 0:T] if i == 4 else WQ[:, i, :]
                    dve.wait_ge(unit_of("wk" if i == 4 else f"wq{i}"), read(l, "wk" if i == 4 else f"wq{i}"))
                    tt(TS[:, 0, :], raw, K_["cos"], ALU.mult).then_inc(dve_step, step())
                    dve.wait_ge(done_by(nm), done(l, nm))
                    tt(split2(TS[:, 1, :]), halves(nm), split2(K_["sin"]), ALU.mult).then_inc(unit_of(nm), 1)
                    dve.wait_ge(dve_step, step.all())
                    dve.wait_ge(unit_of(nm), read(l, nm))
                    tt(raw, TS[:, 0, :], TS[:, 1, :], ALU.add).then_inc(rope_ready, 1)

                for j, i in enumerate((4, 0, 1, 2, 3)):
                    if j:
                        dve.wait_ge(rope_ready, nth(rope_ready, l, j - 1))
                    rope(i)
                dve.wait_ge(done_by("ko"), done(l, "ko"))
                dve.tensor_copy(KOUT[:, 0, :], unit("ko")[:, 0:128]).then_inc(dve_step, step())
                dve.tensor_copy(KOUT[0:64, 1, :], unit("ko")[0:64, 128:256]).then_inc(unit_of("ko"), 1)
                dve.wait_ge(c_stored, l * (16 * C_STORES) + 16 * C_STORES)

                def sw_lo(i):
                    t, g = SWA[i]
                    n = 128 if t < NTT else 64
                    dve.wait_ge(oh_ready, nth(oh_ready, l, i))
                    y = (slice(None), slice(4 + 2 * g, 6 + 2 * g), slice(t * 128, t * 128 + n))
                    tt(YL[y], unit(f"pv{i}")[:, 0:2 * n].rearrange("p (r c) -> p r c", r=2),
                            YH[y].bitcast(f32), ALU.subtract).then_inc(unit_of(f"pv{i}"), 1)

                def sw_max(i):
                    t, g = SWA[i]
                    nm = f"sc{i}"
                    n = 128 if t < NTT else 64
                    kw = 128 if t == 0 else (192 if t == NTT else 256)
                    dve.wait_ge(done_by(nm), done(l, nm))
                    o = unit(nm).rearrange("p (r c) -> p r c", r=4)[0:n, :, 0:kw]
                    s = SM[0:n, i % 2, :, 0:kw]
                    if t == NTT:
                        dve.tensor_scalar(s, o, SW_SCALE, None, ALU.mult).then_inc(unit_of(nm), 1)
                    else:
                        dve.scalar_tensor_tensor(s, o, SW_SCALE, K_["m1"][:, 256 - kw:].unsqueeze(1)
                                                      .to_broadcast([128, 4, kw]), ALU.mult, ALU.add) \
                                                         .then_inc(unit_of(nm), 1)
                    dve.wait_ge(unit_of(nm), read(l, nm))
                    mx = [MX[0:n, i % 2, j, :] for j in range(5)]
                    sink = SINK[0:n, 4 * g:4 * g + 4].rearrange("p (r o) -> p o r", o=2)
                    dve.tensor_reduce(mx[0], s, AX.X, ALU.max).then_inc(dve_step, step())
                    dve.wait_ge(dve_step, step.all())
                    m2 = mx[0].rearrange("p (o r) -> p o r", o=2)
                    tt(m2, m2, sink, ALU.max).then_inc(dve_step, step())
                    dve.wait_ge(dve_step, step.all())
                    dve.tensor_scalar(mx[1], mx[0], -1.0, None, ALU.mult).then_inc(dve_step, step())
                    tt(mx[3].rearrange("p (o r) -> p o r", o=2), sink, m2, ALU.subtract).then_inc(mx_ready, 1)

                def sw_norm(i):
                    t, g = SWA[i]
                    n = 128 if t < NTT else 64
                    kw = 128 if t == 0 else (192 if t == NTT else 256)
                    s = SM[0:n, i % 2, :, 0:kw]
                    mx = [MX[0:n, i % 2, j, :] for j in range(5)]
                    dve.wait_ge(ex_ready, nth(ex_ready, l, i))
                    tt(mx[4], mx[2], mx[3], ALU.add).then_inc(dve_step, step())
                    dve.wait_ge(dve_step, step.all())
                    dve.reciprocal(mx[4], mx[4]).then_inc(dve_step, step())
                    dve.wait_ge(dve_step, step.all())
                    tt(s, s, bc(mx[4], [n, 4, kw]), ALU.mult).then_inc(pn_ready, 1)

                def slot(i, between=None):
                    if 0 <= i - 2 < NS:
                        sw_lo(i - 2)
                    if i < NS:
                        sw_max(i)
                    if between is not None:
                        between()
                    if i < NS:
                        sw_norm(i)

                def gmlp_copy(i):
                    nm = f"svt{i}"
                    dve.wait_ge(done_by(nm), done(l, nm))
                    c = slice(i * 128, (i + 1) * 128)
                    dve.tensor_copy(SV[:, 0:4, c], unit(nm)[:, 0:512].rearrange("p (t c) -> p t c", t=4)) \
                       .then_inc(dve_step, step())
                    dve.tensor_copy(SV[0:64, 4, c], unit(nm)[0:64, 512:640]).then_inc(unit_of(nm), 1)

                for i in range(4):
                    if i:
                        gmlp_copy(i - 1)
                    slot(i)
                gmlp_copy(3)

                def ln_stats():
                    dve.wait_ge(unit_of("svt3"), read(l, "svt3"))
                    for t in range(NTT + 1):
                        n = 128 if t < NTT else 64
                        dve.wait_ge(dve_step, step.all())
                        dve.bn_stats(BN[0:n, :], SV[0:n, t, :]).then_inc(dve_step, step())
                        dve.wait_ge(dve_step, step.all())
                        carry(dve)
                        dve.bn_aggr(MV[0:n, t, :], BN[0:n, :]).then_inc(dve_step, step())
                    dve.wait_ge(dve_step, step.all())
                    dve.tensor_scalar(LR[:, 0:4], MV[:, 0:4, 1], EPS, None, ALU.add).then_inc(dve_step, step())
                    dve.tensor_scalar(LR[0:64, 4:5], MV[0:64, 4, 1:2], EPS, None, ALU.add).then_inc(ms_ready, 1)

                def ln_root():
                    dve.wait_ge(ln_loaded, l * 32 + 32)
                    dve.wait_ge(rt_ready, nth(rt_ready, l, 1))
                    dve.reciprocal(LR[:, :], LR[:, :]).then_inc(dve_step, step())

                def ln_apply(t):
                    n = 128 if t < NTT else 64
                    v = SV[0:n, t, :]
                    dve.wait_ge(dve_step, step.all())
                    dve.tensor_scalar(v, v, MV[0:n, t, 0:1], LR[0:n, t:t + 1], ALU.subtract, ALU.mult) \
                       .then_inc(dve_step, step())
                    dve.wait_ge(dve_step, step.all())
                    tt(v, v, LNG[0:n], ALU.mult).then_inc(dve_step, step())
                    dve.wait_ge(dve_step, step.all())
                    tt(v, v, LNB[0:n], ALU.add).then_inc(ln_ready, 1)

                def merge(b, n, q=0, tile=None):
                    nm, tile = f"br{b}_{n}", n if tile is None else tile
                    dve.wait_ge(unit_of(f"g{b}_{n}"), read(l, f"g{b}_{n}", q * 2))
                    dve.wait_ge(done_by(nm), done(l, nm, q * (6 if nm in CHUNK_OF else 2)))
                    s = split2(TS[:, n % 2, :])
                    m = MID[:, ds(tile, 1), :].rearrange("p o (a c) -> p (o a) c", a=2)
                    if b == 0:
                        dve.scalar_tensor_tensor(m, s, 1.0, halves(nm), ALU.add, ALU.mult) \
                           .then_inc(unit_of(nm), 1)
                        return
                    w = WQ[:, n % 2, :]
                    dve.scalar_tensor_tensor(split2(w), s, 1.0, halves(nm), ALU.add, ALU.mult) \
                       .then_inc(unit_of(nm), 1)
                    dve.wait_ge(unit_of(nm), read(l, nm, q * 2))
                    ins = tt(m, m, split2(w), ALU.add)
                    if b == 2:
                        ins.then_inc(merged2, 1)
                    else:
                        ins.then_inc(dve_step, step())

                x = 4
                for n in range(0, 8, 2):
                    for e in range(2):
                        slot(x, ln_stats if x == 4 else (lambda: ln_apply(x - 7)) if 7 <= x < 12 else None)
                        x += 1
                    merge(0, n)
                    merge(0, n + 1)
                    if n == 0:
                        ln_root()
                    slot(x, (lambda: ln_apply(x - 7)) if 7 <= x < 12 else None)
                    x += 1
                for n in range(0, 8, 2):
                    g = n // 2
                    nm = f"z{g}"
                    dve.wait_ge(done_by(nm), done(l, nm))
                    dve.wait_ge(unit_of(f"su{g}"), read(l, f"su{g}"))
                    tt(WQ[:, 2 + g % 2, :], SU[:, g, :], unit(nm)[:, 0:T], ALU.mult).then_inc(unit_of(nm), 1)
                    dve.wait_ge(unit_of(nm), read(l, nm))
                    y_lo(4 + g, WQ[:, 2 + g % 2, :])
                    for e in range(2):
                        merge(1, n + e)

                with dve.Fori(0, 2) as q:
                    for n in range(4):
                        merge(2, n, q, q * 4 + n)
                dve.wait_ge(done_by("g2_3"), done(l, "g2_3", 6))
                for k in range(8):
                    dve.wait_ge(hh_ready, nth(hh_ready, l, 8 + k))
                    dve.scalar_tensor_tensor(cols(HL, k), MID[:, k, :], 0.5, cols(HH, k).bitcast(f32),
                                             ALU.mult, ALU.subtract).then_inc(hl_ready, 1)

                def add_tile(c, e, i):
                    o = OMID[:, ds(i * 4 + e, 1), :].rearrange("p o (a c) -> p (o a) c", a=2)
                    dve.wait_ge(unit_of(f"fo{c - 1}_{e}"), read(l, f"fo{c - 1}_{e}", i))
                    dve.wait_ge(done_by(f"fo{c}_{e}"), done(l, f"fo{c}_{e}", i * 4))
                    tt(o, o, halves(f"fo{c}_{e}"), ALU.add).then_inc(unit_of(f"fo{c}_{e}"), 1)

                def add_squares(which):
                    with dve.Fori(0, 2) as i:
                        for e in range(4):
                            if which == 1:
                                add_tile(len(BLOCKS) - 1, e, i)
                            dve.wait_ge(sqo_ready, nth(sqo_ready, l, i * 4 + (8 * which + e)))
                            dve.wait_ge(acc_added, nth(acc_added, l, i * 4 + (8 * which + e - 1)))
                            tt(ACC[:, :], ACC[:, :], SQ[:, e % 2, :], ALU.add).then_inc(acc_added, 1)

                dve.memset(ACC[:, :], 0.0).then_inc(dve_step, step())
                dve.wait_ge(dve_step, step.all())
                carry(dve)
                add_squares(0)
                post_norm("p1", 2, 1)
                norm_tail("n2", 3)
                pre_norm(8, 2, 3)
                j0 = 0
                for c, nb in enumerate(BLOCKS):
                    with dve.Fori(0, nb // 2) as i:
                        for e in range(2):
                            gate_nm, up = f"fi{c}_{2 * e}", f"fi{c}_{2 * e + 1}"
                            dve.wait_ge(unit_of(gate_nm), read(l, gate_nm, i))
                            dve.wait_ge(done_by(up), done(l, up, i * 4))
                            tt(split2(TS[:, e, :]), split2(WQ[:, e, :]), halves(up), ALU.mult) \
                               .then_inc(unit_of(up), 1)
                            dve.wait_ge(gh_ready, nth(gh_ready, l, i * 2 + (j0 + e)))
                            y = ds(i * 2 + e, 1)
                            tt(YL[:, y, :].rearrange("p o c -> p (o c)"), TS[:, e, :],
                               YH[:, y, :].bitcast(f32).rearrange("p o c -> p (o c)"),
                               ALU.subtract).then_inc(gl_ready, 1)
                    j0 += nb
                    if c == 1:
                        with dve.Fori(0, 2) as i:
                            for e in range(4):
                                add_tile(1, e, i)
                    if c == 2:
                        dve.wait_ge(o_stored, l * (16 * O_STORES) + 16 * O_STORES)
                        dve.memset(ACC[:, :], 0.0).then_inc(proj_free, 1)
                        dve.wait_ge(proj_free, nth(proj_free, l))
                        carry(dve)
                        add_squares(1)
                post_norm("p2", 4, 3)
                step.end()

            for t in range(NTT + 1):
                n = 128 if t < NTT else 64
                dve.wait_ge(x_out_t, t + 1)
                dve.tensor_copy(XIO[0:n, t, :], PS[0:n, t % 4, :]).then_inc(x_out_copied, 1)


_INS = ["x_prompt", "x_sample", "c_prompt", "c_sample", "state_mlstm_C", "state_mlstm_n", "state_mlstm_m",
        "cache_swa_k", "cache_swa_v", "w_ada", "b_ada", "g_pre_mix", "g_post_mix", "g_pre_ffn", "g_post_ffn",
        "w_in", "b_igate", "b_fgate", "ln_v_g", "ln_v_b", "w_spatial", "b_spatial", "swa_sinks",
        "w_br_mlstm", "w_br_gmlp", "w_br_swa", "w_out", "w_ffn_in", "w_ffn_out"]
_OUTS = [("y_prompt", (1, SEQ, D)), ("y_sample", (1, DSEQ, D)),
         ("C_prompt", (DEPTH, 1, MLH, 128, 128)), ("n_prompt", (DEPTH, 1, MLH, 128)), ("m_prompt", (DEPTH, 1, MLH)),
         ("k_prompt", (DEPTH, 1, 128, 2, 64)), ("v_prompt", (DEPTH, 1, 128, 2, 64)),
         ("C_sample", (DEPTH, 1, MLH, 128, 128)), ("n_sample", (DEPTH, 1, MLH, 128)), ("m_sample", (DEPTH, 1, MLH)),
         ("k_sample", (DEPTH, 1, DSEQ, 2, 64)), ("v_sample", (DEPTH, 1, DSEQ, 2, 64)),
         ("gmlp_v_sample", (DEPTH, 1, DSEQ, 512))]


def kernel(**inputs):
    import numpy as _np
    import concourse.bacc as _bacc
    from concourse import mybir as _mybir
    from concourse.bass_utils import run_bass_kernel_spmd as _run

    nc = _bacc.Bacc("TRN2", target_bir_lowering=False, num_devices=1)
    arrays, ins, outs = {}, {}, {}
    for name in _INS:
        a = _np.ascontiguousarray(inputs[name])
        arrays[f"in_{name}"] = a
        ins[name] = nc.dram_tensor(f"in_{name}", a.shape, _mybir.dt.from_np(a.dtype), kind="ExternalInput").ap()
    arrays["in_consts"] = constants()
    ins["consts"] = nc.dram_tensor("in_consts", (128, NCONST), _mybir.dt.float32, kind="ExternalInput").ap()
    for name, shape in _OUTS:
        outs[name] = nc.dram_tensor(f"out_{name}", shape, _mybir.dt.float32, kind="ExternalOutput").ap()
    build(nc, ins, outs)
    r = _run(nc, [arrays], core_ids=[0])
    return tuple(r.results[0][f"out_{name}"] for name, _ in _OUTS)
```
